# Optimizing a Trainium2 kernel written in Bass

```python
import jax, jax.numpy as jnp
from jax import lax
import numpy as np

D_MODEL = 1024
BATCH = 1
SEQ = 1024
DEPTH = 2

P_DIM = 256
N_MIXERS = 2
CONV_WIDTH = 3
M_HEADS = 4
QK_HEAD = D_MODEL // 2 // M_HEADS
V_HEAD = D_MODEL // M_HEADS
QK_DIM = M_HEADS * QK_HEAD
V_DIM = M_HEADS * V_HEAD
MLSTM_IN = 2 * QK_DIM + 2 * V_DIM + 2 * M_HEADS
CHUNK = 64
D_FF = 2816
EPS = 1e-6
N_CONV_LAYERS = (DEPTH + 1) // 2
N_MLSTM_LAYERS = DEPTH // 2

kernel_name = "hybrid_shortconv_mlstm_convglu_sandwich"

def rms_norm(x, g):
    xf = x.astype(jnp.float32)
    y = xf * lax.rsqrt(jnp.mean(xf * xf, axis=-1, keepdims=True) + EPS)
    return (y * g.astype(jnp.float32)).astype(x.dtype)

def causal_dwconv(x, w):
    k = w.shape[0]
    return lax.conv_general_dilated(
        x, w.astype(x.dtype)[:, None, :], window_strides=(1,), padding=((k - 1, 0),),
        dimension_numbers=("NWC", "WIO", "NWC"), feature_group_count=x.shape[-1])

def short_conv_mixer(x, w_in, w_conv, w_out):
    b_gate, c_gate, u = jnp.split(x @ w_in, 3, axis=-1)
    return (b_gate * causal_dwconv(c_gate * u, w_conv)) @ w_out

def mlstm_chunk_step(carry, xs):
    c_state, n_state, m_state = carry
    q, k, v, ig, lf = xs
    b = jnp.cumsum(lf, axis=-1)
    causal = jnp.tril(jnp.ones((CHUNK, CHUNK), dtype=bool))
    log_d = jnp.where(causal, b[..., :, None] - b[..., None, :] + ig[..., None, :], -jnp.inf)
    log_inter = b + m_state[..., None]
    m_row = jnp.maximum(log_inter, jnp.max(log_d, axis=-1))
    w_intra = jnp.exp(log_d - m_row[..., None])
    w_inter = jnp.exp(log_inter - m_row)
    s = jnp.einsum("bhld,bhsd->bhls", q, k) * w_intra
    num = w_inter[..., None] * jnp.einsum("bhld,bhde->bhle", q, c_state) + jnp.einsum("bhls,bhse->bhle", s, v)
    den = w_inter * jnp.einsum("bhld,bhd->bhl", q, n_state) + jnp.sum(s, axis=-1)
    h = num / jnp.maximum(jnp.abs(den), jnp.exp(-m_row))[..., None]
    b_last = b[..., -1]
    log_a = b_last[..., None] - b + ig
    m_new = jnp.maximum(b_last + m_state, jnp.max(log_a, axis=-1))
    decay = jnp.exp(b_last + m_state - m_new)
    w_a = jnp.exp(log_a - m_new[..., None])
    c_new = decay[..., None, None] * c_state + jnp.einsum("bhs,bhsd,bhse->bhde", w_a, k, v)
    n_new = decay[..., None] * n_state + jnp.einsum("bhs,bhsd->bhd", w_a, k)
    return (c_new, n_new, m_new), h

def mlstm_mixer(x, w_in, gate_bias, head_norm, w_out):
    bsz, seq, _ = x.shape
    nc = seq // CHUNK
    q, k, v, o, ig, fg = jnp.split(
        x @ w_in, [QK_DIM, 2 * QK_DIM, 2 * QK_DIM + V_DIM, 2 * QK_DIM + 2 * V_DIM,
                   2 * QK_DIM + 2 * V_DIM + M_HEADS], axis=-1)
    gb = gate_bias.astype(jnp.float32)
    ig = ig.astype(jnp.float32) + gb[:M_HEADS]
    lf = jax.nn.log_sigmoid(fg.astype(jnp.float32) + gb[M_HEADS:])

    def to_chunks(t, dh):
        return t.astype(jnp.float32).reshape(bsz, nc, CHUNK, M_HEADS, dh).transpose(1, 0, 3, 2, 4)

    def gate_chunks(t):
        return t.reshape(bsz, nc, CHUNK, M_HEADS).transpose(1, 0, 3, 2)

    qc = to_chunks(q, QK_HEAD)
    kc = to_chunks(k, QK_HEAD) * (QK_HEAD ** -0.5)
    vc = to_chunks(v, V_HEAD)
    init = (jnp.zeros((bsz, M_HEADS, QK_HEAD, V_HEAD), jnp.float32),
            jnp.zeros((bsz, M_HEADS, QK_HEAD), jnp.float32),
            jnp.zeros((bsz, M_HEADS), jnp.float32))
    _, h = lax.scan(mlstm_chunk_step, init, (qc, kc, vc, gate_chunks(ig), gate_chunks(lf)))
    h = h.transpose(1, 0, 3, 2, 4).reshape(bsz, seq, M_HEADS, V_HEAD)
    h = h * lax.rsqrt(jnp.mean(h * h, axis=-1, keepdims=True) + EPS)
    h = (h.reshape(bsz, seq, V_DIM) * head_norm.astype(jnp.float32)).astype(x.dtype)
    return (h * jax.nn.sigmoid(o)) @ w_out

def conv_glu(x, w_up, w_conv, w_down):
    g, u = jnp.split(x @ w_up, 2, axis=-1)
    return (jax.nn.gelu(causal_dwconv(g, w_conv), approximate=True) * u) @ w_down

def setup_inputs(seed: int = 0) -> dict:
    key = jax.random.key(seed)
    ks = jax.random.split(key, 24)

    def nrm(k, shape, scale):
        return jax.random.normal(k, shape, jnp.float32) * scale

    def gain(k, shape):
        return 1.0 + 0.05 * jax.random.normal(k, shape, jnp.float32)

    forget_bias = jnp.linspace(3.0, 6.0, M_HEADS, dtype=jnp.float32)
    gate_bias = jnp.concatenate([
        nrm(ks[12], (N_MLSTM_LAYERS, M_HEADS), 0.1),
        forget_bias[None, :] + nrm(ks[13], (N_MLSTM_LAYERS, M_HEADS), 0.1)], axis=-1)
    return {
        "x": nrm(ks[0], (BATCH, SEQ, D_MODEL), 1.0),
        "p": nrm(ks[1], (DEPTH, BATCH, SEQ, P_DIM), 1.0),
        "norm_mix_pre": gain(ks[2], (DEPTH, D_MODEL)),
        "norm_mix_post": gain(ks[3], (DEPTH, D_MODEL)),
        "norm_ffn_pre": gain(ks[4], (DEPTH, D_MODEL)),
        "norm_ffn_post": gain(ks[5], (DEPTH, D_MODEL)),
        "sc_w_in": nrm(ks[6], (N_CONV_LAYERS, D_MODEL, 3 * D_MODEL), D_MODEL ** -0.5),
        "sc_w_conv": nrm(ks[7], (N_CONV_LAYERS, CONV_WIDTH, D_MODEL), CONV_WIDTH ** -0.5),
        "sc_w_out": nrm(ks[8], (N_CONV_LAYERS, D_MODEL, D_MODEL), D_MODEL ** -0.5),
        "ml_w_in": nrm(ks[9], (N_MLSTM_LAYERS, D_MODEL, MLSTM_IN), D_MODEL ** -0.5),
        "ml_gate_bias": gate_bias,
        "ml_head_norm": gain(ks[10], (N_MLSTM_LAYERS, V_DIM)),
        "ml_w_out": nrm(ks[11], (N_MLSTM_LAYERS, V_DIM, D_MODEL), V_DIM ** -0.5),
        "ffn_w_up": nrm(ks[14], (DEPTH, D_MODEL, 2 * D_FF), D_MODEL ** -0.5),
        "ffn_w_conv": nrm(ks[15], (DEPTH, CONV_WIDTH, D_FF), CONV_WIDTH ** -0.5),
        "ffn_w_down": nrm(ks[16], (DEPTH, D_FF, D_MODEL), D_FF ** -0.5),
        "ple_norm_gate": gain(ks[17], (DEPTH, D_MODEL)),
        "ple_w_gate": nrm(ks[18], (DEPTH, D_MODEL, D_MODEL), D_MODEL ** -0.5),
        "ple_w_proj": nrm(ks[19], (DEPTH, P_DIM, D_MODEL), P_DIM ** -0.5),
        "ple_norm_out": gain(ks[20], (DEPTH, D_MODEL)),
    }

def reference(x, p, norm_mix_pre, norm_mix_post, norm_ffn_pre, norm_ffn_post,
              sc_w_in, sc_w_conv, sc_w_out, ml_w_in, ml_gate_bias, ml_head_norm, ml_w_out,
              ffn_w_up, ffn_w_conv, ffn_w_down, ple_norm_gate, ple_w_gate, ple_w_proj, ple_norm_out):
    for i in range(DEPTH):
        j = i // N_MIXERS
        h = rms_norm(x, norm_mix_pre[i])
        if i % N_MIXERS == 0:
            y = short_conv_mixer(h, sc_w_in[j], sc_w_conv[j], sc_w_out[j])
        else:
            y = mlstm_mixer(h, ml_w_in[j], ml_gate_bias[j], ml_head_norm[j], ml_w_out[j])
        x = x + rms_norm(y, norm_mix_post[i])
        y = conv_glu(rms_norm(x, norm_ffn_pre[i]), ffn_w_up[i], ffn_w_conv[i], ffn_w_down[i])
        x = x + rms_norm(y, norm_ffn_post[i])
        gate = jax.nn.sigmoid(rms_norm(x, ple_norm_gate[i]) @ ple_w_gate[i])
        x = x + rms_norm(gate * (p[i] @ ple_w_proj[i]), ple_norm_out[i])
    return x


_drawn_inputs = setup_inputs


def setup_inputs(seed=0):
    import zlib

    import numpy as np

    out = dict(_drawn_inputs(seed))
    spreads = {}
    factors = {'ple_norm_gate': 3.884}
    for name, (base, spread) in spreads.items():
        noise = np.random.default_rng([zlib.crc32(name.encode()), seed]).standard_normal(out[name].shape)
        drawn = base * np.exp(spread * noise) if base else spread * noise
        out[name] = __import__('jax').numpy.asarray(drawn.astype(out[name].dtype))
    for name, factor in factors.items():
        out[name] = (out[name] * factor).astype(out[name].dtype)
    return out
```

```python
import concourse.bass as bass
from concourse import mybir
from contextlib import ExitStack

FP32 = mybir.dt.float32
FP32R = mybir.dt.float32r
ALU = mybir.AluOpType
ACT = mybir.ActivationFunctionType

P = 128
D = 1024
SEQ = 1024
DEPTH = 2
PD = 256
MLSTM_GATES = 3072
HEADS = 4
QKH = 128
VH = 256
FF = 2816
EPS = 1e-6
HALF = SEQ // 2
BLOCKW = 512
DT = D // P
SLOTS = 8
RAWS = 4
CH = SEQ // P
ONES = 1024.0
FIRST_TILES = 2
PARTS = 1 + (FF // P - FIRST_TILES) // 4
LOOPED = PARTS - 2
PER_PART = {"w_hi": 24, "w_lo": 24, "block_used": 14, "acc": 32, "bank_free": 32, "halo": 8, "tap": 24, "gelu": 8,
            "act_prod": 8, "z_hi": 8, "z_ready": 8}


class Plan:

    def __init__(self):
        self.groups = []
        self.block0 = []
        self.at = {}
        self.used0 = []
        self.z0 = []
        self.blocks = self.used = self.z = 0

    def add(self, key, k):
        self.at[key] = len(self.groups)
        self.groups.append(k)
        self.block0.append(self.blocks)
        self.used0.append(self.used)
        self.z0.append(self.z)
        self.blocks += k
        self.used += k - 1 if k == SLOTS else 0
        self.z += 2 * {"b": 4, "o": 4, "up": 2}.get(key[1], 0)


def make_plan():
    plan = Plan()
    for layer in range(DEPTH):
        for part in range(2):
            for kind in ("c", "u", "b") if layer == 0 else ("qk", "v", "o"):
                plan.add((layer, kind, part), DT)
            for g in range(2):
                plan.add((layer, "mix", part, g), 4)
        plan.add((layer, "up", 0, 0), DT)
        for g in range(2):
            plan.add((layer, "down", 0, g), FIRST_TILES)
        for part in range(1, PARTS):
            for g in range(2):
                plan.add((layer, "up", part, g), DT)
            for g in range(2):
                plan.add((layer, "down", part, g), 4)
        for g in range(2):
            plan.add((layer, "proj", g), PD // P)
        for g in range(2):
            plan.add((layer, "gate", g), DT)
    return plan


class Counts:

    def __init__(self, sems):
        self.sems = sems
        self.n = {}
        self.per = None
        self.i = None

    def value(self, name, back=0):
        n = self.n.get(name, 0) - back
        if self.per is None or not self.per.get(name, 0):
            return max(n, 0)
        return self.i * self.per[name] + n

    def up(self, name):
        self.n[name] = self.n.get(name, 0) + 1
        return self.sems[name], 1

    def next(self, name, k=1):
        self.n[name] = self.n.get(name, 0) + k
        return self.sems[name], self.value(name)

    def now(self, name, back=0):
        return self.sems[name], self.value(name, back)

    def skip(self, name, k=1):
        self.n[name] = self.n.get(name, 0) + k

    def enter(self, i):
        self.per, self.i = PER_PART, i

    def leave(self, trips):
        self.n = {k: v + (trips - 1) * self.per.get(k, 0) for k, v in self.n.items()}
        self.per = self.i = None


GATE_ABS, GATE_ROWS_DONE, GATE_COLUMNS_DONE, GATE_EXPS = 13, 22, 28, 5


SEMS = ("pow_in w_hi w_lo block_used acc bank_free sq_tmp sq_sum norm_col norm_c1 norm_c2 norm_diag norm_row rs "
        "x_old x_t x_new x_hi x_ready halo tap cu gelu act_prod z_hi z_ready p_t p_hi p_lo sig gated "
        "const const_t const_c xin_t xin_ss xin_hi xin_ready "
        "gate_w gate_acc gate_ev gate_step gate_e gate_t "
        "core_a core_d core_e core_sw core_num core_u core_r core_den c_upd0 c_upd core_hn core_ss core_rstd "
        "core_h2 core_ht core_h out_t out_c").split()


def decoder_kernel(nc, x, p, norm_mix_pre, norm_mix_post, norm_ffn_pre, norm_ffn_post, sc_w_in, sc_w_conv,
                   sc_w_out, ml_w_in, ml_gate_bias, ml_head_norm, ml_w_out, ffn_w_up, ffn_w_conv, ffn_w_down,
                   ple_norm_gate, ple_w_gate, ple_w_proj, ple_norm_out, out):
    plan = make_plan()
    ctx = ExitStack()
    with ctx:
        def sb(name, shape, dt=FP32):
            return ctx.enter_context(nc.sbuf_tensor(name, shape, dt))

        S = {name: ctx.enter_context(nc.semaphore(name)) for name in SEMS}
        raw_in = [ctx.enter_context(nc.semaphore(f"raw_in{i}")) for i in range(RAWS)]
        x_in = [ctx.enter_context(nc.semaphore(f"x_in{i}")) for i in range(CH)]
        const_in = ctx.enter_context(nc.semaphore("const_in"))
        gate_w_in = ctx.enter_context(nc.semaphore("gate_w_in"))
        p_in = ctx.enter_context(nc.semaphore("p_in"))
        out_done = [ctx.enter_context(nc.semaphore(f"out_done{i}")) for i in range(3)]

        raw = sb("raw", [P, RAWS, BLOCKW])
        w_hi = sb("w_hi", [P, SLOTS, BLOCKW], FP32R)
        w_lo = sb("w_lo", [P, SLOTS, BLOCKW], FP32R)
        x_hi = sb("x_hi", [P, DT, SEQ], FP32R)
        x_lo = sb("x_lo", [P, DT, SEQ], FP32R)
        z_hi = sb("z_hi", [P, 4, SEQ], FP32R)
        z_lo = sb("z_lo", [P, 4, SEQ], FP32R)
        y = sb("y", [P, DT, SEQ])
        rs = sb("rs", [P, SEQ])
        ident = sb("ident", [P, P])
        ones = sb("ones", [P, P])
        gains = sb("gains", [P, 260])
        small = sb("small", [P, 304])
        mask = sb("mask", [P, P])
        big = sb("big", [P, 4, SEQ])
        area = sb("area", [P, 8 * 2 * (VH + 1)])
        us = sb("us", [P, 2, HALF])
        core = sb("core", [P, 2562])
        psum = ctx.enter_context(nc.psum_tensor("psum", [P, 8, BLOCKW], FP32))

        rs_post = area[:, 0:512]
        sq = area[:, 512:1536].rearrange("p (h n) -> p h n", h=2)
        x_old = area[:, 1536:2560].rearrange("p (b n) -> p b n", b=2)
        xn = area[:, 2560:3584].rearrange("p (b n) -> p b n", b=2)
        sqt = area[:, 3584:4096]
        v_sb = area[:, :].rearrange("p (c j e) -> p c j e", c=CH, j=2)
        diag = core[:, 0:512]
        conv_in = core[:, 512:1540].rearrange("p (b n) -> p b n", b=2)
        halo_keep = core[:, 1540:1548].rearrange("p (t n) -> p t n", t=4)
        v_tmp = big[:, 0, :].rearrange("p (b n) -> p b n", b=2)
        p_rows = big[:, 1:3, :].rearrange("p a n -> p (a n)").rearrange("p (c f) -> p c f", c=CH)
        conv_out = big
        out_rows = big[:, 1:4, :]
        sqt_core = us[:, 0, 0:VH]
        rows = core[:, 0:1024]
        state = core[:, 1024:1538].rearrange("p (j e) -> p j e", j=2)
        dmat = core[:, 1538:1666]
        sw = core[:, 1666:1794]
        qw = core[:, 1794:1922]
        kw = core[:, 1922:2050]
        hn = core[:, 2050:2306]
        hn2 = core[:, 2306:2562]
        rows2 = y[:, 6, :]
        pow_in = small[:, 288:296]
        minus_half = small[:, 296:304]
        gate_raw = small[:, 160:224].rearrange("p (k c) -> p k c", k=DT)
        gate_g = small[:, 224:288].rearrange("p (k c) -> p k c", k=DT)
        zf_hi = z_hi[:, :, :].rearrange("p a n -> p (a n)")[:, 0:DT * 68].rearrange("p (k c) -> p k c", k=DT)
        zf_lo = z_lo[:, :, :].rearrange("p a n -> p (a n)")[:, 0:DT * 68].rearrange("p (k c) -> p k c", k=DT)

        c1 = small[:, 0:4]
        c2 = small[:, 4:8]
        c2_pre = small[:, 8:16]
        ss_in = small[:, 16:24]
        dec = small[:, 24:25]
        den = small[:, 25:26]
        ss_raw = small[:, 144:152]
        rden = small[:, 26:27]
        hss = small[:, 27:28]
        hrstd = small[:, 28:29]
        bias_i = small[:, 29:30]
        bias_f = small[:, 30:31]
        head_gain = small[:, 32:40]
        m_state = small[:, 40:48]
        col_g = small[:, 48:80].rearrange("p (c h) -> p c h", c=CH)
        col_a = small[:, 80:112].rearrange("p (c h) -> p c h", c=CH)
        col_m = small[:, 112:144].rearrange("p (c h) -> p c h", c=CH)

        NORMS = [norm_mix_pre, norm_mix_post, norm_ffn_pre, norm_ffn_post, ple_norm_gate, ple_norm_out]
        SC_COL, HN_COL, FF_COL = 96, 120, 128

        def norm_col(which, layer, t=0):
            return (which * DEPTH + layer) * DT + t

        def sc_col(tap, t):
            return SC_COL + tap * DT + t

        def ff_col(layer, tap, t):
            return FF_COL + (layer * 3 + tap) * (FF // P) + t

        def half(h):
            return slice(h * HALF, (h + 1) * HALF)

        def block_source(key, k, i=0):
            layer, kind = key[0], key[1]
            r = slice(k * P, (k + 1) * P)
            if kind in ("c", "u", "b"):
                c0 = {"b": 0, "c": D, "u": 2 * D}[kind] + key[2] * BLOCKW
                return sc_w_in[0, r, c0:c0 + BLOCKW]
            if kind == "qk":
                two = ml_w_in[0, r, 0:2 * HEADS * QKH].rearrange("r (s c) -> r s c", s=2)
                return two[:, :, key[2] * 256:key[2] * 256 + 256]
            if kind in ("v", "o"):
                c0 = 2 * HEADS * QKH + (HEADS * VH if kind == "o" else 0) + key[2] * BLOCKW
                return ml_w_in[0, r, c0:c0 + BLOCKW]
            if kind == "mix":
                w = (sc_w_out, ml_w_out)[layer]
                return w[0, key[2] * 512 + k * P:key[2] * 512 + (k + 1) * P, key[3] * BLOCKW:(key[3] + 1) * BLOCKW]
            if kind == "up":
                part, g = key[2], key[3]
                c0 = 0 if part == 0 else FIRST_TILES * P + (part - 1) * 512 + g * 256
                two = ffn_w_up[layer, r, :].rearrange("r (s c) -> r s c", s=2)
                return two[:, :, bass.ds(i * 512 + c0, 256)] if not isinstance(i, int) else two[:, :, c0:c0 + 256]
            if kind == "down":
                part, g = key[2], key[3]
                r0 = (0 if part == 0 else FIRST_TILES * P + (part - 1) * 512) + k * P
                c = slice(g * BLOCKW, (g + 1) * BLOCKW)
                return ffn_w_down[layer, bass.ds(i * 512 + r0, P), c] if not isinstance(i, int) else ffn_w_down[layer, r0:r0 + P, c]
            if kind == "proj":
                return ple_w_proj[layer, r, key[2] * BLOCKW:(key[2] + 1) * BLOCKW]
            return ple_w_gate[layer, r, key[2] * BLOCKW:(key[2] + 1) * BLOCKW]

        def gain_of(key, k):
            which = {"c": 0, "u": 0, "b": 0, "qk": 0, "v": 0, "o": 0, "up": 2, "gate": 4}.get(key[1])
            return None if which is None else norm_col(which, key[0], k)

        def body_keys(layer, part):
            return [(layer, "up", part, 0), (layer, "up", part, 1), (layer, "down", part, 0), (layer, "down", part, 1)]

        def stages(e):
            e.start()
            for layer in range(DEPTH):
                kinds = ("c", "u", "b") if layer == 0 else ("qk", "v", "o")
                for part in range(2):
                    mix0, mix1 = (layer, "mix", part, 0), (layer, "mix", part, 1)
                    a, b, o = [(layer, kind, part) for kind in kinds]
                    if layer == 1 and part == 0:
                        e.empty(a, 1)
                        e.gates()
                    else:
                        e.empty(a, 0)
                        e.splits(b)
                        e.empty(a, 1)
                    e.empty(b, 0)
                    if layer == 0:
                        e.splits(o)
                        e.empty(b, 1)
                    else:
                        e.core(part, 0, o)
                        e.empty(b, 1)
                        e.core(part, 1, None)
                    e.empty(o, 0)
                    e.splits(mix0)
                    e.empty(o, 1)
                    e.empty(mix0, 0)
                    e.splits(mix1)
                    e.empty(mix0, 1)
                    if part == 0:
                        e.empty(mix1, 0)
                        e.splits((layer, kinds[0], 1))
                        e.empty(mix1, 1)
                up, down0, down1 = (layer, "up", 0, 0), (layer, "down", 0, 0), (layer, "down", 0, 1)
                boundary(e, layer, mix1, up, down0, 1)
                e.empty(up, 1)
                e.empty(down0, 0)
                e.splits(down1)
                e.empty(down0, 1)
                e.empty(down1, 0)
                e.splits((layer, "up", 1, 0))
                e.empty(down1, 1)
                e.loop(LOOPED, lambda: feed_part(e, layer, 1))
                feed_part(e, layer, PARTS - 1)
                proj0, proj1, gate0, gate1 = [(layer, kind, g) for kind in ("proj", "gate") for g in range(2)]
                boundary(e, layer, (layer, "down", PARTS - 1, 1), proj0, proj1, 3)
                e.empty(proj0, 1)
                e.empty(proj1, 0)
                e.splits(gate0)
                e.empty(proj1, 1)
                e.empty(gate0, 0)
                e.splits(gate1)
                e.empty(gate0, 1)
                if layer + 1 < DEPTH:
                    boundary(e, layer, gate1, (1, "qk", 0), (1, "v", 0), 5)
            for h in range(2):
                e.empty(gate1, h)
                e.norm(rs_post, c2)
                e.renew(layer, 5, h, (), final=True)
                e.store(h)

        def feed_part(e, layer, part):
            keys = body_keys(layer, part)
            for n, key in enumerate(keys):
                if part == PARTS - 1 and n == 3:
                    break
                e.empty(key, 0)
                e.splits(keys[n + 1] if n < 3 else (layer, "up", part + 1, 0))
                e.empty(key, 1)

        def boundary(e, layer, done, key0, key1, post):
            blocks = [(key0, k) for k in range(plan.groups[plan.at[key0]])]
            e.empty(done, 0)
            for b in blocks[:4]:
                e.split(*b)
            e.norm(rs_post, c2)
            if key0[1] == "proj":
                e.p_split(0)
            e.renew(layer, post, 0, blocks[4:])
            e.empty(done, 1)
            e.norm(rs[:, half(0)], c2_pre[:, 0:4])
            e.norm(rs_post, c2)
            if key0[1] == "proj":
                e.p_split(1)
            e.renew(layer, post, 1, [(key1, k) for k in range(plan.groups[plan.at[key1]])])
            e.empty(key0, 0)
            e.norm(rs[:, half(1)], c2_pre[:, 4:8])

        def last_branch(key):
            return key[1] == "gate" or (key[1] == "mix" and key[2] == 1) or (key[1] == "down" and key[2] == PARTS - 1)

        def is_loop(key):
            return key[1] in ("up", "down") and 1 <= key[2] < PARTS - 1

        class Common:

            def __init__(self, engine, compute):
                self.eng, self.nc = engine, compute
                self.c = Counts(S)
                self.i = 0

            def splits(self, key):
                for k in range(plan.groups[plan.at[key]]):
                    self.split(key, k)

            def loop(self, trips, body):
                with self.eng.Fori(0, trips) as i:
                    self.i = i
                    self.c.enter(i)
                    body()
                self.i = 0
                self.c.leave(trips)

            def split(self, key, k):
                pass

            def norm(self, dst, factors):
                pass

            def p_split(self, h):
                pass

            def gates(self):
                pass

            def store(self, h):
                pass

        with nc.Block() as block:

            @block.sync
            def _(sp):
                def load(key, k, i=0):
                    b = plan.block0[plan.at[key]] + k
                    if b >= RAWS:
                        sp.wait_ge(S["w_lo"], i * PER_PART["w_lo"] + b - RAWS + 1)
                    src = block_source(key, k, i)
                    dst = raw[:, b % RAWS, :]
                    if len(src.shape) == 3:
                        dst = dst.rearrange("p (s c) -> p s c", s=2)
                    sp.dma_start(dst, src).then_inc(raw_in[b % RAWS], 16)

                def group(key, i=0):
                    for k in range(plan.groups[plan.at[key]]):
                        load(key, k, i)

                for tb in range(CH):
                    sp.dma_start(y[:, tb, :], x[0, tb * P:(tb + 1) * P, :]).then_inc(x_in[tb], 16)
                    if tb == 0:
                        for w, v in enumerate(NORMS):
                            sp.dma_start(us[w * 16:w * 16 + 16, 0, 0:P],
                                         v.rearrange("l (t q) -> (l t) q", q=P)).then_inc(const_in, 16)
                        sp.dma_start(us[96:120, 0, 0:P],
                                     sc_w_conv.rearrange("l j (t q) -> (l j t) q", q=P)).then_inc(const_in, 16)
                        sp.dma_start(us[120:128, 0, 0:P],
                                     ml_head_norm.rearrange("l (t q) -> (l t) q", q=P)).then_inc(const_in, 16)
                        for layer in range(DEPTH):
                            sp.dma_start(us[0:66, 0, P * (1 + layer):P * (2 + layer)],
                                         ffn_w_conv[layer].rearrange("j (t q) -> (j t) q", q=P)).then_inc(const_in, 16)
                        bias = ml_gate_bias.rearrange("l g -> g l")
                        with nc.allow_non_contiguous_dma(reason="eight biases and eight columns of gate weights"):
                            sp.dma_start(bias_i[0:4, :], bias[0:4, :]).then_inc(const_in, 16)
                            sp.dma_start(bias_f[64:68, :], bias[4:8, :]).then_inc(const_in, 16)
                            sp.dma_start(gate_raw, ml_w_in[0, :, MLSTM_GATES:MLSTM_GATES + 2 * HEADS].rearrange(
                                "(k q) c -> q k c", q=P)).then_inc(const_in, 16)
                    if tb == 3:
                        for k in range(RAWS):
                            load((0, "c", 0), k)
                for k in range(RAWS, DT):
                    load((0, "c", 0), k)
                for layer in range(DEPTH):
                    kinds = ("c", "u", "b") if layer == 0 else ("qk", "v", "o")
                    for part in range(2):
                        for kind in kinds:
                            if (layer, kind, part) != (0, "c", 0):
                                group((layer, kind, part))
                        for g in range(2):
                            group((layer, "mix", part, g))
                    group((layer, "up", 0, 0))
                    for g in range(2):
                        group((layer, "down", 0, g))
                    sp.wait_ge(S["bank_free"], 8 * plan.at[(layer, "up", 0, 0)] + 1)
                    sp.dma_start(p_rows, p[layer, 0].rearrange("(c q) f -> q c f", q=P)).then_inc(p_in, 16)
                    with sp.Fori(0, LOOPED) as i:
                        for key in body_keys(layer, 1):
                            group(key, i)
                    for key in body_keys(layer, PARTS - 1):
                        group(key)
                    for g in range(2):
                        group((layer, "proj", g))
                    for g in range(2):
                        group((layer, "gate", g))
                for tb in range(CH):
                    sp.wait_ge(S["out_c"], 2 * tb + 2)
                    sp.dma_start(out[0, tb * P:(tb + 1) * P, :], out_rows[:, tb % 3, :]).then_inc(out_done[tb % 3], 16)
                for s in range(3):
                    sp.wait_ge(out_done[s], 16 * len(range(s, CH, 3)))

            @block.tensor
            def _(pe):
                c = Counts(S)

                def bank_free(n, h, t, i=0):
                    pe.wait_ge(S["bank_free"], i * PER_PART["bank_free"] + 8 * n + 4 * h + t + 1)

                def gemm(key, h, i=0, ready=None, extra=None):
                    n = plan.at[key]
                    b0, K = plan.block0[n], plan.groups[n]
                    src_hi, src_lo = (z_hi, z_lo) if key[1] in ("mix", "down", "proj") else (x_hi, x_lo)
                    for k in range(K):
                        if extra:
                            extra(k)
                        if h == 0:
                            pe.wait_ge(S["w_lo"], i * PER_PART["w_lo"] + b0 + k + 1)
                        if ready:
                            ready(k)
                        slot = (b0 + k) % SLOTS
                        for t in range(4):
                            if k == 0 and n > 0:
                                bank_free(n - 1, h, t, i)
                            for step, (w, m) in enumerate(((w_hi, src_hi), (w_hi, src_lo), (w_lo, src_hi))):
                                if key[1] == "v":
                                    left, right = m[:, k, h * HALF + t * P:h * HALF + (t + 1) * P], w[:, slot, :]
                                else:
                                    left, right = w[:, slot, t * P:(t + 1) * P], m[:, k, half(h)]
                                ins = nc.tensor.matmul(psum[:, 4 * h + t, :], left, right,
                                                       start=(k == 0 and step == 0), stop=(k == K - 1 and step == 2))
                            if k == K - 1:
                                ins.then_inc(S["acc"], 1)
                            elif h == 1 and t == 3 and K == SLOTS:
                                ins.then_inc(S["block_used"], 1)

                def z_ready(key, h, i=0):
                    layer, kind, part, g = key
                    if g == 1:
                        return None
                    per = 4 if kind == "mix" else 2
                    maker = {("mix", 0): "b", ("mix", 1): "o"}.get((kind, layer))

                    def ready(k):
                        m = plan.at[(layer, maker, part) if maker else (layer, "up", part, k // 2)]
                        pe.wait_ge(S["z_ready"], i * PER_PART["z_ready"] + plan.z0[m] + h * per + k % per + 1)
                    return ready

                def group(key, i=0):
                    for h in range(2):
                        gemm(key, h, i, z_ready(key, h, i) if key[1] in ("mix", "down") else None)

                def norm_sums(h, bank, adds):
                    pe.wait_ge(S["sq_sum"], adds)
                    for j in range(4):
                        ins = nc.tensor.matmul(psum[:, bank, j:j + 1], sq[:, h, j * P:(j + 1) * P], ones[:, 0:1],
                                               start=True, stop=True)
                    ins.then_inc(*c.up("norm_col"))

                def norm_spread(bank):
                    pe.wait_ge(*c.next("norm_diag"))
                    nc.tensor.matmul(psum[:, bank, :], ones[:, :], diag, start=True, stop=True).then_inc(
                        *c.up("norm_row"))

                def rs_read(k):
                    pe.wait_ge(S["rs"], k)

                def p_transpose(h):
                    for f in range(2):
                        for j in range(4):
                            ins = nc.tensor.transpose(psum[:, 4 * h + 2 + f, j * P:(j + 1) * P],
                                                      p_rows[:, 4 * h + j, f * P:(f + 1) * P], ident[:, :])
                        ins.then_inc(*c.up("p_t"))

                def turn(nth, done, key0):
                    n = plan.at[done]
                    K = plan.groups[n]
                    proj = key0[1] == "proj"

                    def x_ready(h):
                        if proj:
                            return None
                        return lambda k: pe.wait_ge(S["x_ready"], 2 * DT * nth + DT * h + k + 1)

                    def post0(k):
                        if k == K - 2:
                            bank_free(n, 0, 3)
                            norm_sums(0, 0, 28 * nth + 10)
                        if k == K - 1:
                            norm_spread(0)
                            if proj:
                                pe.wait_ge(p_in, 16 * (done[0] + 1))
                                p_transpose(0)

                    gemm(done, 0)
                    gemm(done, 1, extra=post0)
                    rs_read(2 + 4 * nth + 1)
                    if proj:
                        pe.wait_ge(*c.next("p_lo", 2))
                    gemm(key0, 0, ready=x_ready(0))
                    bank_free(n, 1, 3)
                    norm_sums(0, 4, 28 * nth + 17)
                    norm_sums(1, 5, 28 * nth + 21)
                    norm_spread(4)
                    norm_spread(5)
                    if proj:
                        p_transpose(1)
                        pe.wait_ge(*c.next("p_lo", 2))
                    rs_read(2 + 4 * nth + 3)
                    gemm(key0, 1, ready=x_ready(1))
                    bank_free(n + 1, 0, 0)
                    norm_sums(1, 0, 28 * nth + 28)
                    norm_spread(0)
                    rs_read(2 + 4 * nth + 4)

                def gates_pe():
                    bank_free(plan.at[(1, "qk", 0)], 0, 1)
                    pe.wait_ge(*c.next("gate_w"))
                    for h in range(2):
                        for k in range(DT):
                            for step, (w, m) in enumerate(((zf_hi, x_hi), (zf_hi, x_lo), (zf_lo, x_hi))):
                                ins = nc.tensor.matmul(psum[0:68, h, :], w[:, k, :], m[:, k, half(h)],
                                                       start=(k == 0 and step == 0), stop=(k == DT - 1 and step == 2))
                        ins.then_inc(*c.up("gate_acc"))
                    pe.wait_ge(*c.next("gate_ev", 4))

                def gate_columns(k):
                    if k != DT - 2:
                        return
                    bank_free(plan.at[(1, "qk", 0)], 1, 3)
                    pe.wait_ge(S["gate_step"], GATE_ROWS_DONE)
                    pe.wait_ge(S["gate_e"], GATE_EXPS)
                    for src, bank in ((rows, 4), (rows2, 6)):
                        for ch in range(CH):
                            ins = nc.tensor.transpose(psum[:, bank + ch // 4, (ch % 4) * P:(ch % 4 + 1) * P],
                                                      src[:, ch * P:(ch + 1) * P], ident[:, :])
                            if ch % 4 == 3:
                                ins.then_inc(*c.up("gate_t"))

                def core_step(part, h):
                    s = 4 * h

                    def step(k):
                        if k == 0:
                            bank_free(plan.at[(1, "v", part)], h, 3)
                        if 1 <= k <= 8:
                            u = k - 1
                            ch, j = 4 * h + u // 2, u % 2
                            pe.wait_ge(*c.next("core_sw"))
                            pe.wait_ge(*c.now("core_hn"))
                            pe.wait_ge(*c.now("c_upd"))
                            c.skip("core_hn")
                            c.skip("c_upd")
                            nc.tensor.matmul(psum[:, s + 1, 0:VH + 1], sw, v_sb[:, ch, j, :], start=True, stop=False)
                            nc.tensor.matmul(psum[:, s + 1, 0:VH + 1], qw, state[:, j, :], start=False,
                                             stop=True).then_inc(*c.up("core_num"))
                            nc.tensor.matmul(psum[:, s + 2, 0:VH + 1], kw, v_sb[:, ch, j, :], start=True,
                                             stop=True).then_inc(*c.up("core_u"))
                        if k <= 7:
                            ch, j = 4 * h + k // 2, k % 2
                            cols = slice(ch * P, (ch + 1) * P)
                            head = 2 * part + j
                            nc.tensor.transpose(psum[:, s, 0:P], big[:, 2 + j, cols], ident[:, :])
                            nc.tensor.matmul(psum[:, s, P:2 * P], big[:, 2 + j, cols], big[:, j, cols],
                                             start=True, stop=True)
                            for place, row in ((2, head), (3, 32 + head)):
                                ins = nc.tensor.matmul(psum[:, s, place * P:(place + 1) * P],
                                                       ident[0:64, row:row + 1].to_broadcast([64, P]),
                                                       rows[0:64, cols], start=True, stop=True)
                            ins.then_inc(*c.up("core_a"))
                        if k >= 2:
                            pe.wait_ge(*c.next("core_h2"))
                            pe.wait_ge(*c.now("core_h"))
                            c.skip("core_h", 2)
                            for e in range(2):
                                ins = nc.tensor.transpose(psum[:, s + 3, e * P:(e + 1) * P],
                                                          hn2[:, e * P:(e + 1) * P], ident[:, :])
                            ins.then_inc(*c.up("core_ht"))
                        if k == 9:
                            pe.wait_ge(*c.now("core_h"))
                            pe.wait_ge(*c.now("c_upd"))
                    return step

                pe.wait_ge(S["const"], 5)
                pe.wait_ge(const_in, 16 * 13)
                at = 0
                for j, r in enumerate((P, 66, 66)):
                    ins = nc.tensor.transpose(psum[:, 7, at:at + r], us[0:r, 0, j * P:(j + 1) * P], ident[0:r, 0:r])
                    at += r
                ins.then_inc(*c.up("const_t"))
                for e in range(2 * CH):
                    if e % 2 == 0:
                        pe.wait_ge(x_in[e // 2], 16)
                    if e >= 6:
                        pe.wait_ge(S["xin_ready"], e - 5)
                    for j in range(4):
                        f = 4 * (e % 2) + j
                        ins = nc.tensor.transpose(psum[:, e % 6, j * P:(j + 1) * P], y[:, e // 2, f * P:(f + 1) * P],
                                                  ident[:, :])
                    ins.then_inc(*c.up("xin_t"))
                pe.wait_ge(*c.next("const_c"))
                norm_spread(6)
                norm_spread(7)
                pe.wait_ge(S["xin_ready"], 2 * CH)
                rs_read(2)

                for part in range(2):
                    for kind in ("c", "u", "b"):
                        group((0, kind, part))
                    group((0, "mix", part, 0))
                    if part == 0:
                        group((0, "mix", part, 1))
                for layer in range(DEPTH):
                    if layer == 1:
                        for part in range(2):
                            if part == 0:
                                gates_pe()
                            else:
                                group((1, "qk", 1))
                            gemm((1, "v", part), 0, extra=gate_columns if part == 0 else None)
                            if part == 0:
                                pe.wait_ge(S["gate_step"], GATE_COLUMNS_DONE)
                            for h, (kind, half_of) in enumerate((("v", 1), ("o", 0))):
                                step = core_step(part, h)
                                gemm((1, kind, part), half_of, extra=step)
                                step(8)
                                step(9)
                            gemm((1, "o", part), 1)
                            for h in range(2):
                                gemm((1, "mix", part, 0), h, ready=z_ready((1, "mix", part, 0), h))
                            if part == 0:
                                group((1, "mix", part, 1))
                    turn(3 * layer, (layer, "mix", 1, 1), (layer, "up", 0, 0))
                    for g in range(2):
                        group((layer, "down", 0, g))
                    with pe.Fori(0, LOOPED) as i:
                        for key in body_keys(layer, 1):
                            group(key, i)
                    for key in body_keys(layer, PARTS - 1)[:3]:
                        group(key)
                    turn(3 * layer + 1, (layer, "down", PARTS - 1, 1), (layer, "proj", 0))
                    group((layer, "proj", 1))
                    group((layer, "gate", 0))
                    if layer == 0:
                        turn(2, (0, "gate", 1), (1, "qk", 0))
                gemm((1, "gate", 1), 0)
                gemm((1, "gate", 1), 1)
                n = plan.at[(1, "gate", 1)]
                for h in range(2):
                    bank_free(n, h, 3)
                    norm_sums(h, 4 * h, 28 * 5 + 10 + 4 * h)
                    norm_spread(4 * h)
                    rs_read(2 + 4 * 5 + 1 + h)
                    for e in range(8 * h, 8 * h + 8):
                        if e % 2 == 0:
                            pe.wait_ge(S["x_new"], 2 * DT * 5 + DT * (h + 1))
                        if e >= 4:
                            pe.wait_ge(S["out_c"], e - 3)
                        for j in range(4):
                            ins = nc.tensor.transpose(psum[:, e % 4, j * P:(j + 1) * P],
                                                      y[:, 4 * (e % 2) + j, (e // 2) * P:(e // 2 + 1) * P], ident[:, :])
                        ins.then_inc(*c.up("out_t"))

            @block.scalar
            def _(act):
                class Scalar(Common):
                    norms = 0

                    def banks(self, key, h, t):
                        self.eng.wait_ge(S["bank_free"], self.i * PER_PART["bank_free"] + 8 * plan.at[key] + 4 * h + t + 1)

                    def start(self):
                        act.wait_ge(*self.c.next("const_c", 2))
                        for e in range(2 * CH):
                            tb, r = e // 2, e % 2
                            if r == 0:
                                act.wait_ge(x_in[tb], 16)
                                act.wait_ge(*self.c.now("xin_ss"))
                                nc.scalar.activation(big[:, 0, :], y[:, tb, :], ACT.Square, scale=32.0,
                                                     accum_out=ss_in[:, tb:tb + 1]).then_inc(*self.c.up("xin_ss"))
                            act.wait_ge(*self.c.next("xin_t"))
                            nc.scalar.activation(x_hi[:, 4 * r:4 * r + 4, tb * P:(tb + 1) * P],
                                                 psum[:, e % 6, :].rearrange("p (f n) -> p f n", f=4),
                                                 ACT.Copy).then_inc(*self.c.up("xin_hi"))
                            if e < 8:
                                self.split((0, "c", 0), e)
                        for h in range(2):
                            self.row(rs[:, half(h)])

                    def split(self, key, k):
                        n = plan.at[key]
                        b = plan.block0[n] + k
                        old = b - SLOTS
                        if old >= 0:
                            m = max(g for g in range(len(plan.groups)) if plan.block0[g] <= old)
                            kk = old - plan.block0[m]
                            if plan.groups[m] == SLOTS and kk < SLOTS - 1:
                                self.eng.wait_ge(S["block_used"], self.i * PER_PART["block_used"] + plan.used0[m] + kk + 1)
                            else:
                                self.eng.wait_ge(S["acc"], self.i * PER_PART["acc"] + 8 * m + 8)
                        self.eng.wait_ge(raw_in[b % RAWS], self.i * (16 * PER_PART["w_lo"] // RAWS) + 16 * (b // RAWS + 1))
                        g = gain_of(key, k)
                        self.nc.activation(w_hi[:, b % SLOTS, :], raw[:, b % RAWS, :], ACT.Copy,
                                           scale=1.0 if g is None else gains[:, g:g + 1]).then_inc(*self.c.up("w_hi"))

                    def row(self, dst):
                        bank = ([6, 7] + 5 * [0, 4, 5, 0] + [0, 4])[self.norms]
                        self.norms += 1
                        act.wait_ge(*self.c.next("norm_row"))
                        nc.scalar.activation(dst, psum[:, bank, :], ACT.Copy).then_inc(*self.c.up("rs"))

                    def norm(self, dst, factors):
                        bank = ([6, 7] + 5 * [0, 4, 5, 0] + [0, 4])[self.norms]
                        act.wait_ge(*self.c.next("norm_col"))
                        nc.scalar.activation(c1, psum[:, bank, 0:4], ACT.Copy).then_inc(*self.c.up("norm_c1"))
                        self.row(dst)

                    def square(self, src, h, t):
                        self.eng.wait_ge(*self.c.now("sq_sum"))
                        self.nc.activation(sq[:, h, :] if t == 0 else sqt, src, ACT.Square).then_inc(*self.c.up("sq_tmp"))
                        if t > 0:
                            self.c.skip("sq_sum")

                    def z_part(self, zt, h, b):
                        self.eng.wait_ge(*self.c.next("act_prod"))
                        self.nc.activation(z_hi[:, zt, half(h)], us[:, b, :], ACT.Copy).then_inc(*self.c.up("z_hi"))

                    def empty(self, key, h):
                        kind = key[1]
                        if kind in ("mix", "down") and last_branch(key):
                            for t in range(4):
                                self.banks(key, h, t)
                                self.square(y[:, 4 * key[3] + t, half(h)], h, 4 * key[3] + t)
                        elif kind == "gate":
                            for t in range(5):
                                if t < 4:
                                    self.banks(key, h, t)
                                    self.nc.activation(v_tmp[:, t % 2, :], v_tmp[:, t % 2, :], ACT.Sigmoid).then_inc(
                                        *self.c.up("sig"))
                                if t > 0:
                                    self.eng.wait_ge(*self.c.next("gated"))
                                    self.square(y[:, 4 * key[2] + t - 1, half(h)], h, 4 * key[2] + t - 1)
                        elif kind == "b":
                            for t in range(4):
                                self.z_part(t, h, t % 2)
                        elif kind == "o":
                            for t0 in (0, 2):
                                for t in (t0, t0 + 1):
                                    self.banks(key, h, t)
                                    self.nc.activation(us[:, t % 2, :], us[:, t % 2, :], ACT.Tanh, scale=0.5).then_inc(
                                        *self.c.up("sig"))
                                for t in (t0, t0 + 1):
                                    self.z_part(t, h, t % 2)
                        elif kind == "up":
                            self.c.skip("tap", 4)
                            for j in range(2):
                                self.eng.wait_ge(*self.c.next("tap"))
                                self.nc.activation(v_tmp[:, j, :], v_tmp[:, j, :], ACT.Gelu_apprx_tanh).then_inc(
                                    *self.c.up("gelu"))
                            for j in range(2):
                                self.z_part(2 * key[3] + j, h, j)

                    def renew(self, layer, which, h, blocks, final=False):
                        for k in range(DT):
                            self.eng.wait_ge(*self.c.next("x_new"))
                            if not final:
                                nc.scalar.activation(x_hi[:, k, half(h)], xn[:, k % 2, :], ACT.Copy).then_inc(
                                    *self.c.up("x_hi"))
                                self.square(xn[:, k % 2, :], h, k)
                            if k >= 2 and k - 2 < len(blocks):
                                self.split(*blocks[k - 2])
                        for b in blocks[6:]:
                            self.split(*b)

                    def p_split(self, h):
                        for f in range(2):
                            act.wait_ge(*self.c.next("p_t"))
                            nc.scalar.activation(z_hi[:, f, half(h)], psum[:, 4 * h + 2 + f, :], ACT.Copy).then_inc(
                                *self.c.up("p_hi"))

                    def gates(self):
                        act.wait_ge(S["gate_step"], GATE_ABS)
                        a = y[0:4, 3, :]
                        nc.scalar.activation(a, a, ACT.Exp, scale=-1.0).then_inc(*self.c.up("gate_e"))
                        act.wait_ge(*self.c.now("gate_e"))
                        nc.scalar.activation(a, a, ACT.Ln, bias=1.0).then_inc(*self.c.up("gate_e"))
                        act.wait_ge(S["gate_step"], GATE_ROWS_DONE)
                        for dst, src, scale in ((rows[32:36, :], y[0:4, 1, :], 1.0), (rows[64:68, :], y[0:4, 2, :], 1.0),
                                                (rows2[32:36, :], y[0:4, 5, :], -1.0)):
                            nc.scalar.activation(dst, src, ACT.Exp, scale=scale).then_inc(*self.c.up("gate_e"))

                    def core(self, part, h, nxt):
                        for k in range(10):
                            if 1 <= k <= 8:
                                act.wait_ge(*self.c.next("core_r"))
                                act.wait_ge(*self.c.now("core_h2"))
                                nc.scalar.activation(hn, psum[:, 4 * h + 1, 0:VH], ACT.Copy, scale=rden).then_inc(
                                    *self.c.up("core_hn"))
                                act.wait_ge(*self.c.now("core_hn"))
                                nc.scalar.activation(sqt_core, hn, ACT.Square, accum_out=hss).then_inc(
                                    *self.c.up("core_ss"))
                                self.c.skip("core_h2")
                            if k <= 7:
                                act.wait_ge(*self.c.next("core_d"))
                                nc.scalar.activation(dmat, dmat, ACT.Exp).then_inc(*self.c.up("core_e"))
                            if k >= 2:
                                u = k - 2
                                ch, j = 4 * h + u // 2, u % 2
                                act.wait_ge(*self.c.next("core_ht"))
                                for e in range(2):
                                    hg = 2 * (2 * part + j) + e
                                    nc.scalar.activation(big[:, j + 2 * e, ch * P:(ch + 1) * P],
                                                         psum[:, 4 * h + 3, e * P:(e + 1) * P], ACT.Copy,
                                                         scale=head_gain[:, hg:hg + 1]).then_inc(*self.c.up("core_h"))
                            if nxt and 1 <= k <= 8:
                                self.split(nxt, k - 1)

                stages(Scalar(act, nc.scalar))

            @block.vector
            def _(dve):
                class Vector(Common):
                    def acc(self, key, h, t):
                        self.eng.wait_ge(S["acc"], self.i * PER_PART["acc"] + 8 * plan.at[key] + 4 * h + t + 1)
                        return psum[:, 4 * h + t, :]

                    def column(self, key, tap, t):
                        layer, _, part, g = key
                        c0 = ff_col(layer, tap, (0 if part == 0 else FIRST_TILES + 4 * (part - 1)) + 2 * g + t)
                        return gains[:, c0:c0 + 1] if isinstance(self.i, int) else gains[:, bass.ds(self.i * 4 + c0, 1)]

                    def start(self):
                        dve.wait_ge(*self.c.next("const_t"))
                        nc.vector.tensor_copy(gains[:, :], psum[:, 7, 0:260]).then_inc(*self.c.up("const_c"))
                        dve.wait_ge(*self.c.now("const_c"))
                        nc.vector.tensor_scalar(head_gain, gains[:, HN_COL:HN_COL + 8], 8.0, None, ALU.mult).then_inc(
                            *self.c.up("const_c"))
                        for e in range(2 * CH):
                            tb, r = e // 2, e % 2
                            cols = slice(tb * P, (tb + 1) * P)
                            dve.wait_ge(*self.c.next("xin_hi"))
                            nc.vector.tensor_tensor(x_lo[:, 4 * r:4 * r + 4, cols],
                                                    psum[:, e % 6, :].rearrange("p (f n) -> p f n", f=4),
                                                    x_hi[:, 4 * r:4 * r + 4, cols].bitcast(FP32),
                                                    ALU.subtract).then_inc(*self.c.up("xin_ready"))
                            if e < 8:
                                self.split((0, "c", 0), e)
                        for h in range(2):
                            if h == 0:
                                dve.wait_ge(*self.c.next("norm_c2"))
                            self.spread(c2_pre[:, 4 * h:4 * h + 4])

                    def spread(self, factors):
                        nc.vector.tensor_tensor(diag.rearrange("p (j n) -> p j n", j=4),
                                                ident[:, :].unsqueeze(1).to_broadcast([P, 4, P]),
                                                factors.unsqueeze(2).to_broadcast([P, 4, P]),
                                                ALU.mult).then_inc(*self.c.up("norm_diag"))
                        dve.wait_ge(*self.c.next("rs"))

                    def norm(self, dst, factors):
                        dve.wait_ge(*self.c.next("norm_c2"))
                        self.spread(factors)

                    def split(self, key, k):
                        b = plan.block0[plan.at[key]] + k
                        self.eng.wait_ge(*self.c.next("w_hi"))
                        g = gain_of(key, k)
                        w, hi = raw[:, b % RAWS, :], w_hi[:, b % SLOTS, :].bitcast(FP32)
                        if g is None:
                            ins = self.nc.tensor_tensor(w_lo[:, b % SLOTS, :], w, hi, ALU.subtract)
                        else:
                            ins = self.nc.scalar_tensor_tensor(w_lo[:, b % SLOTS, :], w, gains[:, g:g + 1], hi,
                                                               ALU.mult, ALU.subtract)
                        ins.then_inc(*self.c.up("w_lo"))

                    def add_squares(self, h, t):
                        if t == 0:
                            self.c.skip("sq_tmp")
                            return
                        self.eng.wait_ge(*self.c.next("sq_tmp"))
                        self.eng.wait_ge(*self.c.now("sq_sum"))
                        self.nc.tensor_tensor(sq[:, h, :], sq[:, h, :], sqt, ALU.add).then_inc(*self.c.up("sq_sum"))

                    def empty(self, key, h):
                        kind, c, w = key[1], self.c, self.nc
                        wait = self.eng.wait_ge
                        rsh = rs[:, half(h)]
                        if kind in ("mix", "down"):
                            for t in range(4):
                                bank = self.acc(key, h, t)
                                tile = y[:, 4 * key[3] + t, half(h)]
                                if key[2] == 0:
                                    w.tensor_copy(tile, bank).then_inc(*c.up("bank_free"))
                                else:
                                    wait(*c.now("bank_free", 3))
                                    w.tensor_tensor(tile, bank, tile, ALU.add).then_inc(*c.up("bank_free"))
                                if last_branch(key) and t > 0:
                                    self.add_squares(h, 4 * key[3] + t - 1)
                            if last_branch(key):
                                self.add_squares(h, 4 * key[3] + 3)
                        elif kind == "proj":
                            wait(*c.now("x_t"))
                            for t in range(4):
                                bank = self.acc(key, h, t)
                                w.tensor_copy(y[:, 4 * key[2] + t, half(h)], bank).then_inc(*c.up("bank_free"))
                        elif kind == "gate":
                            for t in range(6):
                                if t < 4:
                                    bank = self.acc(key, h, t)
                                    wait(*c.now("gated"))
                                    w.tensor_tensor(v_tmp[:, t % 2, :], bank, rsh, ALU.mult).then_inc(
                                        *c.up("bank_free"))
                                if 1 <= t <= 4:
                                    tile = y[:, 4 * key[2] + t - 1, half(h)]
                                    wait(*c.next("sig"))
                                    w.tensor_tensor(tile, v_tmp[:, (t - 1) % 2, :], tile, ALU.mult).then_inc(
                                        *c.up("gated"))
                                if t >= 2:
                                    self.add_squares(h, 4 * key[2] + t - 2)
                        elif kind == "c":
                            wait(*c.now("act_prod"))
                            for t in range(4):
                                bank = self.acc(key, h, t)
                                w.tensor_tensor(conv_out[:, t, half(h)], bank, rsh, ALU.mult).then_inc(
                                    *c.up("bank_free"))
                        elif kind == "u":
                            for t in range(4):
                                cu, res = conv_in[:, t % 2, :], conv_out[:, t, half(h)]
                                bank = self.acc(key, h, t)
                                wait(*c.now("cu"))
                                if h == 0:
                                    w.memset(cu[:, 0:2], 0.0).then_inc(*c.up("halo"))
                                else:
                                    w.tensor_copy(cu[:, 0:2], halo_keep[:, t, :]).then_inc(*c.up("halo"))
                                w.tensor_tensor(cu[:, 2:2 + HALF], bank, rsh, ALU.mult).then_inc(*c.up("bank_free"))
                                wait(*c.now("bank_free"))
                                w.tensor_tensor(cu[:, 2:2 + HALF], cu[:, 2:2 + HALF], res, ALU.mult).then_inc(*c.up("cu"))
                                wait(*c.now("cu"))
                                w.tensor_copy(halo_keep[:, t, :], cu[:, HALF:HALF + 2]).then_inc(*c.up("halo"))
                                tile = 4 * key[2] + t
                                col = [gains[:, sc_col(tap, tile):sc_col(tap, tile) + 1] for tap in range(3)]
                                w.tensor_scalar(res, cu[:, 0:HALF], col[0], None, ALU.mult).then_inc(*c.up("cu"))
                                for tap in (1, 2):
                                    wait(*c.now("cu"))
                                    w.scalar_tensor_tensor(res, cu[:, tap:tap + HALF], col[tap], res, ALU.mult,
                                                           ALU.add).then_inc(*c.up("cu"))
                        elif kind == "b":
                            wait(*c.now("cu"))
                            for t in range(5):
                                if t < 4:
                                    bank = self.acc(key, h, t)
                                    if t == 0:
                                        wait(*c.now("z_ready"))
                                    elif t >= 2:
                                        wait(*c.now("z_ready"))
                                    w.tensor_tensor(us[:, t % 2, :], bank, rsh, ALU.mult).then_inc(*c.up("bank_free"))
                                if t >= 1:
                                    wait(*c.now("bank_free", 1 if t < 4 else 0))
                                    w.tensor_tensor(us[:, (t - 1) % 2, :], us[:, (t - 1) % 2, :],
                                                    conv_out[:, t - 1, half(h)], ALU.mult).then_inc(*c.up("act_prod"))
                                    c.skip("z_ready")
                        elif kind == "up":
                            wait(*c.now("tap"))
                            for j in range(2):
                                g_in = conv_in[:, j, :]
                                if h == 0:
                                    w.memset(g_in[:, 0:2], 0.0).then_inc(*c.up("halo"))
                                else:
                                    w.tensor_copy(g_in[:, 0:2], g_in[:, HALF:HALF + 2]).then_inc(*c.up("halo"))
                            wait(*c.now("halo"))
                            for j in range(2):
                                bank = self.acc(key, h, j)
                                w.tensor_tensor(conv_in[:, j, 2:2 + HALF], bank, rsh, ALU.mult).then_inc(
                                    *c.up("bank_free"))
                            wait(*c.now("z_ready"))
                            for j in range(2):
                                bank = self.acc(key, h, 2 + j)
                                w.tensor_tensor(us[:, j, :], bank, rsh, ALU.mult).then_inc(*c.up("bank_free"))
                            wait(*c.now("bank_free", 2))
                            for j in range(2):
                                w.tensor_scalar(v_tmp[:, j, :], conv_in[:, j, 0:HALF], self.column(key, 0, j), None,
                                                ALU.mult).then_inc(*c.up("tap"))
                            for tap in (1, 2):
                                for j in range(2):
                                    wait(*c.now("tap", 1))
                                    w.scalar_tensor_tensor(v_tmp[:, j, :], conv_in[:, j, tap:tap + HALF],
                                                           self.column(key, tap, j), v_tmp[:, j, :], ALU.mult,
                                                           ALU.add).then_inc(*c.up("tap"))
                            for j in range(2):
                                wait(*c.next("gelu"))
                                w.tensor_tensor(us[:, j, :], us[:, j, :], v_tmp[:, j, :], ALU.mult).then_inc(
                                    *c.up("act_prod"))
                            c.skip("z_ready", 2)
                        elif kind == "qk":
                            wait(*c.now("act_prod"))
                            for t in range(4):
                                bank = self.acc(key, h, t)
                                w.scalar_tensor_tensor(big[:, t, half(h)], bank, 1.0 if t < 2 else QKH ** -0.5, rsh,
                                                       ALU.mult, ALU.mult).then_inc(*c.up("bank_free"))
                        elif kind == "v":
                            wait(*c.now("c_upd"))
                            wait(*c.now("core_sw"))
                            for t in range(4):
                                bank = self.acc(key, h, t)
                                w.tensor_scalar(v_sb[:, 4 * h + t, :, 0:VH], bank.rearrange("p (j e) -> p j e", j=2),
                                                c2_pre[:, 4 * h + t:4 * h + t + 1], ONES, ALU.mult,
                                                ALU.mult).then_inc(*c.up("bank_free"))
                        elif kind == "o":
                            if h == 0:
                                wait(*c.now("core_h"))
                            for t0 in (0, 2):
                                wait(*c.now("z_ready"))
                                for t in (t0, t0 + 1):
                                    bank = self.acc(key, h, t)
                                    w.tensor_tensor(us[:, t % 2, :], bank, rsh, ALU.mult).then_inc(*c.up("bank_free"))
                                for t in (t0, t0 + 1):
                                    wait(*c.next("sig"))
                                    w.scalar_tensor_tensor(us[:, t % 2, :], us[:, t % 2, :], 1.0,
                                                           big[:, t // 2 + 2 * (t % 2), half(h)], ALU.add,
                                                           ALU.mult).then_inc(*c.up("act_prod"))
                                    c.skip("z_ready")

                    def renew(self, layer, which, h, blocks, final=False):
                        c = self.c
                        for k in range(DT):
                            g = norm_col(which, layer, k)
                            tile = y[:, k, half(h)]
                            if not final:
                                dve.wait_ge(*c.now("x_ready", 1 if k else 0))
                                dve.wait_ge(*c.now("sq_tmp"))
                            else:
                                dve.wait_ge(*c.now("x_new"))
                            nc.vector.scalar_tensor_tensor(xn[:, k % 2, :], tile, gains[:, g:g + 1], rs_post, ALU.mult,
                                                           ALU.mult).then_inc(*c.up("x_t"))
                            if not final and k > 0:
                                self.add_squares(h, k - 1)
                            dve.wait_ge(*c.now("x_t"))
                            dve.wait_ge(*c.next("x_old"))
                            nc.vector.tensor_tensor(tile if final else xn[:, k % 2, :], xn[:, k % 2, :],
                                                    x_old[:, k % 2, :], ALU.add).then_inc(*c.up("x_new"))
                            c.skip("x_ready")
                            if k >= 2 and k - 2 < len(blocks):
                                self.split(*blocks[k - 2])
                        if not final:
                            self.add_squares(h, DT - 1)
                        for b in blocks[6:]:
                            self.split(*b)

                    def p_split(self, h):
                        for f in range(2):
                            dve.wait_ge(*self.c.next("p_hi"))
                            nc.vector.tensor_tensor(z_lo[:, f, half(h)], psum[:, 4 * h + 2 + f, :],
                                                    z_hi[:, f, half(h)].bitcast(FP32), ALU.subtract).then_inc(
                                *self.c.up("p_lo"))

                    def gates(self):
                        c, v = self.c, nc.vector
                        g0 = norm_col(0, 1)
                        v.tensor_tensor(gate_g, gate_raw, gains[:, g0:g0 + DT].unsqueeze(2).to_broadcast([P, DT, 8]),
                                        ALU.mult).then_inc(*c.up("gate_step"))
                        v.memset(zf_hi.bitcast(FP32), 0.0).then_inc(*c.up("gate_step"))
                        v.memset(zf_lo.bitcast(FP32), 0.0).then_inc(*c.up("gate_step"))
                        dve.wait_ge(*c.now("gate_step"))
                        for to, of in ((0, 0), (64, 4)):
                            v.tensor_copy(zf_hi[:, :, to:to + 4], gate_g[:, :, of:of + 4]).then_inc(*c.up("gate_step"))
                        dve.wait_ge(*c.now("gate_step"))
                        for to, of in ((0, 0), (64, 4)):
                            ins = v.tensor_tensor(zf_lo[:, :, to:to + 4], gate_g[:, :, of:of + 4],
                                                  zf_hi[:, :, to:to + 4].bitcast(FP32), ALU.subtract)
                        ins.then_inc(*c.up("gate_w"))
                        chunk_on = y[0:4, 4, :]
                        v.memset(rows, 0.0).then_inc(*c.up("gate_step"))
                        v.memset(rows2, 0.0).then_inc(*c.up("gate_step"))
                        v.memset(chunk_on, 1.0).then_inc(*c.up("gate_step"))
                        v.memset(v_sb[:, :, :, VH:VH + 1], 1.0).then_inc(*c.up("gate_step"))
                        dve.wait_ge(*c.now("gate_step"))
                        v.memset(chunk_on.rearrange("p (c n) -> p c n", n=P)[:, :, 0:1], 0.0).then_inc(
                            *c.up("gate_step"))
                        for h in range(2):
                            dve.wait_ge(*c.next("gate_acc"))
                            for q, r in ((0, 0), (1, 64)):
                                v.tensor_tensor(y[r:r + 4, q, half(h)], psum[r:r + 4, h, :], rs[r:r + 4, half(h)],
                                                ALU.mult).then_inc(*c.up("gate_ev"))
                        dve.wait_ge(*c.now("gate_ev"))
                        ig, f, lf, m, b = (y[0:4, q, :] for q in (0, 2, 3, 5, 7))
                        v.tensor_scalar(ig, ig, bias_i[0:4, :], None, ALU.add).then_inc(*c.up("gate_step"))
                        v.tensor_scalar(f, y[64:68, 1, :], bias_f[64:68, :], None, ALU.add).then_inc(
                            *c.up("gate_step"))
                        dve.wait_ge(*c.now("gate_step"))
                        v.scalar_tensor_tensor(lf, f, -1.0, f, ALU.mult, ALU.max).then_inc(*c.up("gate_step"))
                        assert c.n["gate_step"] == GATE_ABS
                        dve.wait_ge(*c.next("gate_e", 2))
                        v.scalar_tensor_tensor(lf, f, 0.0, lf, ALU.min, ALU.subtract).then_inc(*c.up("gate_step"))
                        dve.wait_ge(*c.now("gate_step"))
                        v.tensor_tensor_scan(m, lf, ig, 0.0, ALU.add, ALU.max).then_inc(*c.up("gate_step"))
                        v.tensor_tensor_scan(b, chunk_on, lf, 0.0, ALU.mult, ALU.add).then_inc(*c.up("gate_step"))
                        dve.wait_ge(*c.now("gate_step"))
                        bm = rows[0:4, :]
                        v.tensor_tensor(bm, b, m, ALU.subtract).then_inc(*c.up("gate_step"))
                        v.tensor_tensor(rows2[0:4, :], ig, b, ALU.subtract).then_inc(*c.up("gate_step"))
                        v.memset(m_state[0:4, 0:1], 0.0).then_inc(*c.up("gate_step"))
                        v.tensor_copy(m_state[0:4, 1:8],
                                      m.rearrange("p (c n) -> p c n", n=P)[:, 0:7, P - 1]).then_inc(*c.up("gate_step"))
                        dve.wait_ge(*c.now("gate_step"))
                        by_chunk = bm.rearrange("p (c n) -> p c n", n=P)
                        v.tensor_tensor(y[0:4, 1, :].rearrange("p (c n) -> p c n", n=P), by_chunk,
                                        m_state[0:4, 0:8].unsqueeze(2).to_broadcast([4, CH, P]), ALU.add).then_inc(
                            *c.up("gate_step"))
                        v.tensor_tensor(y[0:4, 2, :].rearrange("p (c n) -> p c n", n=P),
                                        rows2[0:4, :].rearrange("p (c n) -> p c n", n=P),
                                        by_chunk[:, :, P - 1:P].to_broadcast([4, CH, P]), ALU.add).then_inc(
                            *c.up("gate_step"))
                        assert c.n["gate_step"] == GATE_ROWS_DONE
                        for n, (dst, r) in enumerate(((col_a, 64), (col_g, 0), (col_m, 32))):
                            for q in range(2):
                                bank = 4 + q if n == 0 else 6 + q
                                if n == 0:
                                    dve.wait_ge(*c.next("gate_t"))
                                elif n == 1:
                                    dve.wait_ge(*c.next("gate_t"))
                                v.tensor_copy(dst[:, 4 * q:4 * q + 4, :],
                                              psum[:, bank, :].rearrange("p (c n) -> p c n", n=P)[:, :, r:r + 4]
                                              ).then_inc(*c.up("gate_step"))
                        assert c.n["gate_step"] == GATE_COLUMNS_DONE

                    def core(self, part, h, nxt):
                        c, v = self.c, nc.vector
                        s = 4 * h
                        if h == 0:
                            v.memset(state, 0.0).then_inc(*c.up("c_upd0"))
                            dve.wait_ge(*c.now("c_upd0"))
                        for k in range(10):
                            if 1 <= k <= 8:
                                u = k - 1
                                ch, j = 4 * h + u // 2, u % 2
                                head = 2 * part + j
                                dve.wait_ge(*c.next("core_num"))
                                d_ps = psum[:, s + 1, VH:VH + 1]
                                v.tensor_scalar(den, d_ps, -1.0, None, ALU.mult).then_inc(*c.up("core_den"))
                                dve.wait_ge(*c.now("core_den"))
                                v.scalar_tensor_tensor(den, d_ps, col_m[:, ch, head:head + 1], den, ALU.max,
                                                       ALU.max).then_inc(*c.up("core_den"))
                                dve.wait_ge(*c.now("core_den"))
                                v.reciprocal(rden, den).then_inc(*c.up("core_r"))
                                dve.wait_ge(*c.next("core_u"))
                                v.scalar_tensor_tensor(state[:, j, :], state[:, j, :], dec, psum[:, s + 2, 0:VH + 1],
                                                       ALU.mult, ALU.add).then_inc(*c.up("c_upd"))
                            if k <= 7:
                                ch, j = 4 * h + k // 2, k % 2
                                head = 2 * part + j
                                dve.wait_ge(*c.next("core_a"))
                                dve.wait_ge(*c.now("core_sw"))
                                v.scalar_tensor_tensor(dmat, psum[:, s, 2 * P:3 * P], col_g[:, ch, head:head + 1],
                                                       mask[:, :], ALU.add, ALU.min).then_inc(*c.up("core_d"))
                                v.tensor_tensor(qw, psum[:, s, 3 * P:4 * P], big[:, j, ch * P:(ch + 1) * P], ALU.mult)
                                v.tensor_scalar(kw, psum[:, s, 0:P], col_a[:, ch, head:head + 1], None, ALU.mult)
                                if k > 0:
                                    dve.wait_ge(*c.now("c_upd"))
                                v.tensor_copy(dec, psum[:, s, 4 * P - 1:4 * P])
                                dve.wait_ge(*c.next("core_e"))
                                v.tensor_tensor(sw, psum[:, s, P:2 * P], dmat, ALU.mult).then_inc(*c.up("core_sw"))
                            if 1 <= k <= 8:
                                dve.wait_ge(*c.next("core_rstd"))
                                dve.wait_ge(*c.now("core_ht"))
                                v.tensor_scalar(hn2, hn, hrstd, None, ALU.mult).then_inc(*c.up("core_h2"))
                                c.skip("core_ht")
                            if nxt and 1 <= k <= 8:
                                self.split(nxt, k - 1)
                        c.skip("core_h", 16)

                    def store(self, h):
                        for e in range(8 * h, 8 * h + 8):
                            tb = e // 2
                            if tb >= 3 and e % 2 == 0:
                                dve.wait_ge(out_done[tb % 3], 16 * (tb // 3))
                            dve.wait_ge(*self.c.next("out_t"))
                            nc.vector.tensor_copy(out_rows[:, tb % 3, (e % 2) * HALF:(e % 2 + 1) * HALF],
                                                  psum[:, e % 4, :]).then_inc(*self.c.up("out_c"))

                stages(Vector(dve, nc.vector))

            @block.gpsimd
            def _(pool):
                class Pool(Common):
                    def start(self):
                        nc.gpsimd.memset(ones[:, :], ONES).then_inc(*self.c.up("const"))
                        nc.gpsimd.memset(minus_half, -0.5).then_inc(*self.c.up("pow_in"))
                        nc.gpsimd.memset(ident[:, :], 0.0).then_inc(*self.c.up("const"))
                        nc.gpsimd.memset(mask[:, :], 0.0).then_inc(*self.c.up("const"))
                        pool.wait_ge(*self.c.now("const"))
                        nc.gpsimd.affine_select(out=ident[:, :], in_=ident[:, :], compare_op=ALU.not_equal, fill=1.0,
                                                base=0, pattern=[[-1, P]], channel_multiplier=1).then_inc(
                            *self.c.up("const"))
                        nc.gpsimd.affine_select(out=mask[:, :], in_=mask[:, :], compare_op=ALU.is_ge, fill=-3.0e38,
                                                base=0, pattern=[[1, P]], channel_multiplier=-1).then_inc(
                            *self.c.up("const"))
                        pool.wait_ge(*self.c.next("xin_ss", CH))
                        self.factors(c2_pre, ss_in, D * EPS * ONES, "norm_c2")

                    def factors(self, dst, sums, eps, name):
                        n = sums.shape[1]
                        nc.gpsimd.tensor_scalar(pow_in[:, 0:n], sums, eps, None, ALU.add).then_inc(*self.c.up("pow_in"))
                        pool.wait_ge(*self.c.now("pow_in"))
                        nc.gpsimd.tensor_tensor(dst, pow_in[:, 0:n], minus_half[:, 0:n], ALU.pow).then_inc(
                            *self.c.up(name))

                    def norm(self, dst, factors):
                        pool.wait_ge(*self.c.next("norm_c1"))
                        self.factors(factors, c1, D * EPS * ONES, "norm_c2")

                    def empty(self, key, h):
                        n = {"up": 2, "b": 4, "o": 4}.get(key[1], 0)
                        for t in range(n):
                            zt = 2 * key[3] + t if key[1] == "up" else t
                            self.eng.wait_ge(*self.c.next("z_hi"))
                            self.nc.tensor_tensor(z_lo[:, zt, half(h)], us[:, t % 2, :],
                                                  z_hi[:, zt, half(h)].bitcast(FP32), ALU.subtract).then_inc(
                                *self.c.up("z_ready"))

                    def renew(self, layer, which, h, blocks, final=False):
                        c = self.c
                        for k in range(DT + 1):
                            if k < DT:
                                pool.wait_ge(*c.now("x_new" if final else "x_ready"))
                                nc.gpsimd.tensor_tensor(x_old[:, k % 2, :], x_hi[:, k, half(h)].bitcast(FP32),
                                                        x_lo[:, k, half(h)].bitcast(FP32), ALU.add).then_inc(
                                    *c.up("x_old"))
                            if k > 0:
                                if final:
                                    c.skip("x_new")
                                else:
                                    pool.wait_ge(*c.next("x_hi"))
                                    nc.gpsimd.tensor_tensor(x_lo[:, k - 1, half(h)], xn[:, (k - 1) % 2, :],
                                                            x_hi[:, k - 1, half(h)].bitcast(FP32),
                                                            ALU.subtract).then_inc(*c.up("x_ready"))
                                    c.skip("x_new")

                    def core(self, part, h, nxt):
                        for _ in range(8):
                            pool.wait_ge(*self.c.next("core_ss"))
                            self.factors(hrstd, hss, VH * EPS, "core_rstd")

                stages(Pool(pool, nc.gpsimd))


_INS = ["x", "p", "norm_mix_pre", "norm_mix_post", "norm_ffn_pre", "norm_ffn_post", "sc_w_in", "sc_w_conv", "sc_w_out",
        "ml_w_in", "ml_gate_bias", "ml_head_norm", "ml_w_out", "ffn_w_up", "ffn_w_conv", "ffn_w_down",
        "ple_norm_gate", "ple_w_gate", "ple_w_proj", "ple_norm_out"]


def kernel(**inputs):
    import numpy as np
    import concourse.bacc as bacc
    from concourse.bass_utils import run_bass_kernel_spmd

    nc = bacc.Bacc("TRN2", target_bir_lowering=False, num_devices=1, dynamic_dma_scratch_size=1024)
    arrays, args = {}, []
    for name in _INS:
        a = np.ascontiguousarray(inputs[name])
        arrays[f"in_{name}"] = a
        args.append(nc.dram_tensor(f"in_{name}", a.shape, mybir.dt.from_np(a.dtype), kind="ExternalInput").ap())
    out = nc.dram_tensor("out", (1, SEQ, D), FP32, kind="ExternalOutput").ap()
    decoder_kernel(nc, *args, out)
    return run_bass_kernel_spmd(nc, [arrays], core_ids=[0]).results[0]["out"]
```

```python
import concourse.bass as bass
from concourse import mybir
from contextlib import ExitStack

FP32 = mybir.dt.float32
FP32R = mybir.dt.float32r
ALU = mybir.AluOpType
ACT = mybir.ActivationFunctionType

P = 128
D = 1024
SEQ = 1024
DEPTH = 2
PD = 256
MLSTM_GATES = 3072
HEADS = 4
QKH = 128
VH = 256
FF = 2816
EPS = 1e-6
HALF = SEQ // 2
BLOCKW = 512
DT = D // P
SLOTS = 8
RAWS = 4
CH = SEQ // P
ONES = 1024.0
SMALL = (FF // P) % 4
PARTS = 1 + FF // P // 4
LOOP0 = 2
LOOPED = PARTS - 1 - LOOP0
PER_PART = {"w_hi": 24, "w_lo": 24, "block_used": 14, "acc": 32, "bank_free": 32, "halo": 8, "tap": 24, "gelu": 8,
            "act_prod": 8, "z_hi": 8, "z_ready": 8}


class Plan:

    def __init__(self):
        self.groups = []
        self.keys = []
        self.block0 = []
        self.at = {}
        self.used0 = []
        self.z0 = []
        self.blocks = self.used = self.z = 0

    def add(self, key, k):
        self.at[key] = len(self.groups)
        self.keys.append(key)
        self.groups.append(k)
        self.block0.append(self.blocks)
        self.used0.append(self.used)
        self.z0.append(self.z)
        self.blocks += k
        self.used += k - 1 if k == SLOTS else 0
        self.z += 2 * {"b": 4, "o": 4, "up": 2}.get(key[1], 0)


    def fill(self, key, h):
        n = self.at[key]
        return 2 * (n - key[3]) + 2 * h + key[3] if key[1] in ("mix", "down") else 2 * n + h


def part_tiles(part):
    return SMALL if part == 1 else 4


def part_start(part):
    return sum(part_tiles(q) for q in range(part))


def make_plan():
    plan = Plan()
    for layer in range(DEPTH):
        for part in range(2):
            for kind in ("c", "u", "b") if layer == 0 else ("qk", "v", "o"):
                plan.add((layer, kind, part), DT)
            for g in range(2):
                plan.add((layer, "mix", part, g), 4)
        for part in range(PARTS):
            tiles = part_tiles(part)
            for g in range(tiles // 2):
                plan.add((layer, "up", part, g), DT)
            for g in range(2):
                plan.add((layer, "down", part, g), tiles)
        for kind, g in ("gate", 0), ("proj", 0), ("proj", 1), ("gate", 1):
            plan.add((layer, kind, g), DT if kind == "gate" else PD // P)
    return plan


class Counts:

    def __init__(self, sems):
        self.sems = sems
        self.n = {}
        self.per = None
        self.i = None

    def value(self, name, back=0):
        n = self.n.get(name, 0) - back
        if self.per is None or not self.per.get(name, 0):
            return max(n, 0)
        return self.i * self.per[name] + n

    def up(self, name):
        self.n[name] = self.n.get(name, 0) + 1
        return self.sems[name], 1

    def next(self, name, k=1):
        self.n[name] = self.n.get(name, 0) + k
        return self.sems[name], self.value(name)

    def now(self, name, back=0):
        return self.sems[name], self.value(name, back)

    def skip(self, name, k=1):
        self.n[name] = self.n.get(name, 0) + k

    def enter(self, i):
        self.per, self.i = PER_PART, i

    def leave(self, trips):
        self.n = {k: v + (trips - 1) * self.per.get(k, 0) for k, v in self.n.items()}
        self.per = self.i = None


NORM_BANKS = [6, 7] + 2 * [7, 6, 7, 3] + [3, 6, 7, 3] + 2 * [7, 6, 7, 3] + [3, 7]
GATE_ABS, GATE_ROWS_DONE, GATE_COLUMNS_DONE, GATE_EXPS = 13, 22, 28, 5


SEMS = ("pow_in w_hi w_lo block_used acc bank_free sq_tmp sq_sum norm_col norm_c1 norm_c2 norm_diag norm_row rs "
        "x_old x_t x_new x_hi x_ready halo tap cu gelu act_prod z_hi z_ready p_t p_hi p_lo sig gated "
        "const const_t const_c xin_t xin_ss xin_hi xin_ready "
        "gate_w gate_acc gate_ev gate_step gate_e gate_t "
        "core_a core_d core_e core_sw core_num core_u core_r core_den c_upd0 c_upd core_hn core_ss core_rstd "
        "core_h2 core_ht core_h out_t out_c").split()


def decoder_kernel(nc, x, p, norm_mix_pre, norm_mix_post, norm_ffn_pre, norm_ffn_post, sc_w_in, sc_w_conv,
                   sc_w_out, ml_w_in, ml_gate_bias, ml_head_norm, ml_w_out, ffn_w_up, ffn_w_conv, ffn_w_down,
                   ple_norm_gate, ple_w_gate, ple_w_proj, ple_norm_out, out):
    plan = make_plan()
    ctx = ExitStack()
    with ctx:
        def sb(name, shape, dt=FP32):
            return ctx.enter_context(nc.sbuf_tensor(name, shape, dt))

        S = {name: ctx.enter_context(nc.semaphore(name)) for name in SEMS}
        raw_in = [ctx.enter_context(nc.semaphore(f"raw_in{i}")) for i in range(RAWS)]
        x_in = [ctx.enter_context(nc.semaphore(f"x_in{i}")) for i in range(CH)]
        const_in = ctx.enter_context(nc.semaphore("const_in"))
        gate_w_in = ctx.enter_context(nc.semaphore("gate_w_in"))
        p_in = ctx.enter_context(nc.semaphore("p_in"))
        out_done = [ctx.enter_context(nc.semaphore(f"out_done{i}")) for i in range(3)]

        raw = sb("raw", [P, RAWS, BLOCKW])
        w_hi = sb("w_hi", [P, SLOTS, BLOCKW], FP32R)
        w_lo = sb("w_lo", [P, SLOTS, BLOCKW], FP32R)
        x_hi = sb("x_hi", [P, DT, SEQ], FP32R)
        x_lo = sb("x_lo", [P, DT, SEQ], FP32R)
        z_hi = sb("z_hi", [P, 4, SEQ], FP32R)
        z_lo = sb("z_lo", [P, 4, SEQ], FP32R)
        y = sb("y", [P, DT, SEQ])
        rs = sb("rs", [P, SEQ])
        ident = sb("ident", [P, P])
        ones = sb("ones", [P, P])
        gains = sb("gains", [P, 260])
        small = sb("small", [P, 312])
        mask = sb("mask", [P, P])
        big = sb("big", [P, 4, SEQ])
        area = sb("area", [P, 8 * 2 * (VH + 1)])
        us = sb("us", [P, 2, HALF])
        core = sb("core", [P, 2562])
        psum = ctx.enter_context(nc.psum_tensor("psum", [P, 8, BLOCKW], FP32))

        rs_post = (area[:, 0:512], us[:, 0, :])
        sq = area[:, 512:1536].rearrange("p (h n) -> p h n", h=2)
        x_old = area[:, 1536:2560].rearrange("p (b n) -> p b n", b=2)
        xn = area[:, 2560:3584].rearrange("p (b n) -> p b n", b=2)
        sqt = (area[:, 3584:4096], core[:, 1538:2050], core[:, 2050:2562])
        v_sb = area[:, :].rearrange("p (c j e) -> p c j e", c=CH, j=2)
        diag = core[:, 0:512]
        conv_in = core[:, 512:1540].rearrange("p (b n) -> p b n", b=2)
        halo_keep = core[:, 1540:1548].rearrange("p (t n) -> p t n", t=4)
        v_tmp = big[:, 0, :].rearrange("p (b n) -> p b n", b=2)
        p_rows = big[:, 1:3, :].rearrange("p a n -> p (a n)").rearrange("p (c f) -> p c f", c=CH)
        conv_out = big
        out_rows = big[:, 1:4, :]
        sqt_core = us[:, 0, 0:VH]
        rows = core[:, 0:1024]
        state = core[:, 1024:1538].rearrange("p (j e) -> p j e", j=2)
        dmat = core[:, 1538:1666]
        sw = core[:, 1666:1794]
        qw = core[:, 1794:1922]
        kw = core[:, 1922:2050]
        hn = core[:, 2050:2306]
        hn2 = core[:, 2306:2562]
        rows2 = y[:, 6, :]
        pow_in = small[:, 288:296]
        minus_half = small[:, 296:304]
        gate_raw = small[:, 160:224].rearrange("p (k c) -> p k c", k=DT)
        gate_g = small[:, 224:288].rearrange("p (k c) -> p k c", k=DT)
        zf_hi = z_hi[:, :, :].rearrange("p a n -> p (a n)")[:, 0:DT * 68].rearrange("p (k c) -> p k c", k=DT)
        zf_lo = z_lo[:, :, :].rearrange("p a n -> p (a n)")[:, 0:DT * 68].rearrange("p (k c) -> p k c", k=DT)

        c1 = small[:, 304:312].rearrange("p (b j) -> p b j", b=2)
        c2 = small[:, 4:8]
        c2_pre = small[:, 8:16]
        ss_in = small[:, 16:24]
        dec = small[:, 24:25]
        den = small[:, 25:26]
        ss_raw = small[:, 144:152]
        rden = small[:, 26:27]
        hss = small[:, 27:28]
        hrstd = small[:, 28:29]
        bias_i = small[:, 29:30]
        bias_f = small[:, 30:31]
        head_gain = small[:, 32:40]
        m_state = small[:, 40:48]
        col_g = small[:, 48:80].rearrange("p (c h) -> p c h", c=CH)
        col_a = small[:, 80:112].rearrange("p (c h) -> p c h", c=CH)
        col_m = small[:, 112:144].rearrange("p (c h) -> p c h", c=CH)

        NORMS = [norm_mix_pre, norm_mix_post, norm_ffn_pre, norm_ffn_post, ple_norm_gate, ple_norm_out]
        SC_COL, HN_COL, FF_COL = 96, 120, 128

        def norm_col(which, layer, t=0):
            return (which * DEPTH + layer) * DT + t

        def sc_col(tap, t):
            return SC_COL + tap * DT + t

        def ff_col(layer, tap, t):
            return FF_COL + (layer * 3 + tap) * (FF // P) + t

        def half(h):
            return slice(h * HALF, (h + 1) * HALF)

        def block_source(key, k, i=0):
            layer, kind = key[0], key[1]
            r = slice(k * P, (k + 1) * P)
            if kind in ("c", "u", "b"):
                c0 = {"b": 0, "c": D, "u": 2 * D}[kind] + key[2] * BLOCKW
                return sc_w_in[0, r, c0:c0 + BLOCKW]
            if kind == "qk":
                two = ml_w_in[0, r, 0:2 * HEADS * QKH].rearrange("r (s c) -> r s c", s=2)
                return two[:, :, key[2] * 256:key[2] * 256 + 256]
            if kind in ("v", "o"):
                c0 = 2 * HEADS * QKH + (HEADS * VH if kind == "o" else 0) + key[2] * BLOCKW
                return ml_w_in[0, r, c0:c0 + BLOCKW]
            if kind == "mix":
                w = (sc_w_out, ml_w_out)[layer]
                return w[0, key[2] * 512 + k * P:key[2] * 512 + (k + 1) * P, key[3] * BLOCKW:(key[3] + 1) * BLOCKW]
            if kind == "up":
                part, g = key[2], key[3]
                c0 = part_start(part) * P + g * 256
                two = ffn_w_up[layer, r, :].rearrange("r (s c) -> r s c", s=2)
                return two[:, :, bass.ds(i * 512 + c0, 256)] if not isinstance(i, int) else two[:, :, c0:c0 + 256]
            if kind == "down":
                part, g = key[2], key[3]
                r0 = (part_start(part) + k) * P
                c = slice(g * BLOCKW, (g + 1) * BLOCKW)
                return ffn_w_down[layer, bass.ds(i * 512 + r0, P), c] if not isinstance(i, int) else ffn_w_down[layer, r0:r0 + P, c]
            if kind == "proj":
                return ple_w_proj[layer, r, key[2] * BLOCKW:(key[2] + 1) * BLOCKW]
            return ple_w_gate[layer, r, key[2] * BLOCKW:(key[2] + 1) * BLOCKW]

        def gain_of(key, k):
            which = {"c": 0, "u": 0, "b": 0, "qk": 0, "v": 0, "o": 0, "up": 2, "gate": 4}.get(key[1])
            return None if which is None else norm_col(which, key[0], k)

        def body_keys(layer, part):
            return [(layer, kind, part, g) for kind in ("up", "down") for g in range(2)
                    if (layer, kind, part, g) in plan.at]

        def stages(e):
            e.start()
            for layer in range(DEPTH):
                kinds = ("c", "u", "b") if layer == 0 else ("qk", "v", "o")
                for part in range(2):
                    mix0, mix1 = (layer, "mix", part, 0), (layer, "mix", part, 1)
                    a, b, o = [(layer, kind, part) for kind in kinds]
                    if layer == 1 and part == 0:
                        e.empty(a, 1)
                        e.gates()
                    else:
                        e.empty(a, 0)
                        e.splits(b)
                        e.empty(a, 1)
                    e.empty(b, 0)
                    if layer == 0:
                        e.splits(o)
                        e.empty(b, 1)
                    else:
                        e.core(part, 0, o)
                        e.empty(b, 1)
                        e.core(part, 1, None)
                    e.empty(o, 0)
                    e.splits(mix0)
                    e.splits(mix1)
                    e.empty(o, 1)
                    if part == 0:
                        e.empty(mix0, 0)
                        e.empty(mix1, 0)
                        e.empty(mix0, 1)
                        e.splits((layer, kinds[0], 1))
                        e.empty(mix1, 1)
                up0, up1 = (layer, "up", 0, 0), (layer, "up", 0, 1)
                boundary(e, layer, mix1, up0, up1, 1)
                e.empty(up0, 1)
                feed_part(e, layer, 0)
                feed_part(e, layer, 1)
                e.loop(LOOPED, lambda: feed_part(e, layer, LOOP0))
                feed_part(e, layer, PARTS - 1)
                gate0, proj0, proj1, gate1 = [(layer, kind, g) for kind, g in
                                              (("gate", 0), ("proj", 0), ("proj", 1), ("gate", 1))]
                boundary(e, layer, (layer, "down", PARTS - 1, 1), gate0, proj0, 3)
                e.empty(gate0, 1)
                e.empty(proj0, 0)
                e.splits(proj1)
                e.empty(proj0, 1)
                e.empty(proj1, 0)
                e.splits(gate1)
                e.empty(proj1, 1)
                if layer + 1 < DEPTH:
                    boundary(e, layer, gate1, (1, "qk", 0), (1, "v", 0), 5)
            e.empty(gate1, 0)
            e.sums_read(c2)
            e.diagonal(c2)
            e.factors_read(rs_post[0])
            e.renew(1, 5, 0)
            e.store(0)
            e.empty(gate1, 1)
            e.sums_read(c2)
            e.diagonal(c2)
            e.factors_read(rs_post[1])
            e.renew(1, 5, 1)
            e.store(1)

        def feed_part(e, layer, part):
            ups, (down0, down1) = body_keys(layer, part)[:-2], body_keys(layer, part)[-2:]
            for up, nxt in zip(ups, ups[1:] + [down0]):
                if up != (layer, "up", 0, 0):
                    e.empty(up, 0)
                    e.splits(nxt)
                    if nxt == down0:
                        e.splits(down1)
                    e.empty(up, 1)
            if part < PARTS - 1:
                e.empty(down0, 0)
                e.empty(down1, 0)
                e.empty(down0, 1)
                e.splits((layer, "up", part + 1, 0))
                e.empty(down1, 1)

        def boundary(e, layer, done, key0, key1, post):
            pair = done[1] != "gate"
            proj = key0[1] == "gate"
            work, blocks = {k: [] for k in range(DT)}, {}
            if pair:
                e.empty(done[:3] + (0,), 0)
            e.empty(done, 0)
            e.sums_read(c2)
            e.diagonal(c2)
            if pair:
                first, second = e.empty_steps(done[:3] + (0,), 1), e.empty_steps(done, 1)
                work[0] += first[:1]
                work[1] += first[1:2]
                work[2] += first[2:]
                work[4] += second[:2]
                work[5] += second[2:]
                blocks |= {1: [0], 2: [1], 3: [2, 3], 4: [4], 5: [5], 6: [6], 7: [7]}
                work[6].append(lambda: e.sums_read(c2))
                if proj:
                    work[5].append(lambda: e.p_split(0))
                    work[6].append(lambda: e.p_split(1))
                work[7].append(lambda: e.diagonal(c2))
            else:
                e.split(key0, 0)
                e.split(key0, 1)
                blocks |= {k: [k + 2] for k in range(DT - 2)}
                for n, step in enumerate(e.empty_steps(done, 1)):
                    work[3 + n].append(step)
            e.factors_read(rs_post[0])
            e.renew(layer, post, 0, work, key0, blocks)
            if not pair:
                e.sums_read(c2)
                e.diagonal(c2)
            e.factors_read(rs_post[1])
            work = {k: [] for k in range(DT)}
            work[0].append(lambda: e.sums_read(c2_pre[:, 0:4]))
            work[1].append(lambda: e.diagonal(c2_pre[:, 0:4]))
            work[2].append(lambda: e.factors_read(rs[:, half(0)]))
            e.renew(layer, post, 1, work, key1, {6: [0], 7: [1]})

            def pre1():
                for k in range(2, plan.groups[plan.at[key1]]):
                    e.split(key1, k)
                e.sums_read(c2_pre[:, 4:8])
                e.diagonal(c2_pre[:, 4:8])
                e.factors_read(rs[:, half(1)])
            e.empty(key0, 0, pre1)

        def last_branch(key):
            return (key[1:] in (("gate", 1), ("proj", 0)) or (key[1] == "mix" and key[2] == 1)
                    or (key[1] == "down" and key[2] == PARTS - 1))

        class Common:

            def __init__(self, engine, compute):
                self.eng, self.nc = engine, compute
                self.c = Counts(S)
                self.i = 0

            def splits(self, key):
                for k in range(plan.groups[plan.at[key]]):
                    self.split(key, k)

            def loop(self, trips, body):
                with self.eng.Fori(0, trips) as i:
                    self.i = i
                    self.c.enter(i)
                    body()
                self.i = 0
                self.c.leave(trips)

            def split(self, key, k):
                pass

            def sums_read(self, factors):
                pass

            def diagonal(self, factors):
                pass

            def factors_read(self, dst):
                pass

            def empty_steps(self, key, h):
                return []

            def p_split(self, h):
                pass

            def gates(self):
                pass

            def store(self, h):
                pass

        with nc.Block() as block:

            @block.sync
            def _(sp):
                def load(key, k, i=0):
                    b = plan.block0[plan.at[key]] + k
                    if b >= RAWS:
                        sp.wait_ge(S["w_lo"], i * PER_PART["w_lo"] + b - RAWS + 1)
                    src = block_source(key, k, i)
                    dst = raw[:, b % RAWS, :]
                    if len(src.shape) == 3:
                        dst = dst.rearrange("p (s c) -> p s c", s=2)
                    sp.dma_start(dst, src).then_inc(raw_in[b % RAWS], 16)

                def group(key, i=0):
                    for k in range(plan.groups[plan.at[key]]):
                        load(key, k, i)

                for tb in range(CH):
                    sp.dma_start(y[:, tb, :], x[0, tb * P:(tb + 1) * P, :]).then_inc(x_in[tb], 16)
                    if tb == 0:
                        for w, v in enumerate(NORMS):
                            sp.dma_start(us[w * 16:w * 16 + 16, 0, 0:P],
                                         v.rearrange("l (t q) -> (l t) q", q=P)).then_inc(const_in, 16)
                        sp.dma_start(us[96:120, 0, 0:P],
                                     sc_w_conv.rearrange("l j (t q) -> (l j t) q", q=P)).then_inc(const_in, 16)
                        sp.dma_start(us[120:128, 0, 0:P],
                                     ml_head_norm.rearrange("l (t q) -> (l t) q", q=P)).then_inc(const_in, 16)
                        for layer in range(DEPTH):
                            sp.dma_start(us[0:66, 0, P * (1 + layer):P * (2 + layer)],
                                         ffn_w_conv[layer].rearrange("j (t q) -> (j t) q", q=P)).then_inc(const_in, 16)
                        bias = ml_gate_bias.rearrange("l g -> g l")
                        with nc.allow_non_contiguous_dma(reason="eight biases and eight columns of gate weights"):
                            sp.dma_start(bias_i[0:4, :], bias[0:4, :]).then_inc(const_in, 16)
                            sp.dma_start(bias_f[64:68, :], bias[4:8, :]).then_inc(const_in, 16)
                            sp.dma_start(gate_raw, ml_w_in[0, :, MLSTM_GATES:MLSTM_GATES + 2 * HEADS].rearrange(
                                "(k q) c -> q k c", q=P)).then_inc(const_in, 16)
                    if tb == 3:
                        for k in range(RAWS):
                            load((0, "c", 0), k)
                for k in range(RAWS, DT):
                    load((0, "c", 0), k)
                for layer in range(DEPTH):
                    kinds = ("c", "u", "b") if layer == 0 else ("qk", "v", "o")
                    for part in range(2):
                        for kind in kinds:
                            if (layer, kind, part) != (0, "c", 0):
                                group((layer, kind, part))
                        for g in range(2):
                            group((layer, "mix", part, g))
                    for key in body_keys(layer, 0):
                        group(key)
                    sp.wait_ge(S["bank_free"], 8 * plan.at[(layer, "up", 0, 0)] + 1)
                    sp.dma_start(p_rows, p[layer, 0].rearrange("(c q) f -> q c f", q=P)).then_inc(p_in, 16)
                    for key in body_keys(layer, 1):
                        group(key)
                    with sp.Fori(0, LOOPED) as i:
                        for key in body_keys(layer, LOOP0):
                            group(key, i)
                    for key in body_keys(layer, PARTS - 1):
                        group(key)
                    for key in (layer, "gate", 0), (layer, "proj", 0), (layer, "proj", 1), (layer, "gate", 1):
                        group(key)
                for tb in range(CH):
                    sp.wait_ge(S["out_c"], 2 * tb + 2)
                    sp.dma_start(out[0, tb * P:(tb + 1) * P, :], out_rows[:, tb % 3, :]).then_inc(out_done[tb % 3], 16)
                for s in range(3):
                    sp.wait_ge(out_done[s], 16 * len(range(s, CH, 3)))

            @block.tensor
            def _(pe):
                c = Counts(S)

                def bank_free(key, h, t):
                    pe.wait_ge(S["bank_free"], 4 * plan.fill(key, h) + t + 1)

                def gemm(key, h, i=0, ready=None, extra=None, order=None, hold=None):
                    n, fill = plan.at[key], plan.fill(key, h)
                    b0, K = plan.block0[n], plan.groups[n]
                    src_hi, src_lo = (z_hi, z_lo) if key[1] in ("mix", "down", "proj") else (x_hi, x_lo)
                    seen = -1
                    for item in order or [(k, t) for k in range(K) for t in range(4)]:
                        if callable(item):
                            item()
                            continue
                        k, t = item
                        if k > seen:
                            seen = k
                            if extra:
                                extra(k)
                            if h == 0:
                                pe.wait_ge(S["w_lo"], i * PER_PART["w_lo"] + b0 + k + 1)
                            if ready:
                                ready(k)
                        slot = (b0 + k) % SLOTS
                        if k == 0:
                            if fill >= 2:
                                pe.wait_ge(S["bank_free"], i * PER_PART["bank_free"] + 4 * (fill - 2) + t + 1)
                            if hold and t in hold:
                                hold[t]()
                        for step, (w, m) in enumerate(((w_hi, src_hi), (w_hi, src_lo), (w_lo, src_hi))):
                            if key[1] == "v":
                                left, right = m[:, k, h * HALF + t * P:h * HALF + (t + 1) * P], w[:, slot, :]
                            else:
                                left, right = w[:, slot, t * P:(t + 1) * P], m[:, k, half(h)]
                            ins = nc.tensor.matmul(psum[:, 4 * (fill % 2) + t, :], left, right,
                                                   start=(k == 0 and step == 0), stop=(k == K - 1 and step == 2))
                        if k == K - 1:
                            ins.then_inc(S["acc"], 1)
                        elif h == 1 and t == 3 and K == SLOTS:
                            ins.then_inc(S["block_used"], 1)

                def late(K, ts, between, after):
                    early = [t for t in range(4) if t not in ts]
                    first = min(K, 3)
                    order = [(k, t) for k in range(min(K, 2)) for t in early] + [between]
                    order += [(k, t) for k in range(2, first) for t in early] + [after]
                    order += [(k, t) for k in range(first) for t in ts]
                    return order + [(k, t) for k in range(first, K) for t in range(4)]

                def z_ready(key, h, i=0):
                    layer, kind, part, g = key
                    per = 4 if kind == "mix" else 2
                    maker = {("mix", 0): "b", ("mix", 1): "o"}.get((kind, layer))

                    def ready(k):
                        m = plan.at[(layer, maker, part) if maker else (layer, "up", part, k // 2)]
                        pe.wait_ge(S["z_ready"], i * PER_PART["z_ready"] + plan.z0[m] + h * per + k % per + 1)
                    return ready

                def group(key, i=0):
                    for h in range(2):
                        gemm(key, h, i)

                def pair(key, i=0):
                    for h in range(2):
                        gemm(key, h, i, z_ready(key, h, i))
                        gemm(key[:3] + (1,), h, i)

                def norm_sums(h, bank, adds):
                    pe.wait_ge(S["sq_sum"], adds)
                    for j in range(4):
                        ins = nc.tensor.matmul(psum[:, bank, j:j + 1], sq[:, h, j * P:(j + 1) * P], ones[:, 0:1],
                                               start=True, stop=True)
                    ins.then_inc(*c.up("norm_col"))

                def norm_spread(bank):
                    pe.wait_ge(*c.next("norm_diag"))
                    nc.tensor.matmul(psum[:, bank, :], ones[:, :], diag, start=True, stop=True).then_inc(
                        *c.up("norm_row"))

                def rs_read(k):
                    pe.wait_ge(S["rs"], k)

                def p_transpose(h):
                    for f in range(2):
                        for j in range(4):
                            ins = nc.tensor.transpose(psum[:, 4 + f, j * P:(j + 1) * P],
                                                      p_rows[:, 4 * h + j, f * P:(f + 1) * P], ident[:, :])
                        ins.then_inc(*c.up("p_t"))

                def turn(nth, done, key0, key1):
                    layer = done[0]
                    first = done[:3] + (0,) if done[1] != "gate" else None
                    proj = key0[1] == "gate"
                    adds, norms = 28 * nth, 2 + 4 * nth

                    def x_ready(h):
                        return lambda k: pe.wait_ge(S["x_ready"], 2 * DT * nth + DT * h + k + 1)

                    def p_read(count):
                        pe.wait_ge(S["p_lo"], 4 * layer + count)

                    def post0(k):
                        if k == (2 if first else 3):
                            bank_free(done, 0, 3)
                            norm_sums(0, 7 if first else 3, adds + (7 if first else 10))
                        if k == (3 if first else 4):
                            norm_spread(7 if first else 3)

                    def post1(k):
                        if first and proj and k == 5:
                            pe.wait_ge(p_in, 16 * (layer + 1))
                            bank_free(done, 1, 1)
                            p_transpose(0)
                        if first and k == 6:
                            bank_free(done, 1, 3)
                            norm_sums(1, 6, adds + 19)
                            if proj:
                                p_read(2)
                                p_transpose(1)
                        if first and k == 7:
                            norm_spread(6)

                    def post0_read():
                        rs_read(norms + 1)

                    if first:
                        gemm(first, 0, ready=z_ready(first, 0))
                        gemm(done, 0)
                        gemm(first, 1, ready=z_ready(first, 1), extra=post0)
                        gemm(done, 1, order=[(k, t) for k in range(4) for t in range(3)] + [(k, 3) for k in range(4)],
                             hold={3: post0_read})
                        gemm(key0, 0, ready=x_ready(0), extra=post1)
                    else:
                        gemm(done, 0)
                        gemm(done, 1, extra=post0)
                        gemm(key0, 0, ready=x_ready(0), hold={3: post0_read})
                        bank_free(done, 1, 3)
                        norm_sums(1, 6, adds + 21)
                    norm_sums(0, 7, adds + 21)
                    if not first:
                        norm_spread(6)
                    gemm(key0, 1, ready=x_ready(1), hold={0: lambda: p_read(3), 1: lambda: p_read(4)} if proj else None,
                         order=late(DT, (2, 3), lambda: norm_spread(7), lambda: rs_read(norms + 3)))
                    bank_free(key0, 0, 3)
                    norm_sums(1, 3, adds + 28)
                    if key0[1] != "qk":
                        gemm(key1, 0, order=late(plan.groups[plan.at[key1]], (3,), lambda: norm_spread(3),
                                                 lambda: rs_read(norms + 4)))
                        gemm(key1, 1)
                    else:
                        norm_spread(3)
                        rs_read(norms + 4)

                def gates_pe():
                    pe.wait_ge(*c.next("gate_w"))
                    for h in range(2):
                        for k in range(DT):
                            for step, (w, m) in enumerate(((zf_hi, x_hi), (zf_hi, x_lo), (zf_lo, x_hi))):
                                ins = nc.tensor.matmul(psum[0:68, h, :], w[:, k, :], m[:, k, half(h)],
                                                       start=(k == 0 and step == 0), stop=(k == DT - 1 and step == 2))
                        ins.then_inc(*c.up("gate_acc"))
                    pe.wait_ge(*c.next("gate_ev", 4))

                def gate_columns(k):
                    if k != DT - 2:
                        return
                    bank_free((1, "qk", 0), 1, 3)
                    pe.wait_ge(S["gate_step"], GATE_ROWS_DONE)
                    pe.wait_ge(S["gate_e"], GATE_EXPS)
                    for src, bank in ((rows, 4), (rows2, 6)):
                        for ch in range(CH):
                            ins = nc.tensor.transpose(psum[:, bank + ch // 4, (ch % 4) * P:(ch % 4 + 1) * P],
                                                      src[:, ch * P:(ch + 1) * P], ident[:, :])
                            if ch % 4 == 3:
                                ins.then_inc(*c.up("gate_t"))

                def core_step(part, h):
                    s = 4 * h

                    def step(k):
                        if k == 0:
                            bank_free((1, "v", part), h, 3)
                        if 1 <= k <= 8:
                            u = k - 1
                            ch, j = 4 * h + u // 2, u % 2
                            pe.wait_ge(*c.next("core_sw"))
                            pe.wait_ge(*c.now("core_hn"))
                            pe.wait_ge(*c.now("c_upd"))
                            c.skip("core_hn")
                            c.skip("c_upd")
                            nc.tensor.matmul(psum[:, s + 1, 0:VH + 1], sw, v_sb[:, ch, j, :], start=True, stop=False)
                            nc.tensor.matmul(psum[:, s + 1, 0:VH + 1], qw, state[:, j, :], start=False,
                                             stop=True).then_inc(*c.up("core_num"))
                            nc.tensor.matmul(psum[:, s + 2, 0:VH + 1], kw, v_sb[:, ch, j, :], start=True,
                                             stop=True).then_inc(*c.up("core_u"))
                        if k <= 7:
                            ch, j = 4 * h + k // 2, k % 2
                            cols = slice(ch * P, (ch + 1) * P)
                            head = 2 * part + j
                            nc.tensor.transpose(psum[:, s, 0:P], big[:, 2 + j, cols], ident[:, :])
                            nc.tensor.matmul(psum[:, s, P:2 * P], big[:, 2 + j, cols], big[:, j, cols],
                                             start=True, stop=True)
                            for place, row in ((2, head), (3, 32 + head)):
                                ins = nc.tensor.matmul(psum[:, s, place * P:(place + 1) * P],
                                                       ident[0:64, row:row + 1].to_broadcast([64, P]),
                                                       rows[0:64, cols], start=True, stop=True)
                            ins.then_inc(*c.up("core_a"))
                        if k >= 2:
                            pe.wait_ge(*c.next("core_h2"))
                            pe.wait_ge(*c.now("core_h"))
                            c.skip("core_h", 2)
                            for e in range(2):
                                ins = nc.tensor.transpose(psum[:, s + 3, e * P:(e + 1) * P],
                                                          hn2[:, e * P:(e + 1) * P], ident[:, :])
                            ins.then_inc(*c.up("core_ht"))
                        if k == 9:
                            pe.wait_ge(*c.now("core_h"))
                            pe.wait_ge(*c.now("c_upd"))
                    return step

                def feed(layer, part, i=0):
                    for key in body_keys(layer, part)[:-2]:
                        group(key, i)
                    pair((layer, "down", part, 0), i)

                pe.wait_ge(S["const"], 5)
                pe.wait_ge(const_in, 16 * 13)
                at = 0
                for j, r in enumerate((P, 66, 66)):
                    ins = nc.tensor.transpose(psum[:, 7, at:at + r], us[0:r, 0, j * P:(j + 1) * P], ident[0:r, 0:r])
                    at += r
                ins.then_inc(*c.up("const_t"))
                for e in range(2 * CH):
                    if e % 2 == 0:
                        pe.wait_ge(x_in[e // 2], 16)
                    if e >= 6:
                        pe.wait_ge(S["xin_ready"], e - 5)
                    for j in range(4):
                        f = 4 * (e % 2) + j
                        ins = nc.tensor.transpose(psum[:, e % 6, j * P:(j + 1) * P], y[:, e // 2, f * P:(f + 1) * P],
                                                  ident[:, :])
                    ins.then_inc(*c.up("xin_t"))
                pe.wait_ge(*c.next("const_c"))
                norm_spread(6)
                norm_spread(7)
                pe.wait_ge(S["xin_ready"], 2 * CH)
                rs_read(2)

                for part in range(2):
                    for kind in ("c", "u", "b"):
                        group((0, kind, part))
                    if part == 0:
                        pair((0, "mix", part, 0))
                for layer in range(DEPTH):
                    if layer == 1:
                        for part in range(2):
                            if part == 0:
                                gates_pe()
                            else:
                                group((1, "qk", 1))
                            gemm((1, "v", part), 0, extra=gate_columns if part == 0 else None)
                            if part == 0:
                                pe.wait_ge(S["gate_step"], GATE_COLUMNS_DONE)
                            for h, (kind, half_of) in enumerate((("v", 1), ("o", 0))):
                                step = core_step(part, h)
                                gemm((1, kind, part), half_of, extra=step)
                                step(8)
                                step(9)
                            gemm((1, "o", part), 1)
                            if part == 0:
                                pair((1, "mix", part, 0))
                    turn(3 * layer, (layer, "mix", 1, 1), (layer, "up", 0, 0), (layer, "up", 0, 1))
                    pair((layer, "down", 0, 0))
                    feed(layer, 1)
                    with pe.Fori(0, LOOPED) as i:
                        feed(layer, LOOP0, i)
                    for key in body_keys(layer, PARTS - 1)[:2]:
                        group(key)
                    turn(3 * layer + 1, (layer, "down", PARTS - 1, 1), (layer, "gate", 0), (layer, "proj", 0))
                    group((layer, "proj", 1))
                    if layer == 0:
                        turn(2, (0, "gate", 1), (1, "qk", 0), None)
                gemm((1, "gate", 1), 0)
                gemm((1, "gate", 1), 1)
                for h in range(2):
                    bank_free((1, "gate", 1), h, 3)
                    norm_sums(h, 3 + 4 * h, 28 * 5 + 10 + 4 * h)
                    norm_spread(3 + 4 * h)
                    rs_read(2 + 4 * 5 + 1 + h)
                    for e in range(8 * h, 8 * h + 8):
                        if e % 2 == 0:
                            pe.wait_ge(S["x_new"], 2 * DT * 5 + DT * (h + 1))
                        if e >= 4:
                            pe.wait_ge(S["out_c"], e - 3)
                        for j in range(4):
                            ins = nc.tensor.transpose(psum[:, e % 4, j * P:(j + 1) * P],
                                                      y[:, 4 * (e % 2) + j, (e // 2) * P:(e // 2 + 1) * P], ident[:, :])
                        ins.then_inc(*c.up("out_t"))

            @block.scalar
            def _(act):
                class Scalar(Common):
                    norms = 0

                    def banks(self, key, h, t):
                        self.eng.wait_ge(S["bank_free"], self.i * PER_PART["bank_free"] + 4 * plan.fill(key, h) + t + 1)

                    def start(self):
                        act.wait_ge(*self.c.next("const_c", 2))
                        for e in range(2 * CH):
                            tb, r = e // 2, e % 2
                            if r == 0:
                                act.wait_ge(x_in[tb], 16)
                                act.wait_ge(*self.c.now("xin_ss"))
                                nc.scalar.activation(big[:, 0, :], y[:, tb, :], ACT.Square, scale=32.0,
                                                     accum_out=ss_in[:, tb:tb + 1]).then_inc(*self.c.up("xin_ss"))
                            act.wait_ge(*self.c.next("xin_t"))
                            nc.scalar.activation(x_hi[:, 4 * r:4 * r + 4, tb * P:(tb + 1) * P],
                                                 psum[:, e % 6, :].rearrange("p (f n) -> p f n", f=4),
                                                 ACT.Copy).then_inc(*self.c.up("xin_hi"))
                            if e < 8:
                                self.split((0, "c", 0), e)
                        for h in range(2):
                            self.row(rs[:, half(h)])

                    def split(self, key, k):
                        n = plan.at[key]
                        b = plan.block0[n] + k
                        old = b - SLOTS
                        if old >= 0:
                            m = max(g for g in range(len(plan.groups)) if plan.block0[g] <= old)
                            kk = old - plan.block0[m]
                            if plan.groups[m] == SLOTS and kk < SLOTS - 1:
                                self.eng.wait_ge(S["block_used"], self.i * PER_PART["block_used"] + plan.used0[m] + kk + 1)
                            else:
                                self.eng.wait_ge(S["acc"], self.i * PER_PART["acc"] + 4 * plan.fill(plan.keys[m], 1) + 4)
                        self.eng.wait_ge(raw_in[b % RAWS], self.i * (16 * PER_PART["w_lo"] // RAWS) + 16 * (b // RAWS + 1))
                        g = gain_of(key, k)
                        self.nc.activation(w_hi[:, b % SLOTS, :], raw[:, b % RAWS, :], ACT.Copy,
                                           scale=1.0 if g is None else gains[:, g:g + 1]).then_inc(*self.c.up("w_hi"))

                    def row(self, dst):
                        bank = NORM_BANKS[self.norms]
                        self.norms += 1
                        act.wait_ge(*self.c.next("norm_row"))
                        nc.scalar.activation(dst, psum[:, bank, :], ACT.Copy).then_inc(*self.c.up("rs"))

                    def sums_read(self, factors):
                        n = self.c.n.get("norm_col", 0)
                        act.wait_ge(*self.c.next("norm_col"))
                        nc.scalar.activation(c1[:, n % 2, :], psum[:, NORM_BANKS[2 + n], 0:4], ACT.Copy).then_inc(
                            *self.c.up("norm_c1"))

                    def factors_read(self, dst):
                        self.row(dst)

                    def square(self, src, h, t):
                        dst = sq[:, h, :]
                        if t > 0:
                            n = self.c.n.get("sq_sum", 0)
                            dst = sqt[n % 3]
                            if n > 2:
                                self.eng.wait_ge(*self.c.now("sq_sum", 2))
                            self.c.skip("sq_sum")
                        self.nc.activation(dst, src, ACT.Square).then_inc(*self.c.up("sq_tmp"))

                    def z_part(self, zt, h, b):
                        self.eng.wait_ge(*self.c.next("act_prod"))
                        self.nc.activation(z_hi[:, zt, half(h)], us[:, b, :], ACT.Copy).then_inc(*self.c.up("z_hi"))

                    def empty_steps(self, key, h):
                        def branch(t):
                            self.banks(key, h, t)
                            self.square(y[:, 4 * key[3] + t, half(h)], h, 4 * key[3] + t)

                        def gated(t):
                            if t < 4:
                                self.banks(key, h, t)
                                nc.scalar.activation(v_tmp[:, t % 2, :], v_tmp[:, t % 2, :], ACT.Sigmoid).then_inc(
                                    *self.c.up("sig"))
                            if t > 0:
                                act.wait_ge(*self.c.next("gated"))
                                self.square(y[:, 3 + t, half(h)], h, 3 + t)
                        if key[1] == "gate":
                            return [lambda t=t: gated(t) for t in range(5)]
                        return [lambda t=t: branch(t) for t in range(4)]

                    def empty(self, key, h, between=None):
                        kind = key[1]
                        if between:
                            between()
                        if last_branch(key) and kind != "proj":
                            for step in self.empty_steps(key, h):
                                step()
                        elif kind == "proj" and key[2] == 0:
                            for t in range(4):
                                self.banks(key, h, t)
                                self.square(y[:, t, half(h)], h, t)
                        elif kind == "gate":
                            for t in range(4):
                                self.banks(key, h, t)
                                nc.scalar.activation(y[:, t, half(h)], y[:, t, half(h)], ACT.Sigmoid).then_inc(
                                    *self.c.up("sig"))
                        elif kind == "b":
                            for t in range(4):
                                self.z_part(t, h, t % 2)
                        elif kind == "o":
                            for t0 in (0, 2):
                                for t in (t0, t0 + 1):
                                    self.banks(key, h, t)
                                    self.nc.activation(us[:, t % 2, :], us[:, t % 2, :], ACT.Tanh, scale=0.5).then_inc(
                                        *self.c.up("sig"))
                                for t in (t0, t0 + 1):
                                    self.z_part(t, h, t % 2)
                        elif kind == "up":
                            self.c.skip("tap", 4)
                            for j in range(2):
                                self.eng.wait_ge(*self.c.next("tap"))
                                self.nc.activation(v_tmp[:, j, :], v_tmp[:, j, :], ACT.Gelu_apprx_tanh).then_inc(
                                    *self.c.up("gelu"))
                            for j in range(2):
                                self.z_part(2 * key[3] + j, h, j)

                    def renew(self, layer, which, h, work=None, key=None, blocks=None):
                        final = work is None
                        for k in range(DT):
                            if not final:
                                for b in blocks.get(k, ()):
                                    self.split(key, b)
                            self.eng.wait_ge(*self.c.next("x_new"))
                            if not final:
                                nc.scalar.activation(x_hi[:, k, half(h)], xn[:, k % 2, :], ACT.Copy).then_inc(
                                    *self.c.up("x_hi"))
                                self.square(xn[:, k % 2, :], h, k)
                                for other in work[k]:
                                    other()

                    def p_split(self, h):
                        for f in range(2):
                            act.wait_ge(*self.c.next("p_t"))
                            nc.scalar.activation(z_hi[:, f, half(h)], psum[:, 4 + f, :], ACT.Copy).then_inc(
                                *self.c.up("p_hi"))

                    def gates(self):
                        act.wait_ge(S["gate_step"], GATE_ABS)
                        a = y[0:4, 3, :]
                        nc.scalar.activation(a, a, ACT.Exp, scale=-1.0).then_inc(*self.c.up("gate_e"))
                        act.wait_ge(*self.c.now("gate_e"))
                        nc.scalar.activation(a, a, ACT.Ln, bias=1.0).then_inc(*self.c.up("gate_e"))
                        act.wait_ge(S["gate_step"], GATE_ROWS_DONE)
                        for dst, src, scale in ((rows[32:36, :], y[0:4, 1, :], 1.0), (rows[64:68, :], y[0:4, 2, :], 1.0),
                                                (rows2[32:36, :], y[0:4, 5, :], -1.0)):
                            nc.scalar.activation(dst, src, ACT.Exp, scale=scale).then_inc(*self.c.up("gate_e"))

                    def core(self, part, h, nxt):
                        for k in range(10):
                            if 1 <= k <= 8:
                                act.wait_ge(*self.c.next("core_r"))
                                act.wait_ge(*self.c.now("core_h2"))
                                nc.scalar.activation(hn, psum[:, 4 * h + 1, 0:VH], ACT.Copy, scale=rden).then_inc(
                                    *self.c.up("core_hn"))
                                act.wait_ge(*self.c.now("core_hn"))
                                nc.scalar.activation(sqt_core, hn, ACT.Square, accum_out=hss).then_inc(
                                    *self.c.up("core_ss"))
                                self.c.skip("core_h2")
                            if k <= 7:
                                act.wait_ge(*self.c.next("core_d"))
                                nc.scalar.activation(dmat, dmat, ACT.Exp).then_inc(*self.c.up("core_e"))
                            if k >= 2:
                                u = k - 2
                                ch, j = 4 * h + u // 2, u % 2
                                act.wait_ge(*self.c.next("core_ht"))
                                for e in range(2):
                                    hg = 2 * (2 * part + j) + e
                                    nc.scalar.activation(big[:, j + 2 * e, ch * P:(ch + 1) * P],
                                                         psum[:, 4 * h + 3, e * P:(e + 1) * P], ACT.Copy,
                                                         scale=head_gain[:, hg:hg + 1]).then_inc(*self.c.up("core_h"))
                            if nxt and 1 <= k <= 8:
                                self.split(nxt, k - 1)

                stages(Scalar(act, nc.scalar))

            @block.vector
            def _(dve):
                class Vector(Common):
                    squared = []

                    def acc(self, key, h, t):
                        self.eng.wait_ge(S["acc"], self.i * PER_PART["acc"] + 4 * plan.fill(key, h) + t + 1)
                        return psum[:, 4 * (plan.fill(key, h) % 2) + t, :]

                    def column(self, key, tap, t):
                        layer, _, part, g = key
                        c0 = ff_col(layer, tap, part_start(part) + 2 * g + t)
                        return gains[:, c0:c0 + 1] if isinstance(self.i, int) else gains[:, bass.ds(self.i * 4 + c0, 1)]

                    def start(self):
                        dve.wait_ge(*self.c.next("const_t"))
                        nc.vector.tensor_copy(gains[:, :], psum[:, 7, 0:260]).then_inc(*self.c.up("const_c"))
                        dve.wait_ge(*self.c.now("const_c"))
                        nc.vector.tensor_scalar(head_gain, gains[:, HN_COL:HN_COL + 8], 8.0, None, ALU.mult).then_inc(
                            *self.c.up("const_c"))
                        for e in range(2 * CH):
                            tb, r = e // 2, e % 2
                            cols = slice(tb * P, (tb + 1) * P)
                            dve.wait_ge(*self.c.next("xin_hi"))
                            nc.vector.tensor_tensor(x_lo[:, 4 * r:4 * r + 4, cols],
                                                    psum[:, e % 6, :].rearrange("p (f n) -> p f n", f=4),
                                                    x_hi[:, 4 * r:4 * r + 4, cols].bitcast(FP32),
                                                    ALU.subtract).then_inc(*self.c.up("xin_ready"))
                            if e < 8:
                                self.split((0, "c", 0), e)
                        for h in range(2):
                            if h == 0:
                                dve.wait_ge(*self.c.next("norm_c2"))
                            self.spread(c2_pre[:, 4 * h:4 * h + 4])
                            self.factors_read(None)

                    def spread(self, factors):
                        nc.vector.tensor_tensor(diag.rearrange("p (j n) -> p j n", j=4),
                                                ident[:, :].unsqueeze(1).to_broadcast([P, 4, P]),
                                                factors.unsqueeze(2).to_broadcast([P, 4, P]),
                                                ALU.mult).then_inc(*self.c.up("norm_diag"))

                    def diagonal(self, factors):
                        dve.wait_ge(*self.c.next("norm_c2"))
                        self.spread(factors)

                    def factors_read(self, dst):
                        dve.wait_ge(*self.c.next("rs"))

                    def split(self, key, k):
                        b = plan.block0[plan.at[key]] + k
                        self.eng.wait_ge(*self.c.next("w_hi"))
                        g = gain_of(key, k)
                        w, hi = raw[:, b % RAWS, :], w_hi[:, b % SLOTS, :].bitcast(FP32)
                        if g is None:
                            ins = self.nc.tensor_tensor(w_lo[:, b % SLOTS, :], w, hi, ALU.subtract)
                        else:
                            ins = self.nc.scalar_tensor_tensor(w_lo[:, b % SLOTS, :], w, gains[:, g:g + 1], hi,
                                                               ALU.mult, ALU.subtract)
                        ins.then_inc(*self.c.up("w_lo"))

                    def add_squares(self):
                        while self.squared:
                            h, t = self.squared.pop(0)
                            if t == 0:
                                self.c.skip("sq_tmp")
                                continue
                            dve.wait_ge(*self.c.next("sq_tmp"))
                            dve.wait_ge(*self.c.now("sq_sum"))
                            n = self.c.n.get("sq_sum", 0)
                            nc.vector.tensor_tensor(sq[:, h, :], sq[:, h, :], sqt[n % 3], ALU.add).then_inc(
                                *self.c.up("sq_sum"))

                    def empty_steps(self, key, h):
                        c, v = self.c, nc.vector

                        def branch(t):
                            bank = self.acc(key, h, t)
                            tile = y[:, 4 * key[3] + t, half(h)]
                            dve.wait_ge(*c.now("bank_free", 3))
                            v.tensor_tensor(tile, bank, tile, ALU.add).then_inc(*c.up("bank_free"))
                            self.squared.append((h, 4 * key[3] + t))

                        def gated(t):
                            if t < 4:
                                bank = self.acc(key, h, t)
                                dve.wait_ge(*c.now("gated"))
                                v.tensor_tensor(v_tmp[:, t % 2, :], bank, rs[:, half(h)], ALU.mult).then_inc(
                                    *c.up("bank_free"))
                            if t > 0:
                                tile = y[:, 3 + t, half(h)]
                                dve.wait_ge(*c.next("sig"))
                                v.tensor_tensor(tile, v_tmp[:, (t - 1) % 2, :], tile, ALU.mult).then_inc(
                                    *c.up("gated"))
                                self.squared.append((h, 3 + t))
                        if key[1] == "gate":
                            return [lambda t=t: gated(t) for t in range(5)]
                        return [lambda t=t: branch(t) for t in range(4)]

                    def empty(self, key, h, between=None):
                        self.drain(key, h, between)
                        if between and key[1] != "up":
                            between()

                    def drain(self, key, h, between):
                        kind, c, w = key[1], self.c, self.nc
                        wait = self.eng.wait_ge
                        rsh = rs[:, half(h)]
                        if last_branch(key) and kind != "proj":
                            for step in self.empty_steps(key, h):
                                self.add_squares()
                                step()
                            self.add_squares()
                        elif kind in ("mix", "down"):
                            for t in range(4):
                                bank = self.acc(key, h, t)
                                tile = y[:, 4 * key[3] + t, half(h)]
                                if key[2] == 0:
                                    w.tensor_copy(tile, bank).then_inc(*c.up("bank_free"))
                                else:
                                    wait(*c.now("bank_free", 3))
                                    w.tensor_tensor(tile, bank, tile, ALU.add).then_inc(*c.up("bank_free"))
                        elif kind == "proj":
                            for t in range(4):
                                bank = self.acc(key, h, t)
                                tile = y[:, 4 * key[2] + t, half(h)]
                                if key[2] == 0:
                                    wait(*c.next("sig"))
                                    w.tensor_tensor(tile, bank, tile, ALU.mult).then_inc(*c.up("bank_free"))
                                    self.add_squares()
                                    self.squared.append((h, t))
                                else:
                                    w.tensor_copy(tile, bank).then_inc(*c.up("bank_free"))
                            self.add_squares()
                        elif kind == "gate":
                            wait(*c.now("x_t"))
                            for t in range(4):
                                bank = self.acc(key, h, t)
                                w.tensor_tensor(y[:, t, half(h)], bank, rsh, ALU.mult).then_inc(*c.up("bank_free"))
                        elif kind == "c":
                            wait(*c.now("act_prod"))
                            for t in range(4):
                                bank = self.acc(key, h, t)
                                w.tensor_tensor(conv_out[:, t, half(h)], bank, rsh, ALU.mult).then_inc(
                                    *c.up("bank_free"))
                        elif kind == "u":
                            for t in range(4):
                                cu, res = conv_in[:, t % 2, :], conv_out[:, t, half(h)]
                                bank = self.acc(key, h, t)
                                wait(*c.now("cu"))
                                if h == 0:
                                    w.memset(cu[:, 0:2], 0.0).then_inc(*c.up("halo"))
                                else:
                                    w.tensor_copy(cu[:, 0:2], halo_keep[:, t, :]).then_inc(*c.up("halo"))
                                w.tensor_tensor(cu[:, 2:2 + HALF], bank, rsh, ALU.mult).then_inc(*c.up("bank_free"))
                                wait(*c.now("bank_free"))
                                w.tensor_tensor(cu[:, 2:2 + HALF], cu[:, 2:2 + HALF], res, ALU.mult).then_inc(*c.up("cu"))
                                wait(*c.now("cu"))
                                w.tensor_copy(halo_keep[:, t, :], cu[:, HALF:HALF + 2]).then_inc(*c.up("halo"))
                                tile = 4 * key[2] + t
                                col = [gains[:, sc_col(tap, tile):sc_col(tap, tile) + 1] for tap in range(3)]
                                w.tensor_scalar(res, cu[:, 0:HALF], col[0], None, ALU.mult).then_inc(*c.up("cu"))
                                for tap in (1, 2):
                                    wait(*c.now("cu"))
                                    w.scalar_tensor_tensor(res, cu[:, tap:tap + HALF], col[tap], res, ALU.mult,
                                                           ALU.add).then_inc(*c.up("cu"))
                        elif kind == "b":
                            wait(*c.now("cu"))
                            for t in range(5):
                                if t < 4:
                                    bank = self.acc(key, h, t)
                                    if t == 0:
                                        wait(*c.now("z_ready"))
                                    elif t >= 2:
                                        wait(*c.now("z_ready"))
                                    w.tensor_tensor(us[:, t % 2, :], bank, rsh, ALU.mult).then_inc(*c.up("bank_free"))
                                if t >= 1:
                                    wait(*c.now("bank_free", 1 if t < 4 else 0))
                                    w.tensor_tensor(us[:, (t - 1) % 2, :], us[:, (t - 1) % 2, :],
                                                    conv_out[:, t - 1, half(h)], ALU.mult).then_inc(*c.up("act_prod"))
                                    c.skip("z_ready")
                        elif kind == "up":
                            wait(*c.now("tap"))
                            for j in range(2):
                                g_in = conv_in[:, j, :]
                                if h == 0:
                                    w.memset(g_in[:, 0:2], 0.0).then_inc(*c.up("halo"))
                                else:
                                    w.tensor_copy(g_in[:, 0:2], g_in[:, HALF:HALF + 2]).then_inc(*c.up("halo"))
                            wait(*c.now("halo"))
                            for j in range(2):
                                bank = self.acc(key, h, j)
                                w.tensor_tensor(conv_in[:, j, 2:2 + HALF], bank, rsh, ALU.mult).then_inc(
                                    *c.up("bank_free"))
                            wait(*c.now("z_ready"))
                            for j in range(2):
                                bank = self.acc(key, h, 2 + j)
                                w.tensor_tensor(us[:, j, :], bank, rsh, ALU.mult).then_inc(*c.up("bank_free"))
                            if between:
                                between()
                            wait(*c.now("bank_free", 2))
                            for j in range(2):
                                w.tensor_scalar(v_tmp[:, j, :], conv_in[:, j, 0:HALF], self.column(key, 0, j), None,
                                                ALU.mult).then_inc(*c.up("tap"))
                            for tap in (1, 2):
                                for j in range(2):
                                    wait(*c.now("tap", 1))
                                    w.scalar_tensor_tensor(v_tmp[:, j, :], conv_in[:, j, tap:tap + HALF],
                                                           self.column(key, tap, j), v_tmp[:, j, :], ALU.mult,
                                                           ALU.add).then_inc(*c.up("tap"))
                            for j in range(2):
                                wait(*c.next("gelu"))
                                w.tensor_tensor(us[:, j, :], us[:, j, :], v_tmp[:, j, :], ALU.mult).then_inc(
                                    *c.up("act_prod"))
                            c.skip("z_ready", 2)
                        elif kind == "qk":
                            wait(*c.now("act_prod"))
                            for t in range(4):
                                bank = self.acc(key, h, t)
                                w.scalar_tensor_tensor(big[:, t, half(h)], bank, 1.0 if t < 2 else QKH ** -0.5, rsh,
                                                       ALU.mult, ALU.mult).then_inc(*c.up("bank_free"))
                        elif kind == "v":
                            wait(*c.now("c_upd"))
                            wait(*c.now("core_sw"))
                            for t in range(4):
                                bank = self.acc(key, h, t)
                                w.tensor_scalar(v_sb[:, 4 * h + t, :, 0:VH], bank.rearrange("p (j e) -> p j e", j=2),
                                                c2_pre[:, 4 * h + t:4 * h + t + 1], ONES, ALU.mult,
                                                ALU.mult).then_inc(*c.up("bank_free"))
                        elif kind == "o":
                            if h == 0:
                                wait(*c.now("core_h"))
                            for t0 in (0, 2):
                                wait(*c.now("z_ready"))
                                for t in (t0, t0 + 1):
                                    bank = self.acc(key, h, t)
                                    w.tensor_tensor(us[:, t % 2, :], bank, rsh, ALU.mult).then_inc(*c.up("bank_free"))
                                for t in (t0, t0 + 1):
                                    wait(*c.next("sig"))
                                    w.scalar_tensor_tensor(us[:, t % 2, :], us[:, t % 2, :], 1.0,
                                                           big[:, t // 2 + 2 * (t % 2), half(h)], ALU.add,
                                                           ALU.mult).then_inc(*c.up("act_prod"))
                                    c.skip("z_ready")

                    def renew(self, layer, which, h, work=None, key=None, blocks=None):
                        final = work is None
                        c = self.c
                        for k in range(DT):
                            g = norm_col(which, layer, k)
                            tile = y[:, k, half(h)]
                            if not final:
                                dve.wait_ge(*c.now("x_ready", 1 if k else 0))
                                dve.wait_ge(*c.now("sq_tmp"))
                            else:
                                dve.wait_ge(*c.now("x_new"))
                            nc.vector.scalar_tensor_tensor(xn[:, k % 2, :], tile, gains[:, g:g + 1], rs_post[h], ALU.mult,
                                                           ALU.mult).then_inc(*c.up("x_t"))
                            if not final:
                                self.add_squares()
                            dve.wait_ge(*c.now("x_t"))
                            dve.wait_ge(*c.next("x_old"))
                            nc.vector.tensor_tensor(tile if final else xn[:, k % 2, :], xn[:, k % 2, :],
                                                    x_old[:, k % 2, :], ALU.add).then_inc(*c.up("x_new"))
                            if not final:
                                self.squared.append((h, k))
                                c.skip("x_ready")
                                for other in work[k]:
                                    other()
                                for b in blocks.get(k, ()):
                                    self.split(key, b)
                        self.add_squares()

                    def p_split(self, h):
                        for f in range(2):
                            dve.wait_ge(*self.c.next("p_hi"))
                            nc.vector.tensor_tensor(z_lo[:, f, half(h)], psum[:, 4 + f, :],
                                                    z_hi[:, f, half(h)].bitcast(FP32), ALU.subtract).then_inc(
                                *self.c.up("p_lo"))

                    def gates(self):
                        c, v = self.c, nc.vector
                        g0 = norm_col(0, 1)
                        v.tensor_tensor(gate_g, gate_raw, gains[:, g0:g0 + DT].unsqueeze(2).to_broadcast([P, DT, 8]),
                                        ALU.mult).then_inc(*c.up("gate_step"))
                        v.memset(zf_hi.bitcast(FP32), 0.0).then_inc(*c.up("gate_step"))
                        v.memset(zf_lo.bitcast(FP32), 0.0).then_inc(*c.up("gate_step"))
                        dve.wait_ge(*c.now("gate_step"))
                        for to, of in ((0, 0), (64, 4)):
                            v.tensor_copy(zf_hi[:, :, to:to + 4], gate_g[:, :, of:of + 4]).then_inc(*c.up("gate_step"))
                        dve.wait_ge(*c.now("gate_step"))
                        for to, of in ((0, 0), (64, 4)):
                            ins = v.tensor_tensor(zf_lo[:, :, to:to + 4], gate_g[:, :, of:of + 4],
                                                  zf_hi[:, :, to:to + 4].bitcast(FP32), ALU.subtract)
                        ins.then_inc(*c.up("gate_w"))
                        chunk_on = y[0:4, 4, :]
                        v.memset(rows, 0.0).then_inc(*c.up("gate_step"))
                        v.memset(rows2, 0.0).then_inc(*c.up("gate_step"))
                        v.memset(chunk_on, 1.0).then_inc(*c.up("gate_step"))
                        v.memset(v_sb[:, :, :, VH:VH + 1], 1.0).then_inc(*c.up("gate_step"))
                        dve.wait_ge(*c.now("gate_step"))
                        v.memset(chunk_on.rearrange("p (c n) -> p c n", n=P)[:, :, 0:1], 0.0).then_inc(
                            *c.up("gate_step"))
                        for h in range(2):
                            dve.wait_ge(*c.next("gate_acc"))
                            for q, r in ((0, 0), (1, 64)):
                                v.tensor_tensor(y[r:r + 4, q, half(h)], psum[r:r + 4, h, :], rs[r:r + 4, half(h)],
                                                ALU.mult).then_inc(*c.up("gate_ev"))
                        dve.wait_ge(*c.now("gate_ev"))
                        ig, f, lf, m, b = (y[0:4, q, :] for q in (0, 2, 3, 5, 7))
                        v.tensor_scalar(ig, ig, bias_i[0:4, :], None, ALU.add).then_inc(*c.up("gate_step"))
                        v.tensor_scalar(f, y[64:68, 1, :], bias_f[64:68, :], None, ALU.add).then_inc(
                            *c.up("gate_step"))
                        dve.wait_ge(*c.now("gate_step"))
                        v.scalar_tensor_tensor(lf, f, -1.0, f, ALU.mult, ALU.max).then_inc(*c.up("gate_step"))
                        assert c.n["gate_step"] == GATE_ABS
                        dve.wait_ge(*c.next("gate_e", 2))
                        v.scalar_tensor_tensor(lf, f, 0.0, lf, ALU.min, ALU.subtract).then_inc(*c.up("gate_step"))
                        dve.wait_ge(*c.now("gate_step"))
                        v.tensor_tensor_scan(m, lf, ig, 0.0, ALU.add, ALU.max).then_inc(*c.up("gate_step"))
                        v.tensor_tensor_scan(b, chunk_on, lf, 0.0, ALU.mult, ALU.add).then_inc(*c.up("gate_step"))
                        dve.wait_ge(*c.now("gate_step"))
                        bm = rows[0:4, :]
                        v.tensor_tensor(bm, b, m, ALU.subtract).then_inc(*c.up("gate_step"))
                        v.tensor_tensor(rows2[0:4, :], ig, b, ALU.subtract).then_inc(*c.up("gate_step"))
                        v.memset(m_state[0:4, 0:1], 0.0).then_inc(*c.up("gate_step"))
                        v.tensor_copy(m_state[0:4, 1:8],
                                      m.rearrange("p (c n) -> p c n", n=P)[:, 0:7, P - 1]).then_inc(*c.up("gate_step"))
                        dve.wait_ge(*c.now("gate_step"))
                        by_chunk = bm.rearrange("p (c n) -> p c n", n=P)
                        v.tensor_tensor(y[0:4, 1, :].rearrange("p (c n) -> p c n", n=P), by_chunk,
                                        m_state[0:4, 0:8].unsqueeze(2).to_broadcast([4, CH, P]), ALU.add).then_inc(
                            *c.up("gate_step"))
                        v.tensor_tensor(y[0:4, 2, :].rearrange("p (c n) -> p c n", n=P),
                                        rows2[0:4, :].rearrange("p (c n) -> p c n", n=P),
                                        by_chunk[:, :, P - 1:P].to_broadcast([4, CH, P]), ALU.add).then_inc(
                            *c.up("gate_step"))
                        assert c.n["gate_step"] == GATE_ROWS_DONE
                        for n, (dst, r) in enumerate(((col_a, 64), (col_g, 0), (col_m, 32))):
                            for q in range(2):
                                bank = 4 + q if n == 0 else 6 + q
                                if n == 0:
                                    dve.wait_ge(*c.next("gate_t"))
                                elif n == 1:
                                    dve.wait_ge(*c.next("gate_t"))
                                v.tensor_copy(dst[:, 4 * q:4 * q + 4, :],
                                              psum[:, bank, :].rearrange("p (c n) -> p c n", n=P)[:, :, r:r + 4]
                                              ).then_inc(*c.up("gate_step"))
                        assert c.n["gate_step"] == GATE_COLUMNS_DONE

                    def core(self, part, h, nxt):
                        c, v = self.c, nc.vector
                        s = 4 * h
                        if h == 0:
                            v.memset(state, 0.0).then_inc(*c.up("c_upd0"))
                            dve.wait_ge(*c.now("c_upd0"))
                        for k in range(10):
                            if 1 <= k <= 8:
                                u = k - 1
                                ch, j = 4 * h + u // 2, u % 2
                                head = 2 * part + j
                                dve.wait_ge(*c.next("core_num"))
                                d_ps = psum[:, s + 1, VH:VH + 1]
                                v.tensor_scalar(den, d_ps, -1.0, None, ALU.mult).then_inc(*c.up("core_den"))
                                dve.wait_ge(*c.now("core_den"))
                                v.scalar_tensor_tensor(den, d_ps, col_m[:, ch, head:head + 1], den, ALU.max,
                                                       ALU.max).then_inc(*c.up("core_den"))
                                dve.wait_ge(*c.now("core_den"))
                                v.reciprocal(rden, den).then_inc(*c.up("core_r"))
                                dve.wait_ge(*c.next("core_u"))
                                v.scalar_tensor_tensor(state[:, j, :], state[:, j, :], dec, psum[:, s + 2, 0:VH + 1],
                                                       ALU.mult, ALU.add).then_inc(*c.up("c_upd"))
                            if k <= 7:
                                ch, j = 4 * h + k // 2, k % 2
                                head = 2 * part + j
                                dve.wait_ge(*c.next("core_a"))
                                dve.wait_ge(*c.now("core_sw"))
                                v.scalar_tensor_tensor(dmat, psum[:, s, 2 * P:3 * P], col_g[:, ch, head:head + 1],
                                                       mask[:, :], ALU.add, ALU.min).then_inc(*c.up("core_d"))
                                v.tensor_tensor(qw, psum[:, s, 3 * P:4 * P], big[:, j, ch * P:(ch + 1) * P], ALU.mult)
                                v.tensor_scalar(kw, psum[:, s, 0:P], col_a[:, ch, head:head + 1], None, ALU.mult)
                                if k > 0:
                                    dve.wait_ge(*c.now("c_upd"))
                                v.tensor_copy(dec, psum[:, s, 4 * P - 1:4 * P])
                                dve.wait_ge(*c.next("core_e"))
                                v.tensor_tensor(sw, psum[:, s, P:2 * P], dmat, ALU.mult).then_inc(*c.up("core_sw"))
                            if 1 <= k <= 8:
                                dve.wait_ge(*c.next("core_rstd"))
                                dve.wait_ge(*c.now("core_ht"))
                                v.tensor_scalar(hn2, hn, hrstd, None, ALU.mult).then_inc(*c.up("core_h2"))
                                c.skip("core_ht")
                            if nxt and 1 <= k <= 8:
                                self.split(nxt, k - 1)
                        c.skip("core_h", 16)

                    def store(self, h):
                        for e in range(8 * h, 8 * h + 8):
                            tb = e // 2
                            if tb >= 3 and e % 2 == 0:
                                dve.wait_ge(out_done[tb % 3], 16 * (tb // 3))
                            dve.wait_ge(*self.c.next("out_t"))
                            nc.vector.tensor_copy(out_rows[:, tb % 3, (e % 2) * HALF:(e % 2 + 1) * HALF],
                                                  psum[:, e % 4, :]).then_inc(*self.c.up("out_c"))

                stages(Vector(dve, nc.vector))

            @block.gpsimd
            def _(pool):
                class Pool(Common):
                    def start(self):
                        nc.gpsimd.memset(ones[:, :], ONES).then_inc(*self.c.up("const"))
                        nc.gpsimd.memset(minus_half, -0.5).then_inc(*self.c.up("pow_in"))
                        nc.gpsimd.memset(ident[:, :], 0.0).then_inc(*self.c.up("const"))
                        nc.gpsimd.memset(mask[:, :], 0.0).then_inc(*self.c.up("const"))
                        pool.wait_ge(*self.c.now("const"))
                        nc.gpsimd.affine_select(out=ident[:, :], in_=ident[:, :], compare_op=ALU.not_equal, fill=1.0,
                                                base=0, pattern=[[-1, P]], channel_multiplier=1).then_inc(
                            *self.c.up("const"))
                        nc.gpsimd.affine_select(out=mask[:, :], in_=mask[:, :], compare_op=ALU.is_ge, fill=-3.0e38,
                                                base=0, pattern=[[1, P]], channel_multiplier=-1).then_inc(
                            *self.c.up("const"))
                        pool.wait_ge(*self.c.next("xin_ss", CH))
                        self.factors(c2_pre, ss_in, D * EPS * ONES, "norm_c2")

                    def factors(self, dst, sums, eps, name):
                        n = sums.shape[1]
                        nc.gpsimd.tensor_scalar(pow_in[:, 0:n], sums, eps, None, ALU.add).then_inc(*self.c.up("pow_in"))
                        pool.wait_ge(*self.c.now("pow_in"))
                        nc.gpsimd.tensor_tensor(dst, pow_in[:, 0:n], minus_half[:, 0:n], ALU.pow).then_inc(
                            *self.c.up(name))

                    def sums_read(self, factors):
                        n = self.c.n.get("norm_c1", 0)
                        pool.wait_ge(*self.c.next("norm_c1"))
                        self.factors(factors, c1[:, n % 2, :], D * EPS * ONES, "norm_c2")

                    def empty(self, key, h, between=None):
                        if between:
                            between()
                        n = {"up": 2, "b": 4, "o": 4}.get(key[1], 0)
                        for t in range(n):
                            zt = 2 * key[3] + t if key[1] == "up" else t
                            self.eng.wait_ge(*self.c.next("z_hi"))
                            self.nc.tensor_tensor(z_lo[:, zt, half(h)], us[:, t % 2, :],
                                                  z_hi[:, zt, half(h)].bitcast(FP32), ALU.subtract).then_inc(
                                *self.c.up("z_ready"))

                    def renew(self, layer, which, h, work=None, key=None, blocks=None):
                        final = work is None
                        c = self.c
                        for k in range(DT + 1):
                            if k < DT:
                                pool.wait_ge(*c.now("x_new" if final else "x_ready"))
                                nc.gpsimd.tensor_tensor(x_old[:, k % 2, :], x_hi[:, k, half(h)].bitcast(FP32),
                                                        x_lo[:, k, half(h)].bitcast(FP32), ALU.add).then_inc(
                                    *c.up("x_old"))
                            if k > 0:
                                if final:
                                    c.skip("x_new")
                                else:
                                    pool.wait_ge(*c.next("x_hi"))
                                    nc.gpsimd.tensor_tensor(x_lo[:, k - 1, half(h)], xn[:, (k - 1) % 2, :],
                                                            x_hi[:, k - 1, half(h)].bitcast(FP32),
                                                            ALU.subtract).then_inc(*c.up("x_ready"))
                                    c.skip("x_new")
                                    for other in work[k - 1]:
                                        other()

                    def core(self, part, h, nxt):
                        for _ in range(8):
                            pool.wait_ge(*self.c.next("core_ss"))
                            self.factors(hrstd, hss, VH * EPS, "core_rstd")

                stages(Pool(pool, nc.gpsimd))


_INS = ["x", "p", "norm_mix_pre", "norm_mix_post", "norm_ffn_pre", "norm_ffn_post", "sc_w_in", "sc_w_conv", "sc_w_out",
        "ml_w_in", "ml_gate_bias", "ml_head_norm", "ml_w_out", "ffn_w_up", "ffn_w_conv", "ffn_w_down",
        "ple_norm_gate", "ple_w_gate", "ple_w_proj", "ple_norm_out"]


def kernel(**inputs):
    import numpy as np
    import concourse.bacc as bacc
    from concourse.bass_utils import run_bass_kernel_spmd

    nc = bacc.Bacc("TRN2", target_bir_lowering=False, num_devices=1, dynamic_dma_scratch_size=1024)
    arrays, args = {}, []
    for name in _INS:
        a = np.ascontiguousarray(inputs[name])
        arrays[f"in_{name}"] = a
        args.append(nc.dram_tensor(f"in_{name}", a.shape, mybir.dt.from_np(a.dtype), kind="ExternalInput").ap())
    out = nc.dram_tensor("out", (1, SEQ, D), FP32, kind="ExternalOutput").ap()
    decoder_kernel(nc, *args, out)
    return run_bass_kernel_spmd(nc, [arrays], core_ids=[0]).results[0]["out"]
```

```python
import concourse.bass as bass
from concourse import mybir
from contextlib import ExitStack

FP32 = mybir.dt.float32
FP32R = mybir.dt.float32r
ALU = mybir.AluOpType
ACT = mybir.ActivationFunctionType

P = 128
D = 1024
SEQ = 1024
DEPTH = 2
PD = 256
MLSTM_GATES = 3072
HEADS = 4
QKH = 128
VH = 256
FF = 2816
EPS = 1e-6
HALF = SEQ // 2
BLOCKW = 512
DT = D // P
SLOTS = 8
RAWS = 4
CH = SEQ // P
ONES = 1024.0
SMALL = (FF // P) % 4
PARTS = 1 + FF // P // 4
LOOP0 = 2
LOOPED = PARTS - 1 - LOOP0
PER_PART = {"w_hi": 24, "w_lo": 24, "block_used": 14, "acc": 32, "bank_free": 32, "halo": 8, "tap": 24, "gelu": 8,
            "act_prod": 8, "z_hi": 8, "z_ready": 8}


class Plan:

    def __init__(self):
        self.groups = []
        self.keys = []
        self.block0 = []
        self.at = {}
        self.used0 = []
        self.z0 = []
        self.blocks = self.used = self.z = 0

    def add(self, key, k):
        self.at[key] = len(self.groups)
        self.keys.append(key)
        self.groups.append(k)
        self.block0.append(self.blocks)
        self.used0.append(self.used)
        self.z0.append(self.z)
        self.blocks += k
        self.used += k - 1 if k == SLOTS else 0
        self.z += 2 * {"b": 4, "o": 4, "up": 2}.get(key[1], 0)


    def fill(self, key, h):
        n = self.at[key]
        return 2 * (n - key[3]) + 2 * h + key[3] if key[1] in ("mix", "down") else 2 * n + h


def part_tiles(part):
    return SMALL if part == 1 else 4


def part_start(part):
    return sum(part_tiles(q) for q in range(part))


def make_plan():
    plan = Plan()
    for layer in range(DEPTH):
        for part in range(2):
            for kind in ("c", "u", "b") if layer == 0 else ("qk", "v", "o"):
                plan.add((layer, kind, part), DT)
            for g in range(2):
                plan.add((layer, "mix", part, g), 4)
        for part in range(PARTS):
            tiles = part_tiles(part)
            for g in range(tiles // 2):
                plan.add((layer, "up", part, g), DT)
            for g in range(2):
                plan.add((layer, "down", part, g), tiles)
        for kind, g in ("gate", 0), ("proj", 0), ("proj", 1), ("gate", 1):
            plan.add((layer, kind, g), DT if kind == "gate" else PD // P)
    return plan


class Counts:

    def __init__(self, sems):
        self.sems = sems
        self.n = {}
        self.per = None
        self.i = None

    def value(self, name, back=0):
        n = self.n.get(name, 0) - back
        if self.per is None or not self.per.get(name, 0):
            return max(n, 0)
        return self.i * self.per[name] + n

    def up(self, name):
        self.n[name] = self.n.get(name, 0) + 1
        return self.sems[name], 1

    def next(self, name, k=1):
        self.n[name] = self.n.get(name, 0) + k
        return self.sems[name], self.value(name)

    def now(self, name, back=0):
        return self.sems[name], self.value(name, back)

    def skip(self, name, k=1):
        self.n[name] = self.n.get(name, 0) + k

    def enter(self, i):
        self.per, self.i = PER_PART, i

    def leave(self, trips):
        self.n = {k: v + (trips - 1) * self.per.get(k, 0) for k, v in self.n.items()}
        self.per = self.i = None


NORM_BANKS = [6, 7] + 2 * [7, 6, 7, 3] + [3, 6, 7, 3] + 2 * [7, 6, 7, 3] + [3, 7]
GATE_ABS, GATE_ROWS_DONE, GATE_COLUMNS_DONE, GATE_EXPS = 13, 22, 28, 5


SEMS = ("pow_in w_hi w_lo block_used acc bank_free sq_tmp sq_sum norm_col norm_c1 norm_c2 norm_diag norm_row rs "
        "x_old x_t x_new x_hi x_ready halo tap cu gelu act_prod z_hi z_ready p_t p_hi p_lo sig gated "
        "const const_t const_c xin_t xin_ss xin_hi xin_ready "
        "gate_w gate_acc gate_ev gate_step gate_e gate_t "
        "core_a core_d core_e core_sw core_num core_u core_r core_den c_upd0 c_upd core_hn core_ss core_rstd "
        "core_h2 core_ht core_h const_r out_t out_c out_d").split()


def decoder_kernel(nc, x, p, norm_mix_pre, norm_mix_post, norm_ffn_pre, norm_ffn_post, sc_w_in, sc_w_conv,
                   sc_w_out, ml_w_in, ml_gate_bias, ml_head_norm, ml_w_out, ffn_w_up, ffn_w_conv, ffn_w_down,
                   ple_norm_gate, ple_w_gate, ple_w_proj, ple_norm_out, tables, out):
    plan = make_plan()
    ctx = ExitStack()
    with ctx:
        def sb(name, shape, dt=FP32):
            return ctx.enter_context(nc.sbuf_tensor(name, shape, dt))

        S = {name: ctx.enter_context(nc.semaphore(name)) for name in SEMS}
        raw_in = [ctx.enter_context(nc.semaphore(f"raw_in{i}")) for i in range(RAWS)]
        x_in = [ctx.enter_context(nc.semaphore(f"x_in{i}")) for i in range(CH)]
        table_in = ctx.enter_context(nc.semaphore("table_in"))
        const_in = ctx.enter_context(nc.semaphore("const_in"))
        gate_w_in = ctx.enter_context(nc.semaphore("gate_w_in"))
        p_in = ctx.enter_context(nc.semaphore("p_in"))
        out_done = ctx.enter_context(nc.semaphore("out_done"))

        raw = sb("raw", [P, RAWS, BLOCKW])
        w_hi = sb("w_hi", [P, SLOTS, BLOCKW], FP32R)
        w_lo = sb("w_lo", [P, SLOTS, BLOCKW], FP32R)
        x_hi = sb("x_hi", [P, DT, SEQ], FP32R)
        x_lo = sb("x_lo", [P, DT, SEQ], FP32R)
        z_hi = sb("z_hi", [P, 4, SEQ], FP32R)
        z_lo = sb("z_lo", [P, 4, SEQ], FP32R)
        y = sb("y", [P, DT, SEQ])
        rs = sb("rs", [P, SEQ])
        ident = sb("ident", [P, P])
        ident_r = sb("ident_r", [P, P], FP32R)
        ones = sb("ones", [P, P])
        gains = sb("gains", [P, 260])
        small = sb("small", [P, 312])
        mask = sb("mask", [P, P])
        big = sb("big", [P, 4, SEQ])
        area = sb("area", [P, 8 * 2 * (VH + 1)])
        us = sb("us", [P, 2, HALF])
        core = sb("core", [P, 2562])
        psum = ctx.enter_context(nc.psum_tensor("psum", [P, 8, BLOCKW], FP32))

        rs_post = (area[:, 0:512], us[:, 0, :])
        sq = area[:, 512:1536].rearrange("p (h n) -> p h n", h=2)
        x_old = area[:, 1536:2560].rearrange("p (b n) -> p b n", b=2)
        xn = area[:, 2560:3584].rearrange("p (b n) -> p b n", b=2)
        sqt = (area[:, 3584:4096], core[:, 1538:2050], core[:, 2050:2562])
        v_sb = area[:, :].rearrange("p (c j e) -> p c j e", c=CH, j=2)
        diag = core[:, 0:512]
        conv_in = core[:, 512:1540].rearrange("p (b n) -> p b n", b=2)
        halo_keep = core[:, 1540:1548].rearrange("p (t n) -> p t n", t=4)
        v_tmp = big[:, 0, :].rearrange("p (b n) -> p b n", b=2)
        p_rows = big[:, 1:3, :].rearrange("p a n -> p (a n)").rearrange("p (c f) -> p c f", c=CH)
        conv_out = big
        raw_rows = raw[:, :, :].rearrange("p a n -> p (a n)")
        out_rows = ((big[:, 1, :], big[:, 2, :], big[:, 3, :], area[:, 1536:2560]),
                    (raw_rows[:, 0:1024], raw_rows[:, 1024:2048], area[:, 2560:3584], big[:, 0, :]))
        sqt_core = us[:, 0, 0:VH]
        rows = core[:, 0:1024]
        state = core[:, 1024:1538].rearrange("p (j e) -> p j e", j=2)
        dmat = core[:, 1538:1666]
        sw = core[:, 1666:1794]
        qw = core[:, 1794:1922]
        kw = core[:, 1922:2050]
        hn = core[:, 2050:2306]
        hn2 = core[:, 2306:2562]
        rows2 = y[:, 6, :]
        pow_in = small[:, 288:296]
        minus_half = small[:, 296:304]
        gate_raw = small[:, 160:224].rearrange("p (k c) -> p k c", k=DT)
        gate_g = small[:, 224:288].rearrange("p (k c) -> p k c", k=DT)
        zf_hi = z_hi[:, :, :].rearrange("p a n -> p (a n)")[:, 0:DT * 68].rearrange("p (k c) -> p k c", k=DT)
        zf_lo = z_lo[:, :, :].rearrange("p a n -> p (a n)")[:, 0:DT * 68].rearrange("p (k c) -> p k c", k=DT)

        c1 = small[:, 304:312].rearrange("p (b j) -> p b j", b=2)
        c2 = small[:, 4:8]
        c2_pre = small[:, 8:16]
        ss_in = small[:, 16:24]
        dec = small[:, 24:25]
        den = small[:, 25:26]
        ss_raw = small[:, 144:152]
        rden = small[:, 26:27]
        hss = small[:, 27:28]
        hrstd = small[:, 28:29]
        bias_i = small[:, 29:30]
        bias_f = small[:, 30:31]
        head_gain = small[:, 32:40]
        m_state = small[:, 40:48]
        col_g = small[:, 48:80].rearrange("p (c h) -> p c h", c=CH)
        col_a = small[:, 80:112].rearrange("p (c h) -> p c h", c=CH)
        col_m = small[:, 112:144].rearrange("p (c h) -> p c h", c=CH)

        NORMS = [norm_mix_pre, norm_mix_post, norm_ffn_pre, norm_ffn_post, ple_norm_gate, ple_norm_out]
        SC_COL, HN_COL, FF_COL = 96, 120, 128

        def norm_col(which, layer, t=0):
            return (which * DEPTH + layer) * DT + t

        def sc_col(tap, t):
            return SC_COL + tap * DT + t

        def ff_col(layer, tap, t):
            return FF_COL + (layer * 3 + tap) * (FF // P) + t

        def half(h):
            return slice(h * HALF, (h + 1) * HALF)

        def x_bank(e):
            return e % 6 if e < 8 else 4 + e % 2

        def block_source(key, k, i=0):
            layer, kind = key[0], key[1]
            r = slice(k * P, (k + 1) * P)
            if kind in ("c", "u", "b"):
                c0 = {"b": 0, "c": D, "u": 2 * D}[kind] + key[2] * BLOCKW
                return sc_w_in[0, r, c0:c0 + BLOCKW]
            if kind == "qk":
                two = ml_w_in[0, r, 0:2 * HEADS * QKH].rearrange("r (s c) -> r s c", s=2)
                return two[:, :, key[2] * 256:key[2] * 256 + 256]
            if kind in ("v", "o"):
                c0 = 2 * HEADS * QKH + (HEADS * VH if kind == "o" else 0) + key[2] * BLOCKW
                return ml_w_in[0, r, c0:c0 + BLOCKW]
            if kind == "mix":
                w = (sc_w_out, ml_w_out)[layer]
                return w[0, key[2] * 512 + k * P:key[2] * 512 + (k + 1) * P, key[3] * BLOCKW:(key[3] + 1) * BLOCKW]
            if kind == "up":
                part, g = key[2], key[3]
                c0 = part_start(part) * P + g * 256
                two = ffn_w_up[layer, r, :].rearrange("r (s c) -> r s c", s=2)
                return two[:, :, bass.ds(i * 512 + c0, 256)] if not isinstance(i, int) else two[:, :, c0:c0 + 256]
            if kind == "down":
                part, g = key[2], key[3]
                r0 = (part_start(part) + k) * P
                c = slice(g * BLOCKW, (g + 1) * BLOCKW)
                return ffn_w_down[layer, bass.ds(i * 512 + r0, P), c] if not isinstance(i, int) else ffn_w_down[layer, r0:r0 + P, c]
            if kind == "proj":
                return ple_w_proj[layer, r, key[2] * BLOCKW:(key[2] + 1) * BLOCKW]
            return ple_w_gate[layer, r, key[2] * BLOCKW:(key[2] + 1) * BLOCKW]

        def gain_of(key, k):
            which = {"c": 0, "u": 0, "b": 0, "qk": 0, "v": 0, "o": 0, "up": 2, "gate": 4}.get(key[1])
            return None if which is None else norm_col(which, key[0], k)

        def body_keys(layer, part):
            return [(layer, kind, part, g) for kind in ("up", "down") for g in range(2)
                    if (layer, kind, part, g) in plan.at]

        def stages(e):
            e.start()
            for layer in range(DEPTH):
                kinds = ("c", "u", "b") if layer == 0 else ("qk", "v", "o")
                for part in range(2):
                    mix0, mix1 = (layer, "mix", part, 0), (layer, "mix", part, 1)
                    a, b, o = [(layer, kind, part) for kind in kinds]
                    if layer == 1 and part == 0:
                        e.empty(a, 1)
                        e.gates()
                    else:
                        e.empty(a, 0)
                        e.splits(b)
                        e.empty(a, 1)
                    e.empty(b, 0)
                    if layer == 0:
                        e.splits(o)
                        e.empty(b, 1)
                    else:
                        e.core(part, 0, o)
                        e.empty(b, 1)
                        e.core(part, 1, None)
                    e.empty(o, 0)
                    e.splits(mix0)
                    e.splits(mix1)
                    e.empty(o, 1)
                    if part == 0:
                        e.empty(mix0, 0)
                        e.empty(mix1, 0)
                        e.empty(mix0, 1)
                        e.splits((layer, kinds[0], 1))
                        e.empty(mix1, 1)
                up0, up1 = (layer, "up", 0, 0), (layer, "up", 0, 1)
                boundary(e, layer, mix1, up0, up1, 1)
                e.empty(up0, 1)
                feed_part(e, layer, 0)
                feed_part(e, layer, 1)
                e.loop(LOOPED, lambda: feed_part(e, layer, LOOP0))
                feed_part(e, layer, PARTS - 1)
                gate0, proj0, proj1, gate1 = [(layer, kind, g) for kind, g in
                                              (("gate", 0), ("proj", 0), ("proj", 1), ("gate", 1))]
                boundary(e, layer, (layer, "down", PARTS - 1, 1), gate0, proj0, 3)
                e.splits(proj1)
                e.empty(gate0, 1)
                e.empty(proj0, 0)
                e.splits(gate1, range(0, 4))
                e.empty(proj0, 1)
                e.splits(gate1, range(4, 6))
                e.empty(proj1, 0)
                e.splits(gate1, range(6, 8))
                e.empty(proj1, 1)
                if layer + 1 < DEPTH:
                    boundary(e, layer, gate1, (1, "qk", 0), (1, "v", 0), 5)
            e.empty(gate1, 0)
            e.sums_read(c2)
            e.diagonal(c2)
            e.factors_read(rs_post[0])
            e.factors_stand()
            e.last_terms(0)
            for b in range(4):
                e.out_copy(0, b)
            for n, step in enumerate(e.empty_steps(gate1, 1)):
                step()
                e.add_squares()
                if n < 4:
                    e.out_copy(0, 4 + n)
            e.sums_read(c2)
            e.diagonal(c2)
            e.factors_read(rs_post[1])
            e.factors_stand()
            e.last_terms(1)
            for b in range(8):
                e.out_copy(1, b)

        def first_blocks(e):
            return {7: range(0, 4), 9: range(4, 6), 11: range(6, 8)}.get(e, ())

        def by_vector(h, b):
            return h == 1 and b in (5, 7)

        def out_copies(h, b):
            done = [by_vector(q // 8, q % 8) for q in range(8 * h + b + 1)]
            return done.count(False), done.count(True)

        def feed_part(e, layer, part):
            ups, (down0, down1) = body_keys(layer, part)[:-2], body_keys(layer, part)[-2:]
            for up, nxt in zip(ups, ups[1:] + [down0]):
                if up != (layer, "up", 0, 0):
                    e.empty(up, 0)
                    e.splits(nxt)
                    if nxt == down0:
                        e.splits(down1)
                    e.empty(up, 1)
            if part < PARTS - 1:
                e.empty(down0, 0)
                e.empty(down1, 0)
                e.empty(down0, 1)
                e.splits((layer, "up", part + 1, 0))
                e.empty(down1, 1)

        def boundary(e, layer, done, key0, key1, post):
            pair = done[1] != "gate"
            proj = key0[1] == "gate"
            work, blocks = {k: [] for k in range(DT)}, {}
            if pair:
                e.empty(done[:3] + (0,), 0)
            e.empty(done, 0)
            e.sums_read(c2)
            e.diagonal(c2)
            if pair:
                first, second = e.empty_steps(done[:3] + (0,), 1), e.empty_steps(done, 1)
                work[0] += first[:1]
                work[1] += first[1:2]
                work[2] += first[2:]
                work[4] += second[:2]
                work[5] += second[2:]
                blocks |= {1: [0], 2: [1], 3: [2, 3], 4: [4], 5: [5], 6: [6], 7: [7]}
            else:
                e.gate_weights()
                e.split(key0, 0)
                e.split(key0, 1)
                blocks |= {k: [k + 2] for k in range(DT - 2)}
                steps = e.empty_steps(done, 1)
                work[3] += steps[:2]
                work[4] += steps[2:4]
                work[5] += steps[4:]
            work[6].append(lambda: e.sums_read(c2))
            if proj:
                work[5].append(lambda: e.p_split(0))
                work[6].append(lambda: e.p_split(1))
            work[7].append(lambda: e.diagonal(c2))
            e.factors_read(rs_post[0])
            e.factors_stand()
            e.renew(layer, post, 0, work, key0, blocks)
            e.factors_read(rs_post[1])
            e.factors_stand()
            work = {k: [] for k in range(DT)}
            work[0].append(lambda: e.sums_read(c2_pre[:, 0:4]))
            work[2].append(lambda: e.diagonal(c2_pre[:, 0:4]))
            work[3].append(lambda: e.factors_read(rs[:, half(0)]))
            e.renew(layer, post, 1, work, key1, {6: [0], 7: [1]})
            e.factors_stand()

            def pre1():
                for k in range(2, plan.groups[plan.at[key1]]):
                    e.split(key1, k)
                e.sums_read(c2_pre[:, 4:8])
                e.diagonal(c2_pre[:, 4:8])
                e.factors_read(rs[:, half(1)])
                e.factors_stand()
            e.empty(key0, 0, pre1)

        def last_branch(key):
            return (key[1:] in (("gate", 1), ("proj", 0)) or (key[1] == "mix" and key[2] == 1)
                    or (key[1] == "down" and key[2] == PARTS - 1))

        class Common:

            def __init__(self, engine, compute):
                self.eng, self.nc = engine, compute
                self.c = Counts(S)
                self.i = 0

            def splits(self, key, blocks=None):
                for k in blocks or range(plan.groups[plan.at[key]]):
                    self.split(key, k)

            def loop(self, trips, body):
                with self.eng.Fori(0, trips) as i:
                    self.i = i
                    self.c.enter(i)
                    body()
                self.i = 0
                self.c.leave(trips)

            def split(self, key, k):
                pass

            def sums_read(self, factors):
                pass

            def diagonal(self, factors):
                pass

            def factors_read(self, dst):
                pass

            def factors_stand(self):
                pass

            def empty_steps(self, key, h):
                return []

            def p_split(self, h):
                pass

            def gate_weights(self):
                pass

            def gates(self):
                pass

            def add_squares(self):
                pass

            def last_terms(self, h):
                pass

            def out_copy(self, h, b):
                pass

        with nc.Block() as block:

            @block.sync
            def _(sp):
                def load(key, k, i=0):
                    b = plan.block0[plan.at[key]] + k
                    if b >= RAWS:
                        sp.wait_ge(S["w_lo"], i * PER_PART["w_lo"] + b - RAWS + 1)
                    src = block_source(key, k, i)
                    dst = raw[:, b % RAWS, :]
                    if len(src.shape) == 3:
                        dst = dst.rearrange("p (s c) -> p s c", s=2)
                    sp.dma_start(dst, src).then_inc(raw_in[b % RAWS], 16)

                def group(key, i=0):
                    for k in range(plan.groups[plan.at[key]]):
                        load(key, k, i)

                def load_x(tb):
                    sp.dma_start(y[:, tb, :], x[0, tb * P:(tb + 1) * P, :]).then_inc(x_in[tb], 16)

                sp.dma_start(ident[:, :], tables[0]).then_inc(table_in, 16)
                sp.dma_start(mask[:, :], tables[1]).then_inc(table_in, 16)
                load_x(0)
                load_x(1)
                for w, v in enumerate(NORMS):
                    sp.dma_start(us[w * 16:w * 16 + 16, 0, 0:P],
                                 v.rearrange("l (t q) -> (l t) q", q=P)).then_inc(const_in, 16)
                sp.dma_start(us[96:120, 0, 0:P],
                             sc_w_conv.rearrange("l j (t q) -> (l j t) q", q=P)).then_inc(const_in, 16)
                sp.dma_start(us[120:128, 0, 0:P],
                             ml_head_norm.rearrange("l (t q) -> (l t) q", q=P)).then_inc(const_in, 16)
                for layer in range(DEPTH):
                    sp.dma_start(us[0:66, 0, P * (1 + layer):P * (2 + layer)],
                                 ffn_w_conv[layer].rearrange("j (t q) -> (j t) q", q=P)).then_inc(const_in, 16)
                load_x(2)
                load_x(3)
                for k in range(RAWS):
                    load((0, "c", 0), k)
                for tb in range(4, CH):
                    load_x(tb)
                    if tb < 6:
                        load((0, "c", 0), 2 * tb - 4)
                        load((0, "c", 0), 2 * tb - 3)
                bias = ml_gate_bias.rearrange("l g -> g l")
                with nc.allow_non_contiguous_dma(reason="eight biases and eight columns of gate weights"):
                    sp.dma_start(bias_i[0:4, :], bias[0:4, :]).then_inc(gate_w_in, 16)
                    sp.dma_start(bias_f[64:68, :], bias[4:8, :]).then_inc(gate_w_in, 16)
                    sp.dma_start(gate_raw, ml_w_in[0, :, MLSTM_GATES:MLSTM_GATES + 2 * HEADS].rearrange(
                        "(k q) c -> q k c", q=P)).then_inc(gate_w_in, 16)
                for layer in range(DEPTH):
                    kinds = ("c", "u", "b") if layer == 0 else ("qk", "v", "o")
                    for part in range(2):
                        for kind in kinds:
                            if (layer, kind, part) != (0, "c", 0):
                                group((layer, kind, part))
                        for g in range(2):
                            group((layer, "mix", part, g))
                    for key in body_keys(layer, 0):
                        group(key)
                    sp.wait_ge(S["bank_free"], 8 * plan.at[(layer, "up", 0, 0)] + 1)
                    sp.dma_start(p_rows, p[layer, 0].rearrange("(c q) f -> q c f", q=P)).then_inc(p_in, 16)
                    for key in body_keys(layer, 1):
                        group(key)
                    with sp.Fori(0, LOOPED) as i:
                        for key in body_keys(layer, LOOP0):
                            group(key, i)
                    for key in body_keys(layer, PARTS - 1):
                        group(key)
                    for key in (layer, "gate", 0), (layer, "proj", 0), (layer, "proj", 1), (layer, "gate", 1):
                        group(key)
                for h in range(2):
                    for b in range(8):
                        tb, c0 = 4 * h + b % 4, b // 4 * HALF
                        by_act, by_dve = out_copies(h, b)
                        sp.wait_ge(S["out_c"], by_act)
                        if by_dve:
                            sp.wait_ge(S["out_d"], by_dve)
                        sp.dma_start(out[0, tb * P:(tb + 1) * P, c0:c0 + HALF],
                                     out_rows[h][b % 4][:, c0:c0 + HALF]).then_inc(out_done, 16)
                sp.wait_ge(out_done, 16 * 16)

            @block.tensor
            def _(pe):
                c = Counts(S)

                def bank_free(key, h, t):
                    pe.wait_ge(S["bank_free"], 4 * plan.fill(key, h) + t + 1)

                def gemm(key, h, i=0, ready=None, extra=None, order=None, hold=None):
                    n, fill = plan.at[key], plan.fill(key, h)
                    b0, K = plan.block0[n], plan.groups[n]
                    src_hi, src_lo = (z_hi, z_lo) if key[1] in ("mix", "down", "proj") else (x_hi, x_lo)
                    seen = -1
                    for item in order or [(k, t) for k in range(K) for t in range(4)]:
                        if callable(item):
                            item()
                            continue
                        k, t = item
                        if k > seen:
                            seen = k
                            if extra:
                                extra(k)
                            if h == 0:
                                pe.wait_ge(S["w_lo"], i * PER_PART["w_lo"] + b0 + k + 1)
                            if ready:
                                ready(k)
                        slot = (b0 + k) % SLOTS
                        if k == 0:
                            if fill >= 2:
                                pe.wait_ge(S["bank_free"], i * PER_PART["bank_free"] + 4 * (fill - 2) + t + 1)
                            if hold and t in hold:
                                hold[t]()
                        for step, (w, m) in enumerate(((w_hi, src_hi), (w_hi, src_lo), (w_lo, src_hi))):
                            if key[1] == "v":
                                left, right = m[:, k, h * HALF + t * P:h * HALF + (t + 1) * P], w[:, slot, :]
                            else:
                                left, right = w[:, slot, t * P:(t + 1) * P], m[:, k, half(h)]
                            ins = nc.tensor.matmul(psum[:, 4 * (fill % 2) + t, :], left, right,
                                                   start=(k == 0 and step == 0), stop=(k == K - 1 and step == 2))
                        if k == K - 1:
                            ins.then_inc(S["acc"], 1)
                        elif h == 1 and t == 3 and K == SLOTS:
                            ins.then_inc(S["block_used"], 1)

                def late(K, ts, between, after, head=3):
                    early = [t for t in range(4) if t not in ts]
                    first = min(K, head)
                    order = [(k, t) for k in range(min(K, head - 1)) for t in early] + [between]
                    order += [(k, t) for k in range(head - 1, first) for t in early] + [after]
                    order += [(k, t) for k in range(first) for t in ts]
                    return order + [(k, t) for k in range(first, K) for t in range(4)]

                def z_ready(key, h, i=0):
                    layer, kind, part, g = key
                    per = 4 if kind == "mix" else 2
                    maker = {("mix", 0): "b", ("mix", 1): "o"}.get((kind, layer))

                    def ready(k):
                        m = plan.at[(layer, maker, part) if maker else (layer, "up", part, k // 2)]
                        pe.wait_ge(S["z_ready"], i * PER_PART["z_ready"] + plan.z0[m] + h * per + k % per + 1)
                    return ready

                def group(key, i=0):
                    for h in range(2):
                        gemm(key, h, i)

                def pair(key, i=0):
                    for h in range(2):
                        gemm(key, h, i, z_ready(key, h, i))
                        gemm(key[:3] + (1,), h, i)

                def norm_sums(h, bank, adds):
                    pe.wait_ge(S["sq_sum"], adds)
                    for j in range(4):
                        ins = nc.tensor.matmul(psum[:, bank, j:j + 1], sq[:, h, j * P:(j + 1) * P], ones[:, 0:1],
                                               start=True, stop=True)
                    ins.then_inc(*c.up("norm_col"))

                def norm_spread(bank):
                    pe.wait_ge(*c.next("norm_diag"))
                    nc.tensor.matmul(psum[:, bank, :], ones[:, :], diag, start=True, stop=True).then_inc(
                        *c.up("norm_row"))

                def rs_read(k):
                    pe.wait_ge(S["rs"], k)

                def p_transpose(h):
                    for f in range(2):
                        for j in range(4):
                            ins = nc.tensor.transpose(psum[:, 4 + f, j * P:(j + 1) * P],
                                                      p_rows[:, 4 * h + j, f * P:(f + 1) * P], ident[:, :])
                        ins.then_inc(*c.up("p_t"))

                def turn(nth, done, key0, key1):
                    layer = done[0]
                    first = done[:3] + (0,) if done[1] != "gate" else None
                    proj = key0[1] == "gate"
                    adds, norms = 28 * nth, 2 + 4 * nth

                    def x_ready(h):
                        return lambda k: pe.wait_ge(S["x_ready"], 2 * DT * nth + DT * h + k + 1)

                    def p_read(count):
                        pe.wait_ge(S["p_lo"], 4 * layer + count)

                    def post0(k):
                        if k == (2 if first else 3):
                            bank_free(done, 0, 3)
                            norm_sums(0, 7 if first else 3, adds + (7 if first else 10))
                        if k == (3 if first else 4):
                            norm_spread(7 if first else 3)

                    def post1(k):
                        if first and proj and k == 5:
                            pe.wait_ge(p_in, 16 * (layer + 1))
                            bank_free(done, 1, 1)
                            p_transpose(0)
                        if k == 6:
                            bank_free(done, 1, 3)
                            norm_sums(1, 6, adds + 19)
                            if proj:
                                p_read(2)
                                p_transpose(1)
                        if k == 7:
                            norm_spread(6)

                    def post0_read():
                        rs_read(norms + 1)

                    if first:
                        gemm(first, 0, ready=z_ready(first, 0))
                        gemm(done, 0)
                        gemm(first, 1, ready=z_ready(first, 1), extra=post0)
                        gemm(done, 1, order=[(k, t) for k in range(4) for t in range(3)] + [(k, 3) for k in range(4)],
                             hold={3: post0_read})
                    else:
                        gemm(done, 0)
                        gemm(done, 1, extra=post0)
                    gemm(key0, 0, ready=x_ready(0), extra=post1, hold=None if first else {3: post0_read})
                    norm_sums(0, 7, adds + 21)
                    gemm(key0, 1, ready=x_ready(1), hold={0: lambda: p_read(3), 1: lambda: p_read(4)} if proj else None,
                         order=late(DT, (2, 3), lambda: norm_spread(7), lambda: rs_read(norms + 3), head=4))
                    bank_free(key0, 0, 3)
                    norm_sums(1, 3, adds + 28)
                    if key0[1] != "qk":
                        gemm(key1, 0, order=late(plan.groups[plan.at[key1]], (3,), lambda: norm_spread(3),
                                                 lambda: rs_read(norms + 4)))
                        gemm(key1, 1)
                def gates_pe():
                    pe.wait_ge(*c.next("gate_w"))
                    for h in range(2):
                        for k in range(DT):
                            for step, (w, m) in enumerate(((zf_hi, x_hi), (zf_hi, x_lo), (zf_lo, x_hi))):
                                ins = nc.tensor.matmul(psum[0:68, h, :], w[:, k, :], m[:, k, half(h)],
                                                       start=(k == 0 and step == 0), stop=(k == DT - 1 and step == 2))
                        ins.then_inc(*c.up("gate_acc"))
                        if h == 0:
                            norm_spread(3)
                    order = [(k, t) for t in (2, 3) for k in range(DT - 1)] + [(k, t) for k in range(DT - 1) for t in (0, 1)]
                    order += [gate_columns] + [(DT - 1, t) for t in range(4)]
                    evicted = c.next("gate_ev", 4)
                    gemm((1, "v", 0), 0, order=order, hold={
                        0: lambda: pe.wait_ge(*evicted),
                        3: lambda: rs_read(2 + 4 * 3)})

                def gate_columns():
                    bank_free((1, "qk", 0), 1, 3)
                    pe.wait_ge(S["gate_step"], GATE_ROWS_DONE)
                    pe.wait_ge(S["gate_e"], GATE_EXPS)
                    for src, bank in ((rows, 4), (rows2, 6)):
                        for ch in range(CH):
                            ins = nc.tensor.transpose(psum[:, bank + ch // 4, (ch % 4) * P:(ch % 4 + 1) * P],
                                                      src[:, ch * P:(ch + 1) * P], ident[:, :])
                            if ch % 4 == 3:
                                ins.then_inc(*c.up("gate_t"))

                def core_step(part, h):
                    s = 4 * h

                    def step(k):
                        if k == 0:
                            bank_free((1, "v", part), h, 3)
                        if 1 <= k <= 8:
                            u = k - 1
                            ch, j = 4 * h + u // 2, u % 2
                            pe.wait_ge(*c.next("core_sw"))
                            pe.wait_ge(*c.now("core_hn"))
                            pe.wait_ge(*c.now("c_upd"))
                            c.skip("core_hn")
                            c.skip("c_upd")
                            nc.tensor.matmul(psum[:, s + 1, 0:VH + 1], sw, v_sb[:, ch, j, :], start=True, stop=False)
                            nc.tensor.matmul(psum[:, s + 1, 0:VH + 1], qw, state[:, j, :], start=False,
                                             stop=True).then_inc(*c.up("core_num"))
                            nc.tensor.matmul(psum[:, s + 2, 0:VH + 1], kw, v_sb[:, ch, j, :], start=True,
                                             stop=True).then_inc(*c.up("core_u"))
                        if k <= 7:
                            ch, j = 4 * h + k // 2, k % 2
                            cols = slice(ch * P, (ch + 1) * P)
                            head = 2 * part + j
                            nc.tensor.transpose(psum[:, s, 0:P], big[:, 2 + j, cols], ident[:, :])
                            nc.tensor.matmul(psum[:, s, P:2 * P], big[:, 2 + j, cols], big[:, j, cols],
                                             start=True, stop=True)
                            for place, row in ((2, head), (3, 32 + head)):
                                ins = nc.tensor.matmul(psum[:, s, place * P:(place + 1) * P],
                                                       ident[0:64, row:row + 1].to_broadcast([64, P]),
                                                       rows[0:64, cols], start=True, stop=True)
                            ins.then_inc(*c.up("core_a"))
                        if k >= 2:
                            pe.wait_ge(*c.next("core_h2"))
                            pe.wait_ge(*c.now("core_h"))
                            c.skip("core_h", 2)
                            for e in range(2):
                                ins = nc.tensor.transpose(psum[:, s + 3, e * P:(e + 1) * P],
                                                          hn2[:, e * P:(e + 1) * P], ident[:, :])
                            ins.then_inc(*c.up("core_ht"))
                    return step

                def behind_core(key, h, step, following=None):
                    order = [(k, 0) for k in range(4)] + [lambda: step(9)] + [(k, t) for k in (0, 1) for t in (1, 2)]
                    rest = [(k, t) for k in range(DT) for t in range(4) if (k, t) not in order]
                    for n, item in enumerate(rest):
                        if following and n % 3 == 0:
                            order.append(lambda k=n // 3: following(k))
                        order.append(item)
                    gemm(key, h, order=order, hold={
                        1: lambda: pe.wait_ge(*c.now("core_hn")),
                        2: lambda: pe.wait_ge(*c.now("c_upd")),
                        3: lambda: pe.wait_ge(*c.now("core_h"))})

                def feed(layer, part, i=0):
                    for key in body_keys(layer, part)[:-2]:
                        group(key, i)
                    pair((layer, "down", part, 0), i)

                def x_turn(e):
                    if e % 2 == 0:
                        pe.wait_ge(x_in[e // 2], 16)
                    if e >= 6:
                        pe.wait_ge(S["xin_ready"], e - 5 if e < 8 else e - 1)
                    for j in range(4):
                        f = 4 * (e % 2) + j
                        ins = nc.tensor.transpose(psum[:, x_bank(e), j * P:(j + 1) * P],
                                                  y[:, e // 2, f * P:(f + 1) * P], ident[:, :])
                    ins.then_inc(*c.up("xin_t"))

                def with_x(k):
                    if k == 2:
                        norm_spread(6)
                    if k >= 4:
                        x_turn(2 * k)
                        x_turn(2 * k + 1)

                pe.wait_ge(table_in, 16 * 2)
                x_turn(0)
                x_turn(1)
                pe.wait_ge(const_in, 16 * 10)
                at = 0
                for j, r in enumerate((P, 66, 66)):
                    ins = nc.tensor.transpose(psum[:, 7, at:at + r], us[0:r, 0, j * P:(j + 1) * P], ident[0:r, 0:r])
                    at += r
                ins.then_inc(*c.up("const_t"))
                for e in range(2, 8):
                    x_turn(e)
                pe.wait_ge(*c.next("const_c"))
                pe.wait_ge(S["const"], 1)
                pe.wait_ge(S["xin_ready"], 8)

                gemm((0, "c", 0), 0, extra=with_x)
                pe.wait_ge(S["xin_ready"], 2 * CH)
                gemm((0, "c", 0), 1, order=late(DT, (2, 3), lambda: norm_spread(7), lambda: rs_read(2)))
                for part in range(2):
                    for kind in ("c", "u", "b")[1 - part:]:
                        group((0, kind, part))
                    if part == 0:
                        pair((0, "mix", part, 0))
                for layer in range(DEPTH):
                    if layer == 1:
                        for part in range(2):
                            if part == 0:
                                gates_pe()
                            else:
                                group((1, "qk", 1))
                                gemm((1, "v", part), 0)
                            if part == 0:
                                pe.wait_ge(S["gate_step"], GATE_COLUMNS_DONE)
                            step0, step1 = core_step(part, 0), core_step(part, 1)
                            gemm((1, "v", part), 1, extra=step0)
                            step0(8)
                            behind_core((1, "o", part), 0, step0, step1)
                            step1(8)
                            behind_core((1, "o", part), 1, step1)
                            if part == 0:
                                pair((1, "mix", part, 0))
                    turn(3 * layer, (layer, "mix", 1, 1), (layer, "up", 0, 0), (layer, "up", 0, 1))
                    pair((layer, "down", 0, 0))
                    feed(layer, 1)
                    with pe.Fori(0, LOOPED) as i:
                        feed(layer, LOOP0, i)
                    for key in body_keys(layer, PARTS - 1)[:2]:
                        group(key)
                    turn(3 * layer + 1, (layer, "down", PARTS - 1, 1), (layer, "gate", 0), (layer, "proj", 0))
                    group((layer, "proj", 1))
                    if layer == 0:
                        turn(2, (0, "gate", 1), (1, "qk", 0), None)
                last = (1, "gate", 1)
                adds = 28 * 5 + 10

                def out_turn(h, r):
                    for tb in range(4):
                        if h + r > 0 and (h, r) != (1, 1):
                            pe.wait_ge(S["out_c"], 4 * (h + r - 1) + tb + 1)
                        cols = slice(h * HALF + tb * P, h * HALF + (tb + 1) * P)
                        bank = tb + (4 if (h, r) == (1, 1) else 0)
                        for j in range(4):
                            f = 4 * r + j
                            if tb == 0:
                                pe.wait_ge(S["x_new"], 2 * DT * 5 + DT * h + f + 1)
                            dst = psum[:, bank, j * P:(j + 1) * P]
                            nc.tensor.matmul(dst, x_hi[:, f, cols], ident_r[:, :], start=True, stop=False)
                            nc.tensor.matmul(dst, x_lo[:, f, cols], ident_r[:, :], start=False, stop=False)
                            ins = nc.tensor.matmul(dst, y[:, f, cols], ident[:, :], start=False, stop=True)
                        ins.then_inc(S["out_t"], 1)

                def with_output(k):
                    if k == 3:
                        bank_free(last, 0, 3)
                        norm_sums(0, 3, adds)
                    if k == 4:
                        norm_spread(3)
                    if k == DT - 1:
                        out_turn(0, 0)

                pe.wait_ge(S["const_r"], 1)
                gemm(last, 0)
                gemm(last, 1, extra=with_output)
                out_turn(0, 1)
                bank_free(last, 1, 3)
                norm_sums(1, 7, adds + 4)
                norm_spread(7)
                out_turn(1, 0)
                out_turn(1, 1)

            @block.scalar
            def _(act):
                class Scalar(Common):
                    norms = 0

                    def banks(self, key, h, t):
                        self.eng.wait_ge(S["bank_free"], self.i * PER_PART["bank_free"] + 4 * plan.fill(key, h) + t + 1)

                    def start(self):
                        for e in range(2 * CH):
                            tb, r = e // 2, e % 2
                            if r == 0:
                                act.wait_ge(x_in[tb], 16)
                                act.wait_ge(*self.c.now("xin_ss"))
                                nc.scalar.activation(big[:, 0, :], y[:, tb, :], ACT.Square, scale=32.0,
                                                     accum_out=ss_in[:, tb:tb + 1]).then_inc(*self.c.up("xin_ss"))
                            act.wait_ge(*self.c.next("xin_t"))
                            nc.scalar.activation(x_hi[:, 4 * r:4 * r + 4, tb * P:(tb + 1) * P],
                                                 psum[:, x_bank(e), :].rearrange("p (f n) -> p f n", f=4),
                                                 ACT.Copy).then_inc(*self.c.up("xin_hi"))
                            if e == 7:
                                act.wait_ge(*self.c.next("const_c", 2))
                            for k in first_blocks(e):
                                self.split((0, "c", 0), k)
                            if e == 9:
                                self.row(rs[:, half(0)])
                        self.row(rs[:, half(1)])

                    def split(self, key, k):
                        n = plan.at[key]
                        b = plan.block0[n] + k
                        old = b - SLOTS
                        if old >= 0:
                            m = max(g for g in range(len(plan.groups)) if plan.block0[g] <= old)
                            kk = old - plan.block0[m]
                            if plan.groups[m] == SLOTS and kk < SLOTS - 1:
                                self.eng.wait_ge(S["block_used"], self.i * PER_PART["block_used"] + plan.used0[m] + kk + 1)
                            else:
                                self.eng.wait_ge(S["acc"], self.i * PER_PART["acc"] + 4 * plan.fill(plan.keys[m], 1) + 4)
                        self.eng.wait_ge(raw_in[b % RAWS], self.i * (16 * PER_PART["w_lo"] // RAWS) + 16 * (b // RAWS + 1))
                        g = gain_of(key, k)
                        self.nc.activation(w_hi[:, b % SLOTS, :], raw[:, b % RAWS, :], ACT.Copy,
                                           scale=1.0 if g is None else gains[:, g:g + 1]).then_inc(*self.c.up("w_hi"))

                    def row(self, dst):
                        bank = NORM_BANKS[self.norms]
                        self.norms += 1
                        act.wait_ge(*self.c.next("norm_row"))
                        nc.scalar.activation(dst, psum[:, bank, :], ACT.Copy).then_inc(*self.c.up("rs"))

                    def sums_read(self, factors):
                        n = self.c.n.get("norm_col", 0)
                        act.wait_ge(*self.c.next("norm_col"))
                        nc.scalar.activation(c1[:, n % 2, :], psum[:, NORM_BANKS[2 + n], 0:4], ACT.Copy).then_inc(
                            *self.c.up("norm_c1"))

                    def factors_read(self, dst):
                        self.row(dst)

                    def square(self, src, h, t):
                        dst = sq[:, h, :]
                        if t > 0:
                            n = self.c.n.get("sq_sum", 0)
                            dst = sqt[n % 3]
                            if n > 2:
                                self.eng.wait_ge(*self.c.now("sq_sum", 2))
                            self.c.skip("sq_sum")
                        self.nc.activation(dst, src, ACT.Square).then_inc(*self.c.up("sq_tmp"))

                    def z_part(self, zt, h, b):
                        self.eng.wait_ge(*self.c.next("act_prod"))
                        self.nc.activation(z_hi[:, zt, half(h)], us[:, b, :], ACT.Copy).then_inc(*self.c.up("z_hi"))

                    def empty_steps(self, key, h):
                        def branch(t):
                            self.banks(key, h, t)
                            self.square(y[:, 4 * key[3] + t, half(h)], h, 4 * key[3] + t)

                        def gated(t):
                            if t < 4:
                                self.banks(key, h, t)
                                nc.scalar.activation(v_tmp[:, t % 2, :], v_tmp[:, t % 2, :], ACT.Sigmoid).then_inc(
                                    *self.c.up("sig"))
                            if t > 0:
                                act.wait_ge(*self.c.next("gated"))
                                self.square(y[:, 3 + t, half(h)], h, 3 + t)
                        if key[1] == "gate":
                            return [lambda t=t: gated(t) for t in range(5)]
                        return [lambda t=t: branch(t) for t in range(4)]

                    def empty(self, key, h, between=None):
                        kind = key[1]
                        if between:
                            between()
                        if last_branch(key) and kind != "proj":
                            for step in self.empty_steps(key, h):
                                step()
                        elif kind == "proj" and key[2] == 0:
                            for t in range(4):
                                self.banks(key, h, t)
                                self.square(y[:, t, half(h)], h, t)
                        elif kind == "gate":
                            for t in range(4):
                                self.banks(key, h, t)
                                nc.scalar.activation(y[:, t, half(h)], y[:, t, half(h)], ACT.Sigmoid).then_inc(
                                    *self.c.up("sig"))
                        elif kind == "b":
                            for t in range(4):
                                self.z_part(t, h, t % 2)
                        elif kind == "o":
                            for t0 in (0, 2):
                                for t in (t0, t0 + 1):
                                    self.banks(key, h, t)
                                    self.nc.activation(us[:, t % 2, :], us[:, t % 2, :], ACT.Tanh, scale=0.5).then_inc(
                                        *self.c.up("sig"))
                                for t in (t0, t0 + 1):
                                    self.z_part(t, h, t % 2)
                        elif kind == "up":
                            self.c.skip("tap", 4)
                            for j in range(2):
                                self.eng.wait_ge(*self.c.next("tap"))
                                self.nc.activation(v_tmp[:, j, :], v_tmp[:, j, :], ACT.Gelu_apprx_tanh).then_inc(
                                    *self.c.up("gelu"))
                            for j in range(2):
                                self.z_part(2 * key[3] + j, h, j)

                    def renew(self, layer, which, h, work, key, blocks):
                        for k in range(DT):
                            for b in blocks.get(k, ()):
                                self.split(key, b)
                            self.eng.wait_ge(*self.c.next("x_new"))
                            nc.scalar.activation(x_hi[:, k, half(h)], xn[:, k % 2, :], ACT.Copy).then_inc(
                                *self.c.up("x_hi"))
                            self.square(xn[:, k % 2, :], h, k)
                            for other in work[k]:
                                other()

                    def out_copy(self, h, b):
                        if not by_vector(h, b):
                            bank = b if h == 1 else b % 4
                            act.wait_ge(S["out_t"], 8 * h + b + 1)
                            nc.scalar.activation(out_rows[h][b % 4][:, b // 4 * HALF:(b // 4 + 1) * HALF],
                                                 psum[:, bank, :], ACT.Copy).then_inc(*self.c.up("out_c"))

                    def p_split(self, h):
                        for f in range(2):
                            act.wait_ge(*self.c.next("p_t"))
                            nc.scalar.activation(z_hi[:, f, half(h)], psum[:, 4 + f, :], ACT.Copy).then_inc(
                                *self.c.up("p_hi"))

                    def gates(self):
                        act.wait_ge(S["gate_step"], GATE_ABS)
                        a = y[0:4, 3, :]
                        nc.scalar.activation(a, a, ACT.Exp, scale=-1.0).then_inc(*self.c.up("gate_e"))
                        act.wait_ge(*self.c.now("gate_e"))
                        nc.scalar.activation(a, a, ACT.Ln, bias=1.0).then_inc(*self.c.up("gate_e"))
                        act.wait_ge(S["gate_step"], GATE_ROWS_DONE)
                        for dst, src, scale in ((rows[32:36, :], y[0:4, 1, :], 1.0), (rows[64:68, :], y[0:4, 2, :], 1.0),
                                                (rows2[32:36, :], y[0:4, 5, :], -1.0)):
                            nc.scalar.activation(dst, src, ACT.Exp, scale=scale).then_inc(*self.c.up("gate_e"))

                    def core(self, part, h, nxt):
                        for k in range(10):
                            if 1 <= k <= 8:
                                act.wait_ge(*self.c.next("core_r"))
                                act.wait_ge(*self.c.now("core_h2"))
                                nc.scalar.activation(hn, psum[:, 4 * h + 1, 0:VH], ACT.Copy, scale=rden).then_inc(
                                    *self.c.up("core_hn"))
                                act.wait_ge(*self.c.now("core_hn"))
                                nc.scalar.activation(sqt_core, hn, ACT.Square, accum_out=hss).then_inc(
                                    *self.c.up("core_ss"))
                                self.c.skip("core_h2")
                            if k <= 7:
                                act.wait_ge(*self.c.next("core_d"))
                                nc.scalar.activation(dmat, dmat, ACT.Exp).then_inc(*self.c.up("core_e"))
                            if k >= 2:
                                u = k - 2
                                ch, j = 4 * h + u // 2, u % 2
                                act.wait_ge(*self.c.next("core_ht"))
                                for e in range(2):
                                    hg = 2 * (2 * part + j) + e
                                    nc.scalar.activation(big[:, j + 2 * e, ch * P:(ch + 1) * P],
                                                         psum[:, 4 * h + 3, e * P:(e + 1) * P], ACT.Copy,
                                                         scale=head_gain[:, hg:hg + 1]).then_inc(*self.c.up("core_h"))
                            if nxt and 1 <= k <= 8:
                                self.split(nxt, k - 1)

                stages(Scalar(act, nc.scalar))

            @block.vector
            def _(dve):
                class Vector(Common):
                    squared = []

                    def acc(self, key, h, t):
                        self.eng.wait_ge(S["acc"], self.i * PER_PART["acc"] + 4 * plan.fill(key, h) + t + 1)
                        return psum[:, 4 * (plan.fill(key, h) % 2) + t, :]

                    def column(self, key, tap, t):
                        layer, _, part, g = key
                        c0 = ff_col(layer, tap, part_start(part) + 2 * g + t)
                        return gains[:, c0:c0 + 1] if isinstance(self.i, int) else gains[:, bass.ds(self.i * 4 + c0, 1)]

                    def start(self):
                        for e in range(2 * CH):
                            if e == 2:
                                dve.wait_ge(*self.c.next("const_t"))
                                nc.vector.tensor_copy(gains[:, :], psum[:, 7, 0:260]).then_inc(*self.c.up("const_c"))
                                dve.wait_ge(*self.c.now("const_c"))
                                nc.vector.tensor_scalar(head_gain, gains[:, HN_COL:HN_COL + 8], 8.0, None,
                                                        ALU.mult).then_inc(*self.c.up("const_c"))
                            tb, r = e // 2, e % 2
                            cols = slice(tb * P, (tb + 1) * P)
                            dve.wait_ge(*self.c.next("xin_hi"))
                            nc.vector.tensor_tensor(x_lo[:, 4 * r:4 * r + 4, cols],
                                                    psum[:, x_bank(e), :].rearrange("p (f n) -> p f n", f=4),
                                                    x_hi[:, 4 * r:4 * r + 4, cols].bitcast(FP32),
                                                    ALU.subtract).then_inc(*self.c.up("xin_ready"))
                            for k in first_blocks(e):
                                self.split((0, "c", 0), k)
                            if e == 7:
                                self.diagonal(c2_pre[:, 0:4])
                        nc.vector.tensor_copy(ident_r[:, :], ident[:, :]).then_inc(*self.c.up("const_r"))
                        self.factors_stand()
                        self.diagonal(c2_pre[:, 4:8])
                        self.factors_stand()

                    def spread(self, factors):
                        nc.vector.tensor_tensor(diag.rearrange("p (j n) -> p j n", j=4),
                                                ident[:, :].unsqueeze(1).to_broadcast([P, 4, P]),
                                                factors.unsqueeze(2).to_broadcast([P, 4, P]),
                                                ALU.mult).then_inc(*self.c.up("norm_diag"))

                    def diagonal(self, factors):
                        dve.wait_ge(*self.c.next("norm_c2"))
                        self.spread(factors)

                    def factors_stand(self):
                        dve.wait_ge(*self.c.next("rs"))

                    def split(self, key, k):
                        b = plan.block0[plan.at[key]] + k
                        self.eng.wait_ge(*self.c.next("w_hi"))
                        g = gain_of(key, k)
                        w, hi = raw[:, b % RAWS, :], w_hi[:, b % SLOTS, :].bitcast(FP32)
                        if g is None:
                            ins = self.nc.tensor_tensor(w_lo[:, b % SLOTS, :], w, hi, ALU.subtract)
                        else:
                            ins = self.nc.scalar_tensor_tensor(w_lo[:, b % SLOTS, :], w, gains[:, g:g + 1], hi,
                                                               ALU.mult, ALU.subtract)
                        ins.then_inc(*self.c.up("w_lo"))

                    def add_squares(self):
                        while self.squared:
                            h, t = self.squared.pop(0)
                            if t == 0:
                                self.c.skip("sq_tmp")
                                continue
                            dve.wait_ge(*self.c.next("sq_tmp"))
                            dve.wait_ge(*self.c.now("sq_sum"))
                            n = self.c.n.get("sq_sum", 0)
                            nc.vector.tensor_tensor(sq[:, h, :], sq[:, h, :], sqt[n % 3], ALU.add).then_inc(
                                *self.c.up("sq_sum"))

                    def empty_steps(self, key, h):
                        c, v = self.c, nc.vector

                        def branch(t):
                            bank = self.acc(key, h, t)
                            tile = y[:, 4 * key[3] + t, half(h)]
                            dve.wait_ge(*c.now("bank_free", 3))
                            v.tensor_tensor(tile, bank, tile, ALU.add).then_inc(*c.up("bank_free"))
                            self.squared.append((h, 4 * key[3] + t))

                        def gated(t):
                            if t < 4:
                                bank = self.acc(key, h, t)
                                dve.wait_ge(*c.now("gated"))
                                v.tensor_tensor(v_tmp[:, t % 2, :], bank, rs[:, half(h)], ALU.mult).then_inc(
                                    *c.up("bank_free"))
                            if t > 0:
                                tile = y[:, 3 + t, half(h)]
                                dve.wait_ge(*c.next("sig"))
                                v.tensor_tensor(tile, v_tmp[:, (t - 1) % 2, :], tile, ALU.mult).then_inc(
                                    *c.up("gated"))
                                self.squared.append((h, 3 + t))
                        if key[1] == "gate":
                            return [lambda t=t: gated(t) for t in range(5)]
                        return [lambda t=t: branch(t) for t in range(4)]

                    def empty(self, key, h, between=None):
                        self.drain(key, h, between)
                        if between and key[1] != "up":
                            between()

                    def drain(self, key, h, between):
                        kind, c, w = key[1], self.c, self.nc
                        wait = self.eng.wait_ge
                        rsh = rs[:, half(h)]
                        if last_branch(key) and kind != "proj":
                            for step in self.empty_steps(key, h):
                                self.add_squares()
                                step()
                            self.add_squares()
                        elif kind in ("mix", "down"):
                            for t in range(4):
                                bank = self.acc(key, h, t)
                                tile = y[:, 4 * key[3] + t, half(h)]
                                if key[2] == 0:
                                    w.tensor_copy(tile, bank).then_inc(*c.up("bank_free"))
                                else:
                                    wait(*c.now("bank_free", 3))
                                    w.tensor_tensor(tile, bank, tile, ALU.add).then_inc(*c.up("bank_free"))
                        elif kind == "proj":
                            for t in range(4):
                                bank = self.acc(key, h, t)
                                tile = y[:, 4 * key[2] + t, half(h)]
                                if key[2] == 0:
                                    wait(*c.next("sig"))
                                    w.tensor_tensor(tile, bank, tile, ALU.mult).then_inc(*c.up("bank_free"))
                                    self.add_squares()
                                    self.squared.append((h, t))
                                else:
                                    w.tensor_copy(tile, bank).then_inc(*c.up("bank_free"))
                            self.add_squares()
                        elif kind == "gate":
                            wait(*c.now("x_t"))
                            for t in range(4):
                                bank = self.acc(key, h, t)
                                w.tensor_tensor(y[:, t, half(h)], bank, rsh, ALU.mult).then_inc(*c.up("bank_free"))
                        elif kind == "c":
                            wait(*c.now("act_prod"))
                            for t in range(4):
                                bank = self.acc(key, h, t)
                                w.tensor_tensor(conv_out[:, t, half(h)], bank, rsh, ALU.mult).then_inc(
                                    *c.up("bank_free"))
                        elif kind == "u":
                            for t in range(4):
                                cu, res = conv_in[:, t % 2, :], conv_out[:, t, half(h)]
                                bank = self.acc(key, h, t)
                                wait(*c.now("cu"))
                                if h == 0:
                                    w.memset(cu[:, 0:2], 0.0).then_inc(*c.up("halo"))
                                else:
                                    w.tensor_copy(cu[:, 0:2], halo_keep[:, t, :]).then_inc(*c.up("halo"))
                                w.tensor_tensor(cu[:, 2:2 + HALF], bank, rsh, ALU.mult).then_inc(*c.up("bank_free"))
                                wait(*c.now("bank_free"))
                                w.tensor_tensor(cu[:, 2:2 + HALF], cu[:, 2:2 + HALF], res, ALU.mult).then_inc(*c.up("cu"))
                                wait(*c.now("cu"))
                                w.tensor_copy(halo_keep[:, t, :], cu[:, HALF:HALF + 2]).then_inc(*c.up("halo"))
                                tile = 4 * key[2] + t
                                col = [gains[:, sc_col(tap, tile):sc_col(tap, tile) + 1] for tap in range(3)]
                                w.tensor_scalar(res, cu[:, 0:HALF], col[0], None, ALU.mult).then_inc(*c.up("cu"))
                                for tap in (1, 2):
                                    wait(*c.now("cu"))
                                    w.scalar_tensor_tensor(res, cu[:, tap:tap + HALF], col[tap], res, ALU.mult,
                                                           ALU.add).then_inc(*c.up("cu"))
                        elif kind == "b":
                            wait(*c.now("cu"))
                            for t in range(5):
                                if t < 4:
                                    bank = self.acc(key, h, t)
                                    if t == 0:
                                        wait(*c.now("z_ready"))
                                    elif t >= 2:
                                        wait(*c.now("z_ready"))
                                    w.tensor_tensor(us[:, t % 2, :], bank, rsh, ALU.mult).then_inc(*c.up("bank_free"))
                                if t >= 1:
                                    wait(*c.now("bank_free", 1 if t < 4 else 0))
                                    w.tensor_tensor(us[:, (t - 1) % 2, :], us[:, (t - 1) % 2, :],
                                                    conv_out[:, t - 1, half(h)], ALU.mult).then_inc(*c.up("act_prod"))
                                    c.skip("z_ready")
                        elif kind == "up":
                            wait(*c.now("tap"))
                            for j in range(2):
                                g_in = conv_in[:, j, :]
                                if h == 0:
                                    w.memset(g_in[:, 0:2], 0.0).then_inc(*c.up("halo"))
                                else:
                                    w.tensor_copy(g_in[:, 0:2], g_in[:, HALF:HALF + 2]).then_inc(*c.up("halo"))
                            wait(*c.now("halo"))
                            for j in range(2):
                                bank = self.acc(key, h, j)
                                w.tensor_tensor(conv_in[:, j, 2:2 + HALF], bank, rsh, ALU.mult).then_inc(
                                    *c.up("bank_free"))
                            wait(*c.now("z_ready"))
                            for j in range(2):
                                bank = self.acc(key, h, 2 + j)
                                w.tensor_tensor(us[:, j, :], bank, rsh, ALU.mult).then_inc(*c.up("bank_free"))
                            if between:
                                between()
                            wait(*c.now("bank_free", 2))
                            for j in range(2):
                                w.tensor_scalar(v_tmp[:, j, :], conv_in[:, j, 0:HALF], self.column(key, 0, j), None,
                                                ALU.mult).then_inc(*c.up("tap"))
                            for tap in (1, 2):
                                for j in range(2):
                                    wait(*c.now("tap", 1))
                                    w.scalar_tensor_tensor(v_tmp[:, j, :], conv_in[:, j, tap:tap + HALF],
                                                           self.column(key, tap, j), v_tmp[:, j, :], ALU.mult,
                                                           ALU.add).then_inc(*c.up("tap"))
                            for j in range(2):
                                wait(*c.next("gelu"))
                                w.tensor_tensor(us[:, j, :], us[:, j, :], v_tmp[:, j, :], ALU.mult).then_inc(
                                    *c.up("act_prod"))
                            c.skip("z_ready", 2)
                        elif kind == "qk":
                            wait(*c.now("act_prod"))
                            for t in range(4):
                                bank = self.acc(key, h, t)
                                w.scalar_tensor_tensor(big[:, t, half(h)], bank, 1.0 if t < 2 else QKH ** -0.5, rsh,
                                                       ALU.mult, ALU.mult).then_inc(*c.up("bank_free"))
                        elif kind == "v":
                            wait(*c.now("c_upd"))
                            wait(*c.now("core_sw"))
                            for t in range(4):
                                bank = self.acc(key, h, t)
                                w.tensor_scalar(v_sb[:, 4 * h + t, :, 0:VH], bank.rearrange("p (j e) -> p j e", j=2),
                                                c2_pre[:, 4 * h + t:4 * h + t + 1], ONES, ALU.mult,
                                                ALU.mult).then_inc(*c.up("bank_free"))
                        elif kind == "o":
                            if h == 0:
                                wait(*c.now("core_h"))
                            for t0 in (0, 2):
                                wait(*c.now("z_ready"))
                                for t in (t0, t0 + 1):
                                    bank = self.acc(key, h, t)
                                    w.tensor_tensor(us[:, t % 2, :], bank, rsh, ALU.mult).then_inc(*c.up("bank_free"))
                                for t in (t0, t0 + 1):
                                    wait(*c.next("sig"))
                                    w.scalar_tensor_tensor(us[:, t % 2, :], us[:, t % 2, :], 1.0,
                                                           big[:, t // 2 + 2 * (t % 2), half(h)], ALU.add,
                                                           ALU.mult).then_inc(*c.up("act_prod"))
                                    c.skip("z_ready")

                    def renew(self, layer, which, h, work, key, blocks):
                        c = self.c
                        for k in range(DT):
                            g = norm_col(which, layer, k)
                            dve.wait_ge(*c.now("x_ready", 1 if k else 0))
                            dve.wait_ge(*c.now("sq_tmp"))
                            nc.vector.scalar_tensor_tensor(xn[:, k % 2, :], y[:, k, half(h)], gains[:, g:g + 1],
                                                           rs_post[h], ALU.mult, ALU.mult).then_inc(*c.up("x_t"))
                            self.add_squares()
                            dve.wait_ge(*c.now("x_t"))
                            dve.wait_ge(*c.next("x_old"))
                            nc.vector.tensor_tensor(xn[:, k % 2, :], xn[:, k % 2, :], x_old[:, k % 2, :],
                                                    ALU.add).then_inc(*c.up("x_new"))
                            self.squared.append((h, k))
                            c.skip("x_ready")
                            for b in blocks.get(k, ()):
                                self.split(key, b)
                            for other in work[k]:
                                other()
                        self.add_squares()

                    def last_terms(self, h):
                        for k in range(DT):
                            g = norm_col(5, 1, k)
                            tile = y[:, k, half(h)]
                            nc.vector.scalar_tensor_tensor(tile, tile, gains[:, g:g + 1], rs_post[h], ALU.mult,
                                                           ALU.mult).then_inc(*self.c.up("x_new"))

                    def out_copy(self, h, b):
                        if by_vector(h, b):
                            dve.wait_ge(S["out_t"], 8 * h + b + 1)
                            nc.vector.tensor_copy(out_rows[h][b % 4][:, b // 4 * HALF:(b // 4 + 1) * HALF],
                                                  psum[:, b, :]).then_inc(*self.c.up("out_d"))

                    def p_split(self, h):
                        for f in range(2):
                            dve.wait_ge(*self.c.next("p_hi"))
                            nc.vector.tensor_tensor(z_lo[:, f, half(h)], psum[:, 4 + f, :],
                                                    z_hi[:, f, half(h)].bitcast(FP32), ALU.subtract).then_inc(
                                *self.c.up("p_lo"))

                    def gate_weights(self):
                        c, v = self.c, nc.vector
                        g0 = norm_col(0, 1)
                        dve.wait_ge(gate_w_in, 16 * 3)
                        v.tensor_tensor(gate_g, gate_raw, gains[:, g0:g0 + DT].unsqueeze(2).to_broadcast([P, DT, 8]),
                                        ALU.mult).then_inc(*c.up("gate_step"))
                        v.memset(zf_hi.bitcast(FP32), 0.0).then_inc(*c.up("gate_step"))
                        v.memset(zf_lo.bitcast(FP32), 0.0).then_inc(*c.up("gate_step"))
                        dve.wait_ge(*c.now("gate_step"))
                        for to, of in ((0, 0), (64, 4)):
                            v.tensor_copy(zf_hi[:, :, to:to + 4], gate_g[:, :, of:of + 4]).then_inc(*c.up("gate_step"))
                        dve.wait_ge(*c.now("gate_step"))
                        for to, of in ((0, 0), (64, 4)):
                            ins = v.tensor_tensor(zf_lo[:, :, to:to + 4], gate_g[:, :, of:of + 4],
                                                  zf_hi[:, :, to:to + 4].bitcast(FP32), ALU.subtract)
                        ins.then_inc(*c.up("gate_w"))

                    def gates(self):
                        c, v = self.c, nc.vector
                        chunk_on = y[0:4, 4, :]
                        v.memset(rows, 0.0).then_inc(*c.up("gate_step"))
                        v.memset(rows2, 0.0).then_inc(*c.up("gate_step"))
                        v.memset(chunk_on, 1.0).then_inc(*c.up("gate_step"))
                        v.memset(v_sb[:, :, :, VH:VH + 1], 1.0).then_inc(*c.up("gate_step"))
                        dve.wait_ge(*c.now("gate_step"))
                        v.memset(chunk_on.rearrange("p (c n) -> p c n", n=P)[:, :, 0:1], 0.0).then_inc(
                            *c.up("gate_step"))
                        for h in range(2):
                            dve.wait_ge(*c.next("gate_acc"))
                            for q, r in ((0, 0), (1, 64)):
                                v.tensor_tensor(y[r:r + 4, q, half(h)], psum[r:r + 4, h, :], rs[r:r + 4, half(h)],
                                                ALU.mult).then_inc(*c.up("gate_ev"))
                        dve.wait_ge(*c.now("gate_ev"))
                        ig, f, lf, m, b = (y[0:4, q, :] for q in (0, 2, 3, 5, 7))
                        v.tensor_scalar(ig, ig, bias_i[0:4, :], None, ALU.add).then_inc(*c.up("gate_step"))
                        v.tensor_scalar(f, y[64:68, 1, :], bias_f[64:68, :], None, ALU.add).then_inc(
                            *c.up("gate_step"))
                        dve.wait_ge(*c.now("gate_step"))
                        v.scalar_tensor_tensor(lf, f, -1.0, f, ALU.mult, ALU.max).then_inc(*c.up("gate_step"))
                        assert c.n["gate_step"] == GATE_ABS
                        dve.wait_ge(*c.next("gate_e", 2))
                        v.scalar_tensor_tensor(lf, f, 0.0, lf, ALU.min, ALU.subtract).then_inc(*c.up("gate_step"))
                        dve.wait_ge(*c.now("gate_step"))
                        v.tensor_tensor_scan(m, lf, ig, 0.0, ALU.add, ALU.max).then_inc(*c.up("gate_step"))
                        v.tensor_tensor_scan(b, chunk_on, lf, 0.0, ALU.mult, ALU.add).then_inc(*c.up("gate_step"))
                        dve.wait_ge(*c.now("gate_step"))
                        bm = rows[0:4, :]
                        v.tensor_tensor(bm, b, m, ALU.subtract).then_inc(*c.up("gate_step"))
                        v.tensor_tensor(rows2[0:4, :], ig, b, ALU.subtract).then_inc(*c.up("gate_step"))
                        v.memset(m_state[0:4, 0:1], 0.0).then_inc(*c.up("gate_step"))
                        v.tensor_copy(m_state[0:4, 1:8],
                                      m.rearrange("p (c n) -> p c n", n=P)[:, 0:7, P - 1]).then_inc(*c.up("gate_step"))
                        dve.wait_ge(*c.now("gate_step"))
                        by_chunk = bm.rearrange("p (c n) -> p c n", n=P)
                        v.tensor_tensor(y[0:4, 1, :].rearrange("p (c n) -> p c n", n=P), by_chunk,
                                        m_state[0:4, 0:8].unsqueeze(2).to_broadcast([4, CH, P]), ALU.add).then_inc(
                            *c.up("gate_step"))
                        v.tensor_tensor(y[0:4, 2, :].rearrange("p (c n) -> p c n", n=P),
                                        rows2[0:4, :].rearrange("p (c n) -> p c n", n=P),
                                        by_chunk[:, :, P - 1:P].to_broadcast([4, CH, P]), ALU.add).then_inc(
                            *c.up("gate_step"))
                        assert c.n["gate_step"] == GATE_ROWS_DONE
                        for n, (dst, r) in enumerate(((col_a, 64), (col_g, 0), (col_m, 32))):
                            for q in range(2):
                                bank = 4 + q if n == 0 else 6 + q
                                if n == 0:
                                    dve.wait_ge(*c.next("gate_t"))
                                elif n == 1:
                                    dve.wait_ge(*c.next("gate_t"))
                                v.tensor_copy(dst[:, 4 * q:4 * q + 4, :],
                                              psum[:, bank, :].rearrange("p (c n) -> p c n", n=P)[:, :, r:r + 4]
                                              ).then_inc(*c.up("gate_step"))
                        assert c.n["gate_step"] == GATE_COLUMNS_DONE

                    def core(self, part, h, nxt):
                        c, v = self.c, nc.vector
                        s = 4 * h
                        if h == 0:
                            v.memset(state, 0.0).then_inc(*c.up("c_upd0"))
                            dve.wait_ge(*c.now("c_upd0"))
                        for k in range(10):
                            if 1 <= k <= 8:
                                u = k - 1
                                ch, j = 4 * h + u // 2, u % 2
                                head = 2 * part + j
                                dve.wait_ge(*c.next("core_num"))
                                d_ps = psum[:, s + 1, VH:VH + 1]
                                v.tensor_scalar(den, d_ps, -1.0, None, ALU.mult).then_inc(*c.up("core_den"))
                                dve.wait_ge(*c.now("core_den"))
                                v.scalar_tensor_tensor(den, d_ps, col_m[:, ch, head:head + 1], den, ALU.max,
                                                       ALU.max).then_inc(*c.up("core_den"))
                                dve.wait_ge(*c.now("core_den"))
                                v.reciprocal(rden, den).then_inc(*c.up("core_r"))
                                dve.wait_ge(*c.next("core_u"))
                                v.scalar_tensor_tensor(state[:, j, :], state[:, j, :], dec, psum[:, s + 2, 0:VH + 1],
                                                       ALU.mult, ALU.add).then_inc(*c.up("c_upd"))
                            if k <= 7:
                                ch, j = 4 * h + k // 2, k % 2
                                head = 2 * part + j
                                dve.wait_ge(*c.next("core_a"))
                                dve.wait_ge(*c.now("core_sw"))
                                v.scalar_tensor_tensor(dmat, psum[:, s, 2 * P:3 * P], col_g[:, ch, head:head + 1],
                                                       mask[:, :], ALU.add, ALU.min).then_inc(*c.up("core_d"))
                                v.tensor_tensor(qw, psum[:, s, 3 * P:4 * P], big[:, j, ch * P:(ch + 1) * P], ALU.mult)
                                v.tensor_scalar(kw, psum[:, s, 0:P], col_a[:, ch, head:head + 1], None, ALU.mult)
                                if k > 0:
                                    dve.wait_ge(*c.now("c_upd"))
                                v.tensor_copy(dec, psum[:, s, 4 * P - 1:4 * P])
                                dve.wait_ge(*c.next("core_e"))
                                v.tensor_tensor(sw, psum[:, s, P:2 * P], dmat, ALU.mult).then_inc(*c.up("core_sw"))
                            if 1 <= k <= 8:
                                dve.wait_ge(*c.next("core_rstd"))
                                dve.wait_ge(*c.now("core_ht"))
                                v.tensor_scalar(hn2, hn, hrstd, None, ALU.mult).then_inc(*c.up("core_h2"))
                                c.skip("core_ht")
                            if nxt and 1 <= k <= 8:
                                self.split(nxt, k - 1)
                        c.skip("core_h", 16)

                stages(Vector(dve, nc.vector))

            @block.gpsimd
            def _(pool):
                class Pool(Common):
                    def start(self):
                        nc.gpsimd.memset(ones[:, :], ONES).then_inc(*self.c.up("const"))
                        nc.gpsimd.memset(minus_half, -0.5).then_inc(*self.c.up("pow_in"))
                        for h in range(2):
                            pool.wait_ge(*self.c.next("xin_ss", 4))
                            self.factors(c2_pre[:, 4 * h:4 * h + 4], ss_in[:, 4 * h:4 * h + 4], D * EPS * ONES,
                                         "norm_c2")

                    def factors(self, dst, sums, eps, name):
                        n = sums.shape[1]
                        nc.gpsimd.tensor_scalar(pow_in[:, 0:n], sums, eps, None, ALU.add).then_inc(*self.c.up("pow_in"))
                        pool.wait_ge(*self.c.now("pow_in"))
                        nc.gpsimd.tensor_tensor(dst, pow_in[:, 0:n], minus_half[:, 0:n], ALU.pow).then_inc(
                            *self.c.up(name))

                    def sums_read(self, factors):
                        n = self.c.n.get("norm_c1", 0)
                        pool.wait_ge(*self.c.next("norm_c1"))
                        self.factors(factors, c1[:, n % 2, :], D * EPS * ONES, "norm_c2")

                    def empty(self, key, h, between=None):
                        if between:
                            between()
                        n = {"up": 2, "b": 4, "o": 4}.get(key[1], 0)
                        for t in range(n):
                            zt = 2 * key[3] + t if key[1] == "up" else t
                            self.eng.wait_ge(*self.c.next("z_hi"))
                            self.nc.tensor_tensor(z_lo[:, zt, half(h)], us[:, t % 2, :],
                                                  z_hi[:, zt, half(h)].bitcast(FP32), ALU.subtract).then_inc(
                                *self.c.up("z_ready"))

                    def renew(self, layer, which, h, work, key, blocks):
                        c = self.c
                        for k in range(DT + 1):
                            if k < DT:
                                pool.wait_ge(*c.now("x_ready"))
                                nc.gpsimd.tensor_tensor(x_old[:, k % 2, :], x_hi[:, k, half(h)].bitcast(FP32),
                                                        x_lo[:, k, half(h)].bitcast(FP32), ALU.add).then_inc(
                                    *c.up("x_old"))
                            if k > 0:
                                pool.wait_ge(*c.next("x_hi"))
                                nc.gpsimd.tensor_tensor(x_lo[:, k - 1, half(h)], xn[:, (k - 1) % 2, :],
                                                        x_hi[:, k - 1, half(h)].bitcast(FP32), ALU.subtract).then_inc(
                                    *c.up("x_ready"))
                                c.skip("x_new")
                                for other in work[k - 1]:
                                    other()

                    def core(self, part, h, nxt):
                        for _ in range(8):
                            pool.wait_ge(*self.c.next("core_ss"))
                            self.factors(hrstd, hss, VH * EPS, "core_rstd")

                stages(Pool(pool, nc.gpsimd))


_INS = ["x", "p", "norm_mix_pre", "norm_mix_post", "norm_ffn_pre", "norm_ffn_post", "sc_w_in", "sc_w_conv", "sc_w_out",
        "ml_w_in", "ml_gate_bias", "ml_head_norm", "ml_w_out", "ffn_w_up", "ffn_w_conv", "ffn_w_down",
        "ple_norm_gate", "ple_w_gate", "ple_w_proj", "ple_norm_out"]


def kernel(**inputs):
    import numpy as np
    import concourse.bacc as bacc
    from concourse.bass_utils import run_bass_kernel_spmd

    nc = bacc.Bacc("TRN2", target_bir_lowering=False, num_devices=1, dynamic_dma_scratch_size=1024)
    arrays, args = {}, []
    for name in _INS:
        a = np.ascontiguousarray(inputs[name])
        arrays[f"in_{name}"] = a
        args.append(nc.dram_tensor(f"in_{name}", a.shape, mybir.dt.from_np(a.dtype), kind="ExternalInput").ap())
    tables = np.zeros((2, P, P), np.float32)
    tables[0] = np.eye(P)
    tables[1][np.tril_indices(P, -1)] = -3.0e38
    arrays["in_tables"] = tables
    args.append(nc.dram_tensor("in_tables", tables.shape, FP32, kind="ExternalInput").ap())
    out = nc.dram_tensor("out", (1, SEQ, D), FP32, kind="ExternalOutput").ap()
    decoder_kernel(nc, *args, out)
    return run_bass_kernel_spmd(nc, [arrays], core_ids=[0]).results[0]["out"]
```
